# Optimizing a Trainium2 kernel written in Bass

```python
import math
import jax
import jax.numpy as jnp
from jax import lax
import numpy as np

D_MODEL = 1024
BATCH = 1
SEQ = 256
DEPTH = 2

GRID_W = 64
CTX_LEN = 256
EPS = 1e-6
N_BRANCH = 3
F32 = jnp.float32

CONV_DIM = 512
CONV_WIDTH = 31

GLA_HEADS = 4
GLA_DK = 64
GLA_DV = 128
GLA_RANK = 16
GLA_GATE_NORM = 16.0
GLA_CHUNK = 64
GLA_QK = GLA_HEADS * GLA_DK
GLA_V = GLA_HEADS * GLA_DV
ROPE_BASE = 10000.0

NA_HEADS = 8
NA_HD = 64
NA_DIM = NA_HEADS * NA_HD
NA_KH = 8
NA_KW = 16
NA_QR = 8
NA_QC = 16

PEER_HEADS = 8
PEER_NKEYS = 128
PEER_EXPERTS = PEER_NKEYS * PEER_NKEYS
PEER_TOPK = 16
PEER_DKEY = 256
PEER_CHUNK = 128

IN_SPLITS = (2 * CONV_DIM, GLA_QK, GLA_QK, GLA_V, GLA_V, 2 * GLA_RANK, NA_DIM, NA_DIM, NA_DIM, N_BRANCH * D_MODEL)
IN_DIM = sum(IN_SPLITS)

kernel_name = 'hybrid_conv_gla_natten_peer_dit'

def rmsnorm(x, g):
    xf = x.astype(F32)
    y = xf * lax.rsqrt(jnp.mean(xf * xf, axis=-1, keepdims=True) + EPS)
    return (y * g.astype(F32)).astype(x.dtype)

def layernorm(x, g, b):
    xf = x.astype(F32)
    mu = jnp.mean(xf, axis=-1, keepdims=True)
    xc = xf - mu
    var = jnp.mean(xc * xc, axis=-1, keepdims=True)
    return (xc * lax.rsqrt(var + EPS) * g.astype(F32) + b.astype(F32)).astype(x.dtype)

def split_cols(p):
    return jnp.split(p, np.cumsum(IN_SPLITS)[:-1].tolist(), axis=-1)

def conv_module(glu_in, conv_w, conv_b, ln_g, ln_b, w_o):
    u = glu_in[..., :CONV_DIM] * jax.nn.sigmoid(glu_in[..., CONV_DIM:])
    u = lax.conv_general_dilated(
        u, conv_w.astype(u.dtype)[:, None, :], (1,), [(CONV_WIDTH // 2, CONV_WIDTH // 2)],
        dimension_numbers=('NWC', 'WIO', 'NWC'), feature_group_count=CONV_DIM) + conv_b.astype(u.dtype)
    u = jax.nn.silu(layernorm(u, ln_g, ln_b))
    return u @ w_o

def axial_rope(L):
    t = jnp.arange(L)
    row = (t // GRID_W).astype(F32)
    col = (t % GRID_W).astype(F32)
    n_freq = GLA_DK // 4
    inv = ROPE_BASE ** (-jnp.arange(n_freq, dtype=F32) / n_freq)
    ang = jnp.concatenate([row[:, None] * inv, col[:, None] * inv], axis=-1)
    return jnp.cos(ang), jnp.sin(ang)

def apply_rope(x, cos, sin):
    x1, x2 = x[..., 0::2], x[..., 1::2]
    c = cos[None, :, None, :]
    s = sin[None, :, None, :]
    return jnp.stack([x1 * c - x2 * s, x1 * s + x2 * c], axis=-1).reshape(x.shape)

def gla_features(pq, pk, pv, pa, wa2, ba, rope):
    B, L, _ = pq.shape
    q = pq.astype(F32).reshape(B, L, GLA_HEADS, GLA_DK) * GLA_DK ** -0.5
    k = pk.astype(F32).reshape(B, L, GLA_HEADS, GLA_DK)
    if rope is not None:
        q = apply_rope(q, *rope)
        k = apply_rope(k, *rope)
    v = pv.astype(F32).reshape(B, L, GLA_HEADS, GLA_DV)
    z = jnp.einsum('blzr,zrk->blzk', pa.astype(F32).reshape(B, L, 2, GLA_RANK), wa2.astype(F32)) + ba.astype(F32)
    log_a = (jax.nn.log_sigmoid(z) / GLA_GATE_NORM).reshape(B, L, 2, GLA_HEADS, GLA_DK)
    return q, k, v, log_a[:, :, 0], log_a[:, :, 1]

def gla_scan(q, k, v, log_a, s0):
    B, L, H, _ = q.shape
    DV = v.shape[-1]
    C = GLA_CHUNK
    n = L // C

    def blocks(t):
        return t.reshape(B, n, C, H, t.shape[-1]).transpose(1, 0, 3, 2, 4)

    lower = jnp.tril(jnp.ones((C, C), dtype=bool))

    def step(state, inp):
        qb, kb, vb, ab = inp
        b = jnp.cumsum(ab, axis=2)
        b_mid = b[:, :, C // 2:C // 2 + 1]
        b_end = b[:, :, C - 1:]
        o_inter = jnp.einsum('bhcd,bhde->bhce', qb * jnp.exp(b), state)
        att = jnp.einsum('bhid,bhjd->bhij', qb * jnp.exp(b - b_mid), kb * jnp.exp(b_mid - b))
        att = jnp.where(lower, att, 0.0)
        o_intra = jnp.einsum('bhij,bhje->bhie', att, vb)
        state = state * jnp.exp(b_end[:, :, 0])[..., None] + jnp.einsum('bhcd,bhce->bhde', kb * jnp.exp(b_end - b), vb)
        return state, o_inter + o_intra

    s_fin, o = lax.scan(step, s0, (blocks(q), blocks(k), blocks(v), blocks(log_a)))
    return o.transpose(1, 0, 3, 2, 4).reshape(B, L, H, DV), s_fin

def gla_bidir(q, k, v, la_f, la_b, s0_f, s0_b):
    o_f, s_f = gla_scan(q, k, v, la_f, s0_f)
    flip = lambda t: jnp.flip(t, axis=1)
    o_b, s_b = gla_scan(flip(q), flip(k), flip(v), flip(la_b), s0_b)
    return o_f + flip(o_b), s_f, s_b

def gla_output(o, pg, norm_g, w_o):
    B, L = o.shape[:2]
    on = rmsnorm(o, norm_g.reshape(GLA_HEADS, GLA_DV)).reshape(B, L, GLA_V)
    return (on.astype(pg.dtype) * jax.nn.silu(pg)) @ w_o

def na_latent(q, k, v, kc, vc, rpb):
    B, S, H, hd = q.shape
    rows = S // GRID_W
    kh = min(NA_KH, rows)
    kw, qc = NA_KW, NA_QC
    qr = math.gcd(rows, NA_QR)
    rr = min(qr + kh - 1, rows)
    cr = qc + kw - 1
    nrb, ncb = rows // qr, GRID_W // qc
    rs = np.clip(np.arange(rows) - kh // 2, 0, rows - kh)
    cs = np.clip(np.arange(GRID_W) - kw // 2, 0, GRID_W - kw)
    row_idx = np.minimum(rs[::qr], rows - rr)[:, None] + np.arange(rr)
    col_idx = np.minimum(cs[::qc], GRID_W - cr)[:, None] + np.arange(cr)
    q_rows = np.arange(rows).reshape(nrb, qr)
    q_cols = np.arange(GRID_W).reshape(ncb, qc)
    d_r = row_idx[:, None, :] - q_rows[:, :, None]
    d_c = col_idx[:, None, :] - q_cols[:, :, None]
    ok_r = (row_idx[:, None, :] >= rs[q_rows][:, :, None]) & (row_idx[:, None, :] < rs[q_rows][:, :, None] + kh)
    ok_c = (col_idx[:, None, :] >= cs[q_cols][:, :, None]) & (col_idx[:, None, :] < cs[q_cols][:, :, None] + kw)
    i_r = np.clip(d_r + NA_KH - 1, 0, 2 * NA_KH - 2)[:, :, :, None, None, None]
    i_c = np.clip(d_c + NA_KW - 1, 0, 2 * NA_KW - 2)[None, None, None]
    ok = ok_r[:, :, :, None, None, None] & ok_c[None, None, None]
    bias = jnp.where(ok, rpb.astype(F32)[:, i_r, i_c], -jnp.inf).transpose(0, 1, 4, 2, 5, 3, 6)
    n_lat = rr * cr

    def one_sample(args):
        qs, ks_, vs, kcs, vcs = args
        qg = qs.reshape(nrb, qr, ncb, qc, H, hd)
        kg = jnp.take(jnp.take(ks_.reshape(rows, GRID_W, H, hd), row_idx, axis=0), col_idx, axis=2)
        vg = jnp.take(jnp.take(vs.reshape(rows, GRID_W, H, hd), row_idx, axis=0), col_idx, axis=2)
        s_lat = jnp.einsum('xqyphd,xryshd->hxyqprs', qg, kg).astype(F32) + bias
        s_ctx = jnp.einsum('xqyphd,chd->hxyqpc', qg, kcs).astype(F32)
        prob = jax.nn.softmax(jnp.concatenate([s_lat.reshape(*s_lat.shape[:5], n_lat), s_ctx], axis=-1), axis=-1)
        p_lat = prob[..., :n_lat].reshape(s_lat.shape).astype(vs.dtype)
        p_ctx = prob[..., n_lat:].astype(vs.dtype)
        out = jnp.einsum('hxyqprs,xryshd->xqyphd', p_lat, vg) + jnp.einsum('hxyqpc,chd->xqyphd', p_ctx, vcs)
        return out.reshape(S, H * hd)

    return lax.map(one_sample, (q * NA_HD ** -0.5, k, v, kc, vc))

def na_context(qc, kc, vc):
    s = jnp.einsum('bihd,bjhd->bhij', qc * NA_HD ** -0.5, kc).astype(F32)
    p = jax.nn.softmax(s, axis=-1).astype(vc.dtype)
    o = jnp.einsum('bhij,bjhd->bihd', p, vc)
    return o.reshape(qc.shape[0], qc.shape[1], NA_DIM)

def merge_branches(pre_gate, b_gate, y_conv, y_gla, y_na, w_out):
    g = jax.nn.sigmoid((pre_gate + b_gate).astype(F32)).reshape(*pre_gate.shape[:-1], N_BRANCH, D_MODEL)
    m = g[..., 0, :] * y_conv + g[..., 1, :] * y_gla + g[..., 2, :] * y_na
    return m.astype(pre_gate.dtype) @ w_out

def token_mixer(h, hc, need_ctx, w_in, b_gate, conv_w, conv_b, conv_ln_g, conv_ln_b, w_conv_o,
                gla_wa2, gla_ba, gla_norm_g, w_gla_o, na_rpb, w_na_o, w_out):
    B, S, _ = h.shape
    Lc = hc.shape[1]
    l_glu, l_q, l_k, l_v, l_g, l_a, l_nq, l_nk, l_nv, l_br = split_cols(h @ w_in)
    c_glu, c_q, c_k, c_v, c_g, c_a, c_nq, c_nk, c_nv, c_br = split_cols(hc @ w_in)

    cq, ck, cv, cla_f, cla_b = gla_features(c_q, c_k, c_v, c_a, gla_wa2, gla_ba, None)
    zero = jnp.zeros((B, GLA_HEADS, GLA_DK, GLA_DV), F32)
    co_gla, s_f, s_b = gla_bidir(cq, ck, cv, cla_f, cla_b, zero, zero)
    q, k, v, la_f, la_b = gla_features(l_q, l_k, l_v, l_a, gla_wa2, gla_ba, axial_rope(S))
    o_gla, _, _ = gla_bidir(q, k, v, la_f, la_b, s_f, s_b)

    heads = lambda t, L: t.reshape(B, L, NA_HEADS, NA_HD)
    nkc, nvc = heads(c_nk, Lc), heads(c_nv, Lc)
    y_na = na_latent(heads(l_nq, S), heads(l_nk, S), heads(l_nv, S), nkc, nvc, na_rpb)

    y = merge_branches(l_br, b_gate,
                       conv_module(l_glu, conv_w, conv_b, conv_ln_g, conv_ln_b, w_conv_o),
                       gla_output(o_gla, l_g, gla_norm_g, w_gla_o),
                       y_na @ w_na_o, w_out)
    yc = None
    if need_ctx:
        yc = merge_branches(c_br, b_gate,
                            conv_module(c_glu, conv_w, conv_b, conv_ln_g, conv_ln_b, w_conv_o),
                            gla_output(co_gla, c_g, gla_norm_g, w_gla_o),
                            na_context(heads(c_nq, Lc), nkc, nvc) @ w_na_o, w_out)
    return y, yc

def peer_ffn(h, wq, sub_keys, u_tab, v_tab):
    B, L, D = h.shape
    T = B * L
    hf = h.reshape(T, D)
    qry = (hf @ wq).reshape(T, PEER_HEADS, 2, PEER_DKEY // 2)
    s = jnp.einsum('thzd,hzkd->thzk', qry, sub_keys).astype(F32)
    ts, ti = lax.top_k(s, PEER_TOPK)
    cand_s = (ts[:, :, 0, :, None] + ts[:, :, 1, None, :]).reshape(T, PEER_HEADS, PEER_TOPK * PEER_TOPK)
    cand_e = (ti[:, :, 0, :, None] * PEER_NKEYS + ti[:, :, 1, None, :]).reshape(T, PEER_HEADS, PEER_TOPK * PEER_TOPK)
    best_s, best_j = lax.top_k(cand_s, PEER_TOPK)
    experts = jnp.take_along_axis(cand_e, best_j, axis=-1)
    gates = jax.nn.softmax(best_s, axis=-1).astype(h.dtype)
    nb = T // PEER_CHUNK

    def block(args):
        hb, eb, gb = args
        act = jax.nn.gelu(jnp.einsum('td,thkd->thk', hb, jnp.take(u_tab, eb, axis=0)), approximate=False)
        return jnp.einsum('thk,thkd->td', gb * act, jnp.take(v_tab, eb, axis=0))

    out = lax.map(block, (hf.reshape(nb, PEER_CHUNK, D),
                          experts.reshape(nb, PEER_CHUNK, PEER_HEADS, PEER_TOPK),
                          gates.reshape(nb, PEER_CHUNK, PEER_HEADS, PEER_TOPK)))
    return out.reshape(B, L, D)

def setup_inputs(seed: int = 0) -> dict:
    key = jax.random.key(seed)
    ks = iter(jax.random.split(key, 40))
    D = D_MODEL
    L = DEPTH

    def nrm(shape, scale):
        return jax.random.normal(next(ks), shape, jnp.float32) * scale

    return {
        'x': nrm((BATCH, SEQ, D), 1.0),
        'c': nrm((BATCH, D), 1.0),
        'ctx': nrm((BATCH, CTX_LEN, D), 1.0),
        'c_ctx': nrm((D,), 1.0),
        'w_mod': nrm((L, D, 6 * D), 0.5 * D ** -0.5),
        'b_mod': nrm((L, 6 * D), 0.02),
        'norm1_g': 1.0 + nrm((L, D), 0.05),
        'norm2_g': 1.0 + nrm((L, D), 0.05),
        'w_in': nrm((L, D, IN_DIM), D ** -0.5),
        'b_gate': nrm((L, N_BRANCH * D), 0.02),
        'conv_w': nrm((L, CONV_WIDTH, CONV_DIM), CONV_WIDTH ** -0.5),
        'conv_b': nrm((L, CONV_DIM), 0.02),
        'conv_ln_g': 1.0 + nrm((L, CONV_DIM), 0.05),
        'conv_ln_b': nrm((L, CONV_DIM), 0.02),
        'w_conv_o': nrm((L, CONV_DIM, D), CONV_DIM ** -0.5),
        'gla_wa2': nrm((L, 2, GLA_RANK, GLA_QK), GLA_RANK ** -0.5),
        'gla_ba': nrm((L, 2, GLA_QK), 0.1),
        'gla_norm_g': 1.0 + nrm((L, GLA_V), 0.05),
        'w_gla_o': nrm((L, GLA_V, D), GLA_V ** -0.5),
        'na_rpb': nrm((L, NA_HEADS, 2 * NA_KH - 1, 2 * NA_KW - 1), 0.1),
        'w_na_o': nrm((L, NA_DIM, D), NA_DIM ** -0.5),
        'w_out': nrm((L, D, D), D ** -0.5),
        'peer_wq': nrm((L, D, PEER_HEADS * PEER_DKEY), D ** -0.5),
        'peer_keys': nrm((L, PEER_HEADS, 2, PEER_NKEYS, PEER_DKEY // 2), (PEER_DKEY // 2) ** -0.5),
        'peer_u': nrm((L, PEER_EXPERTS, D), D ** -0.5),
        'peer_v': nrm((L, PEER_EXPERTS, D), 1.0),
        'final_g': 1.0 + nrm((D,), 0.05),
    }

def reference(x, c, ctx, c_ctx, w_mod, b_mod, norm1_g, norm2_g, w_in, b_gate, conv_w, conv_b,
              conv_ln_g, conv_ln_b, w_conv_o, gla_wa2, gla_ba, gla_norm_g, w_gla_o, na_rpb, w_na_o,
              w_out, peer_wq, peer_keys, peer_u, peer_v, final_g):
    xc = ctx
    cond = jax.nn.silu(c.astype(F32))
    cond_ctx = jax.nn.silu(c_ctx.astype(F32))
    for i in range(DEPTH):
        last = i == DEPTH - 1
        mod = (cond @ w_mod[i].astype(F32) + b_mod[i].astype(F32)).astype(x.dtype)[:, None, :]
        modc = (cond_ctx @ w_mod[i].astype(F32) + b_mod[i].astype(F32)).astype(x.dtype)
        sh1, sc1, g1, sh2, sc2, g2 = jnp.split(mod, 6, axis=-1)
        csh1, csc1, cg1, csh2, csc2, cg2 = jnp.split(modc, 6, axis=-1)

        h = rmsnorm(x, norm1_g[i]) * (1 + sc1) + sh1
        hc = rmsnorm(xc, norm1_g[i]) * (1 + csc1) + csh1
        y, yc = token_mixer(h, hc, not last, w_in[i], b_gate[i], conv_w[i], conv_b[i], conv_ln_g[i],
                            conv_ln_b[i], w_conv_o[i], gla_wa2[i], gla_ba[i], gla_norm_g[i], w_gla_o[i],
                            na_rpb[i], w_na_o[i], w_out[i])
        x = x + g1 * y.astype(x.dtype)
        h2 = rmsnorm(x, norm2_g[i]) * (1 + sc2) + sh2
        x = x + g2 * peer_ffn(h2, peer_wq[i], peer_keys[i], peer_u[i], peer_v[i]).astype(x.dtype)
        if not last:
            xc = xc + cg1 * yc.astype(xc.dtype)
            hc2 = rmsnorm(xc, norm2_g[i]) * (1 + csc2) + csh2
            xc = xc + cg2 * peer_ffn(hc2, peer_wq[i], peer_keys[i], peer_u[i], peer_v[i]).astype(xc.dtype)
    return rmsnorm(x, final_g)


_drawn_inputs = setup_inputs


def setup_inputs(seed=0):
    import zlib

    import numpy as np

    out = dict(_drawn_inputs(seed))
    spreads = {}
    factors = {'b_gate': 4.209, 'conv_ln_b': 3.514, 'na_rpb': 5.467}
    for name, (base, spread) in spreads.items():
        noise = np.random.default_rng([zlib.crc32(name.encode()), seed]).standard_normal(out[name].shape)
        drawn = base * np.exp(spread * noise) if base else spread * noise
        out[name] = jnp.asarray(drawn.astype(out[name].dtype))
    for name, factor in factors.items():
        out[name] = (out[name] * factor).astype(out[name].dtype)
    return out
```

```python
from contextlib import ExitStack

import numpy as np

import concourse.bass as bass
from concourse import mybir

F32 = mybir.dt.float32
U32 = mybir.dt.uint32
ALU = mybir.AluOpType
ACT = mybir.ActivationFunctionType
AX = mybir.AxisListType

P = 128
D = 1024
KC = D // P
S = 256
NT = 2 * S
DEPTH = 2
EPS = 1e-6
GRID_W = 64
CONV, TAPS = 512, 31
HALO = TAPS // 2
CT = CONV // P
GH, GDK, GDV, GR = 4, 64, 128, 16
CH = 64
NCH = NT // CH
GATE_NORM = 16.0
NH, NHD = 8, 64
KH, KW = 8, 16
RPW = 2 * GRID_W - 1
PH, PK, NKEYS = 8, 16, 128
ET = NKEYS
RING = 8
NEG = -3.0e38

PARAMS = {}
_at = 0
for _name, _n in (("b_mod", 48), ("norm1", KC), ("norm2", KC), ("b_gate", 24), ("conv_w", TAPS * CT), ("conv_b", CT),
                  ("ln_g", CT), ("ln_b", CT), ("ba", 4), ("gla_g", GH), ("final", KC)):
    PARAMS[_name] = (_at, _at + _n)
    _at += _n
NPARAM = _at

T_GLU, T_G, T_NQ, T_Q, T_K, T_NK = 0, 8, 12, 16, 18, 20
CHANNEL_TILES = 24


class Count:

    def __init__(self, sem):
        self.sem, self.base, self.made = sem, 0, 0

    def at(self, n):
        return self.base + n

    def link(self, eng, ins):
        ins.then_inc(self.sem, 1)
        self.made += 1
        eng.wait_ge(self.sem, self.base + self.made)

    def close(self):
        self.base, self.made = self.base + self.made, 0


def build_program(nc, A, out, debug=None):
    ctx = ExitStack()
    with ctx:
        def sb(name, shape, dt=F32):
            return ctx.enter_context(nc.sbuf_tensor(name, shape, dt))

        counts = []

        def sem(name):
            return ctx.enter_context(nc.semaphore(name))

        def count(name):
            counts.append(Count(sem(name)))
            return counts[-1]

        xT = sb("xT", [P, KC, NT])
        hT = sb("hT", [P, KC, NT])
        ring = sb("ring", [P, RING, D])
        blocks = [ring[:, b, :].rearrange("p (k c) -> p k c", k=KC) for b in range(RING)]
        par = sb("par", [P, DEPTH, NPARAM])
        mod = sb("mod", [P, 48, 2])
        scale1 = sb("scale1", [P, KC, 2])
        cond = sb("cond", [P, KC, 2])
        ident = sb("ident", [P, P])
        ones = sb("ones", [P, P])
        iota = sb("iota", [P, P])
        eps_col = sb("eps_col", [P, 1])
        sel_t = sb("sel_t", [P, 3, S])
        row_onehot = sb("row_onehot", [P, 2, 2, P])
        col_onehot = sb("col_onehot", [P, 2, 2, P])
        gelu = sb("gelu", [P, 2, S])
        wact = sb("wact", [P, 2, S])
        arena = sb("arena", [P, ET * S])
        psum = ctx.enter_context(nc.psum_tensor("psum", [P, 8, 512], F32))

        def carve(at, n):
            return arena[:, at:at + n]

        proj = carve(0, CHANNEL_TILES * NT).rearrange("p (n t) -> p n t", n=CHANNEL_TILES)
        v_tok = carve(12288, 2048).rearrange("p (t c) -> p t c", t=4)
        nv_tok = carve(14336, 2048).rearrange("p (t c) -> p t c", t=4)
        conv = carve(16384, 2048).rearrange("p (n t) -> p n t", n=CT)
        o_t = carve(18432, 2048).rearrange("p (n t) -> p n t", n=GH)
        na_t = carve(20480, 2048).rearrange("p (n t) -> p n t", n=4)
        work = 22528
        upad = carve(work, CT * 2 * (S + 2 * HALO)).rearrange("p (n s t) -> p n s t", n=CT, s=2)
        sq = carve(work + 2304, 2048).rearrange("p (n t) -> p n t", n=CT)
        stat = carve(work + 4352, 1024).rearrange("p (n t) -> p n t", n=2)
        decay = carve(0, 2048).rearrange("p (n t) -> p n t", n=4)
        runsum = carve(2048, 2048).rearrange("p (n t) -> p n t", n=4)
        feat = carve(work, 4096).rearrange("p (f n t) -> p f n t", f=4, n=2)
        F_Q, F_K, F_QE, F_KE = range(4)
        ke_tok = carve(work + 4096, 1024).rearrange("p (t c) -> p t c", t=4)
        attm = carve(work + 5120, 1024).rearrange("p (t h i) -> p t h i", t=4, h=GH)
        state = carve(work + 6144, 512).rearrange("p (h e) -> p h e", h=GH)
        chunk_decay = carve(work + 6656, 16)
        a_t = carve(work + 6720, 1024).rearrange("p (z t) -> p z t", z=2)
        w_a = carve(work + 7744, 256).rearrange("p (k c) -> p k c", k=KC)
        wa2 = carve(work + 8000, 512).rearrange("p (z c) -> p z c", z=2)
        rope = carve(work + 8512, 512).rearrange("p (n t) -> p n t", n=2)
        swap = carve(work + 9024, 128)
        resets = carve(work + 9152, 512)
        na_bias = carve(work, 4096).rearrange("p (r h k) -> p r h k", r=2, h=NH)
        prob = carve(work + 4096, 1024).rearrange("p (b k) -> p b k", b=2)
        prob_t = carve(work + 5120, 1024).rearrange("p (b k q) -> p b k q", b=2, k=4)
        na_stat = carve(work + 6144, 32 * 3).rearrange("p (n u) -> p n u", n=3)
        na_mask = carve(work + 6272, 64)
        merged = carve(work, 4096).rearrange("p (n t) -> p n t", n=KC)
        gate_s = carve(work + 4096, 2048).rearrange("p (n t) -> p n t", n=4)
        branch_m = carve(work + 6144, 1024).rearrange("p (n t) -> p n t", n=2)
        nsq = carve(work, 4096).rearrange("p (n t) -> p n t", n=KC)
        nrs = carve(work + 4096, 512)
        gates = arena[:, :].rearrange("p (i t) -> p i t", i=ET)
        qry = carve(0, 4096).rearrange("p (n t) -> p n t", n=16)
        keys = carve(4096, 2048).rearrange("p (n k) -> p n k", n=16)
        score = carve(6144, 4096).rearrange("p (t n k) -> p t n k", t=2, n=16)
        top_s = carve(10240, 512).rearrange("p (t h z k) -> p t h z k", t=2, h=PH, z=2)
        top_i = carve(10752, 512)
        top_iu = top_i.bitcast(U32).rearrange("p (t h z k) -> p t h z k", t=2, h=PH, z=2)
        top_f = carve(11264, 512).rearrange("p (t h z k) -> p t h z k", t=2, h=PH, z=2)
        cand = carve(11776, 4096).rearrange("p (t h c) -> p t h c", t=2, h=PH)
        best_s = carve(15872, 256).rearrange("p (t h k) -> p t h k", t=2, h=PH)
        best_j = carve(16128, 256)
        best_ju = best_j.bitcast(U32).rearrange("p (t h k) -> p t h k", t=2, h=PH)
        best_ab = carve(16384, 512)
        best_abu = best_ab.bitcast(U32).rearrange("p (z u) -> p z u", z=2)
        best_abf = carve(16896, 512).rearrange("p (z t h k) -> p z t h k", z=2, t=2, h=PH)
        hot = carve(17408, 2048).rearrange("p (h k c) -> p h k c", h=PH, k=PK)
        picked = carve(19456, 768).rearrange("p (n t u) -> p n t u", n=3, t=2)
        gsum = carve(20224, 32).rearrange("p (n u) -> p n u", n=2)

        landed = [sem(f"block_landed_{b}") for b in range(RING)]
        used = count("block_used")
        par_in = count("param_landed")
        stage_in = count("stage_input_landed")
        pe_done = count("pe_group_done")
        act_done = count("act_step_done")
        dve_done = count("dve_step_done")
        pool_done = count("pool_step_done")
        out_done = count("output_written")
        tile_act = count("tile_evacuated_by_act")
        tile_dve = count("tile_evacuated_by_dve")

        def end_stage():
            for c in counts:
                c.close()

        segments = []
        for l in range(DEPTH):
            segments += [(A["w_mod"], l, 6), (A["w_proj"], l, 4), (A["w_merge"], l, 5), (A["w_out"], l, 1)]
            for s in range(2 if l == 0 else 1):
                segments += [(A["w_query"], l, 2), (A["w_expert"], l, 32)]
        at_segment = [0]
        rounds_before = [0]

        def load_round(sp, seg, r, before):
            src, l, _ = segments[seg]
            for b in range(RING):
                sp.wait_ge(used.sem, (before + r - 1) * RING + b + 1)
                sp.dma_start(ring[:, b, :], src[l, r * RING + b]).then_inc(landed[b], 16)

        def load_first(sp):
            src, l, _ = segments[0]
            for b in range(RING):
                sp.dma_start(ring[:, b, :], src[l, b]).then_inc(landed[b], 16)

        def load_segment(sp):
            seg, before = at_segment[0], rounds_before[0]
            n = segments[seg][2]
            if n > 2:
                with sp.Fori(1, n) as r:
                    load_round(sp, seg, r, before)
            elif n == 2:
                load_round(sp, seg, 1, before)
            if seg + 1 < len(segments):
                load_round(sp, seg + 1, 0, before + n)

        def end_segment():
            rounds_before[0] += segments[at_segment[0]][2]
            at_segment[0] += 1
            end_stage()

        def arrived(pe, r, b):
            pe.wait_ge(landed[b], (r + rounds_before[0] + 1) * 16)

        def col(l, name, i):
            a = PARAMS[name][0] + i
            return par[:, l, a:a + 1]

        def start():
            block = nc.Block()
            with block as block:
                @block.sync
                def _(sp):
                    sp.dma_start(xT[:], A["x"]).then_inc(par_in.sem, 16)
                    sp.dma_start(par[:], A["params"]).then_inc(par_in.sem, 16)
                    sp.dma_start(cond[:], A["cond"]).then_inc(par_in.sem, 16)
                    sp.dma_start(ident[:], A["ident"]).then_inc(par_in.sem, 16)
                    sp.dma_start(iota[:], A["iota"]).then_inc(par_in.sem, 16)
                    load_first(sp)

                @block.vector
                def _(dve):
                    nc.vector.memset(ones[:], 1.0)
                    nc.vector.memset(eps_col[:], EPS)
                    dve.sem_inc(tile_dve.sem, 8)

                @block.scalar
                def _(act):
                    act.wait_ge(par_in.sem, 80)
                    nc.scalar.activation(cond[:], cond[:], ACT.Silu)
                    act.sem_inc(tile_act.sem, 8)
            par_in.made = 80
            tile_dve.made = 8
            tile_act.made = 8
            end_stage()

        def modulation(l):
            with nc.Block() as block:
                @block.sync
                def _(sp):
                    load_segment(sp)

                @block.tensor
                def _(pe):
                    with pe.Fori(0, 6) as r:
                        for b in range(RING):
                            arrived(pe, r, b)
                            m = psum[:, 0, 0:96].rearrange("p (n s) -> p n s", s=2)
                            for k in range(KC):
                                mm = nc.tensor.matmul(m[:, r * RING + b, :], blocks[b][:, k, :], cond[:, k, :],
                                                      start=(k == 0), stop=(k == KC - 1))
                            mm.then_inc(used.sem, 1)
                    used.made += 48

                @block.vector
                def _(dve):
                    dve.wait_ge(used.sem, used.at(48))
                    a, b = PARAMS["b_mod"]
                    m = psum[:, 0, 0:96].rearrange("p (n s) -> p n s", s=2)
                    for s in range(2):
                        dve_done.link(dve, nc.vector.tensor_tensor(mod[:, :, s], m[:, :, s], par[:, l, a:b], ALU.add))
            end_segment()

        def adaln(l, which, nt):
            sh, sc = (0, 8) if which == 0 else (24, 32)
            g0, g1 = PARAMS["norm1" if which == 0 else "norm2"]
            with nc.Block() as block:
                @block.scalar
                def _(act):
                    for k in range(KC):
                        nc.scalar.activation(nsq[:, k, 0:nt], xT[:, k, 0:nt], ACT.Square).then_inc(act_done.sem, 1)
                    act.wait_ge(pe_done.sem, pe_done.at(1))
                    nc.scalar.activation(nrs[:, 0:nt], psum[:, 0, 0:nt], ACT.Sqrt, bias=eps_col[:],
                                         scale=1.0 / D).then_inc(act_done.sem, 1)
                    for k in range(KC):
                        for s in range(nt // S):
                            act.wait_ge(dve_done.sem, dve_done.at(3 + k * (nt // S) + s + 1))
                            nc.scalar.activation(hT[:, k, s * S:s * S + S], hT[:, k, s * S:s * S + S], ACT.Identity,
                                                 bias=mod[:, sh + k, s:s + 1]).then_inc(act_done.sem, 1)
                    act_done.made += KC + 1 + KC * nt // S

                @block.tensor
                def _(pe):
                    for k in range(KC):
                        pe.wait_ge(act_done.sem, act_done.at(k + 1))
                        mm = nc.tensor.matmul(psum[:, 0, 0:nt], ones[:], nsq[:, k, 0:nt], start=(k == 0), stop=(k == KC - 1))
                    mm.then_inc(pe_done.sem, 1)
                    pe_done.made += 1

                @block.vector
                def _(dve):
                    for s in range(2):
                        dve_done.link(dve, nc.vector.scalar_tensor_tensor(
                            out=scale1[:, :, s], in0=mod[:, sc:sc + KC, s], scalar=1.0, in1=par[:, l, g0:g1],
                            op0=ALU.add, op1=ALU.mult))
                    dve.wait_ge(act_done.sem, act_done.at(KC + 1))
                    dve_done.link(dve, nc.vector.reciprocal(nrs[:, 0:nt], nrs[:, 0:nt]))
                    for k in range(KC):
                        for s in range(nt // S):
                            t = slice(s * S, s * S + S)
                            nc.vector.scalar_tensor_tensor(
                                out=hT[:, k, t], in0=xT[:, k, t], scalar=scale1[:, k, s:s + 1], in1=nrs[:, t],
                                op0=ALU.mult, op1=ALU.mult).then_inc(dve_done.sem, 1)
                    dve_done.made += KC * nt // S
            end_stage()

        def projection(l, nt):
            with nc.Block() as block:
                @block.sync
                def _(sp):
                    load_segment(sp)

                @block.tensor
                def _(pe):
                    def tile(r, b, width):
                        arrived(pe, r, b)
                        back = tile_act if b % 2 == 0 else tile_dve
                        pe.wait_ge(back.sem, r * 4 + back.at(b // 2 - 3))
                        for k in range(KC):
                            mm = nc.tensor.matmul(psum[:, b, 0:width], blocks[b][:, k, :], hT[:, k, 0:width],
                                                  start=(k == 0), stop=(k == KC - 1))
                        mm.then_inc(used.sem, 1)

                    with pe.Fori(0, 2) as r:
                        for b in range(RING):
                            tile(r, b, nt)
                    for b in range(RING):
                        tile(2, b, nt if b < 2 else NT)
                    for b in range(RING):
                        arrived(pe, 3, b)
                        back = tile_act if b % 2 == 0 else tile_dve
                        pe.wait_ge(back.sem, back.at(12 + b // 2 - 3))
                        for tt in range(4):
                            for k in range(KC):
                                mm = nc.tensor.matmul(psum[:, b, tt * P:tt * P + P], hT[:, k, tt * P:tt * P + P],
                                                      blocks[b][:, k, :], start=(k == 0), stop=(k == KC - 1))
                        mm.then_inc(used.sem, 1)
                    used.made += 32

                def evacuate(eng, copy, parity, back):
                    def one(r, b, width):
                        eng.wait_ge(used.sem, r * RING + used.at(b + 1))
                        copy(proj[:, r * RING + b, 0:width], psum[:, b, 0:width]).then_inc(back.sem, 1)

                    with eng.Fori(0, 2) as r:
                        for b in range(parity, RING, 2):
                            one(r, b, nt)
                    for b in range(parity, RING, 2):
                        one(2, b, nt if b < 2 else NT)
                    for b in range(parity, RING, 2):
                        eng.wait_ge(used.sem, used.at(24 + b + 1))
                        to = (v_tok if b < 4 else nv_tok)[:, :, (b % 4) * P:(b % 4) * P + P]
                        copy(to, psum[:, b, :].rearrange("p (t c) -> p t c", t=4)).then_inc(back.sem, 1)
                    back.made += 16

                @block.scalar
                def _(act):
                    evacuate(act, nc.scalar.copy, 0, tile_act)

                @block.vector
                def _(dve):
                    evacuate(dve, nc.vector.tensor_copy, 1, tile_dve)
            end_segment()

        def conv_module(l, nt):
            ns = nt // S
            acc = [conv[:, c, 0:nt].rearrange("p (s t) -> p s t", s=ns) for c in range(CT)]
            glu = proj[:, T_GLU:T_GLU + 4, 0:nt]
            gate = proj[:, T_GLU + 4:T_GLU + 8, 0:nt]
            w0 = PARAMS["conv_w"][0]
            cw = par[:, l, w0:w0 + TAPS * CT].rearrange("p (w c) -> p w c", c=CT)
            with nc.Block() as block:
                @block.scalar
                def _(act):
                    act_done.link(act, nc.scalar.activation(gate, gate, ACT.Sigmoid))
                    for c in range(CT):
                        act.wait_ge(dve_done.sem, dve_done.at(5 + CT * TAPS + 1 + c + 1))
                        nc.scalar.activation(sq[:, c, 0:nt], conv[:, c, 0:nt], ACT.Square).then_inc(act_done.sem, 1)
                    act.wait_ge(pe_done.sem, pe_done.at(2))
                    nc.scalar.activation(stat[:, 1, 0:nt], psum[:, 1, 0:nt], ACT.Sqrt, bias=eps_col[:],
                                         scale=1.0 / CONV).then_inc(act_done.sem, 1)
                    for c in range(CT):
                        act.wait_ge(dve_done.sem, dve_done.at(5 + CT * TAPS + 1 + CT + 1 + c + 1))
                        nc.scalar.activation(conv[:, c, 0:nt], conv[:, c, 0:nt], ACT.Silu,
                                             bias=col(l, "ln_b", c)).then_inc(act_done.sem, 1)
                    act_done.made += CT + 1 + CT

                @block.tensor
                def _(pe):
                    pe.wait_ge(dve_done.sem, dve_done.at(5 + CT * TAPS))
                    for c in range(CT):
                        mm = nc.tensor.matmul(psum[:, 0, 0:nt], ones[:], conv[:, c, 0:nt], start=(c == 0), stop=(c == CT - 1))
                    mm.then_inc(pe_done.sem, 1)
                    for c in range(CT):
                        pe.wait_ge(act_done.sem, act_done.at(1 + c + 1))
                        mm = nc.tensor.matmul(psum[:, 1, 0:nt], ones[:], sq[:, c, 0:nt], start=(c == 0), stop=(c == CT - 1))
                    mm.then_inc(pe_done.sem, 1)
                    pe_done.made += 2

                @block.vector
                def _(dve):
                    nc.vector.memset(upad, 0.0).then_inc(dve_done.sem, 1)
                    dve.wait_ge(dve_done.sem, dve_done.at(1))
                    dve.wait_ge(act_done.sem, act_done.at(1))
                    for c in range(CT):
                        nc.vector.tensor_tensor(
                            upad[:, c, 0:ns, HALO:HALO + S], glu[:, c, :].rearrange("p (s t) -> p s t", s=ns),
                            gate[:, c, :].rearrange("p (s t) -> p s t", s=ns), ALU.mult).then_inc(dve_done.sem, 1)
                    for c in range(CT):
                        dve.wait_ge(dve_done.sem, dve_done.at(1 + c + 1))
                        nc.vector.tensor_scalar(acc[c], upad[:, c, 0:ns, 0:S], cw[:, 0, c:c + 1], col(l, "conv_b", c),
                                                ALU.mult, ALU.add).then_inc(dve_done.sem, 1)
                    with dve.Fori(1, TAPS) as w:
                        for c in range(CT):
                            dve.wait_ge(dve_done.sem, w * CT + dve_done.at(5 + c + 1 - CT))
                            nc.vector.scalar_tensor_tensor(
                                out=acc[c], in0=upad[:, c, 0:ns, bass.ds(w, S)], scalar=cw[:, w, c:c + 1], in1=acc[c],
                                op0=ALU.mult, op1=ALU.add).then_inc(dve_done.sem, 1)
                    n = 5 + CT * TAPS
                    dve.wait_ge(pe_done.sem, pe_done.at(1))
                    nc.vector.tensor_scalar(stat[:, 0, 0:nt], psum[:, 0, 0:nt], 1.0 / CONV, None,
                                            ALU.mult).then_inc(dve_done.sem, 1)
                    dve.wait_ge(dve_done.sem, dve_done.at(n + 1))
                    for c in range(CT):
                        nc.vector.tensor_tensor(conv[:, c, 0:nt], conv[:, c, 0:nt], stat[:, 0, 0:nt],
                                                ALU.subtract).then_inc(dve_done.sem, 1)
                    dve.wait_ge(act_done.sem, act_done.at(1 + CT + 1))
                    nc.vector.reciprocal(stat[:, 1, 0:nt], stat[:, 1, 0:nt]).then_inc(dve_done.sem, 1)
                    dve.wait_ge(dve_done.sem, dve_done.at(n + 1 + CT + 1))
                    for c in range(CT):
                        nc.vector.scalar_tensor_tensor(
                            out=conv[:, c, 0:nt], in0=conv[:, c, 0:nt], scalar=col(l, "ln_g", c), in1=stat[:, 1, 0:nt],
                            op0=ALU.mult, op1=ALU.mult).then_inc(dve_done.sem, 1)
                    dve_done.made += n + 1 + CT + 1 + CT
            end_stage()

        def gla_features(l):
            with nc.Block() as block:
                @block.sync
                def _(sp):
                    for to, src in ((w_a, A["w_a"][l]), (wa2[0:GR], A["wa2"][l]), (rope, A["rope"]), (swap, A["swap"]),
                                    (resets, A["resets"])):
                        sp.dma_start(to, src).then_inc(stage_in.sem, 16)
                    stage_in.made += 80

                @block.tensor
                def _(pe):
                    pe.wait_ge(stage_in.sem, stage_in.at(80))
                    for z in range(2):
                        for k in range(KC):
                            mm = nc.tensor.matmul(psum[0:GR, z, :], w_a[:, k, z * GR:z * GR + GR], hT[:, k, :],
                                                  start=(k == 0), stop=(k == KC - 1))
                        mm.then_inc(pe_done.sem, 1)
                    for i in range(4):
                        nc.tensor.matmul(psum[:, 6 + i // 2, (i % 2) * S:(i % 2) * S + S], swap, proj[:, T_Q + i, 0:S],
                                         start=True, stop=True).then_inc(pe_done.sem, 1)
                    for z in range(2):
                        pe.wait_ge(act_done.sem, act_done.at(z + 1))
                        for n in range(2):
                            mm = nc.tensor.matmul(psum[:, 2 + 2 * z + n, :], wa2[0:GR, z, n * P:n * P + P], a_t[0:GR, z, :],
                                                  start=True, stop=True)
                        mm.then_inc(pe_done.sem, 1)
                    pe_done.made += 8

                @block.scalar
                def _(act):
                    for z in range(2):
                        act.wait_ge(pe_done.sem, pe_done.at(z + 1))
                        nc.scalar.copy(a_t[0:GR, z, :], psum[0:GR, z, :]).then_inc(act_done.sem, 1)
                    act.wait_ge(pe_done.sem, pe_done.at(8))
                    for i in range(4):
                        nc.scalar.activation(decay[:, i, :], psum[:, 2 + i, :], ACT.Identity,
                                             bias=col(l, "ba", i)).then_inc(act_done.sem, 1)
                    act.wait_ge(dve_done.sem, dve_done.at(12 + 1))
                    nc.scalar.activation(runsum, runsum, ACT.Exp, scale=-1.0).then_inc(act_done.sem, 1)
                    act.wait_ge(act_done.sem, act_done.at(7))
                    nc.scalar.activation(runsum, runsum, ACT.Ln, bias=1.0).then_inc(act_done.sem, 1)
                    act_done.made += 8

                @block.vector
                def _(dve):
                    dve.wait_ge(pe_done.sem, pe_done.at(6))
                    dve.wait_ge(stage_in.sem, stage_in.at(80))
                    for i in range(4):
                        x = proj[:, T_Q + i, 0:S]
                        tmp = feat[:, 0, 0, 0:S]
                        dve_done.link(dve, nc.vector.tensor_tensor(tmp, psum[:, 6 + i // 2, (i % 2) * S:(i % 2) * S + S],
                                                                   rope[:, 1, :], ALU.mult))
                        dve_done.link(dve, nc.vector.tensor_tensor(x, x, rope[:, 0, :], ALU.mult))
                        dve_done.link(dve, nc.vector.tensor_tensor(x, x, tmp, ALU.add))
                    dve.wait_ge(act_done.sem, act_done.at(6))
                    dve_done.link(dve, nc.vector.scalar_tensor_tensor(out=runsum, in0=decay, scalar=-1.0, in1=decay,
                                                                      op0=ALU.mult, op1=ALU.max))
                    dve.wait_ge(act_done.sem, act_done.at(8))
                    dve_done.link(dve, nc.vector.scalar_tensor_tensor(out=decay, in0=decay, scalar=0.0, in1=runsum,
                                                                      op0=ALU.min, op1=ALU.subtract))
                    for i in range(4):
                        step = 1 if i < 2 else -1
                        dve_done.link(dve, nc.vector.tensor_tensor_scan(
                            runsum[:, i, ::step], resets, decay[:, i, ::step], 0.0, ALU.mult, ALU.add))
            end_stage()

        def gla_direction(l, z, nt):
            mid, end = (CH // 2, CH - 1) if z == 0 else (CH // 2 - 1, 0)
            b = runsum[:, 2 * z:2 * z + 2, :]
            bc = b.rearrange("p n (c i) -> p (n c) i", i=CH)
            fq, fk, fqe, fke = (feat[:, f, :, :] for f in (F_Q, F_K, F_QE, F_KE))

            def chunks(x):
                return x.rearrange("p n (c i) -> p (n c) i", i=CH)
            with nc.Block() as block:
                @block.vector
                def _(dve):
                    n = [P, 2 * NCH, CH]
                    dve_done.link(dve, nc.vector.tensor_tensor(chunks(fq), bc, bc[:, :, mid:mid + 1].to_broadcast(n),
                                                               ALU.subtract))
                    dve_done.link(dve, nc.vector.tensor_tensor(chunks(fke), bc[:, :, end:end + 1].to_broadcast(n), bc,
                                                               ALU.subtract))
                    k = proj[:, T_K:T_K + 2, :]
                    q = proj[:, T_Q:T_Q + 2, 0:nt]
                    dve.wait_ge(act_done.sem, act_done.at(1))
                    nc.vector.tensor_tensor(fk, fk, k, ALU.mult).then_inc(dve_done.sem, 1)
                    dve.wait_ge(act_done.sem, act_done.at(2))
                    nc.vector.tensor_tensor(fke, fke, k, ALU.mult).then_inc(dve_done.sem, 1)
                    for j, f in ((3, fq), (4, fqe)):
                        dve.wait_ge(act_done.sem, act_done.at(j))
                        nc.vector.scalar_tensor_tensor(out=f[:, :, 0:nt], in0=q, scalar=GDK ** -0.5, in1=f[:, :, 0:nt],
                                                       op0=ALU.mult, op1=ALU.mult).then_inc(dve_done.sem, 1)
                    nc.vector.memset(state, 0.0).then_inc(dve_done.sem, 1)
                    for n in range(2):
                        dve.wait_ge(pe_done.sem, pe_done.at(n + 1))
                        nc.vector.tensor_copy(ke_tok[:, :, n * P:n * P + P],
                                              psum[:, 2 + n, :].rearrange("p (t c) -> p t c", t=4)).then_inc(dve_done.sem, 1)
                    dve_done.made += 7

                @block.scalar
                def _(act):
                    s = 1.0 / GATE_NORM
                    act.wait_ge(dve_done.sem, dve_done.at(2))
                    nc.scalar.activation(fk, fq, ACT.Exp, scale=-s).then_inc(act_done.sem, 1)
                    nc.scalar.activation(fke, fke, ACT.Exp, scale=s).then_inc(act_done.sem, 1)
                    act.wait_ge(act_done.sem, act_done.at(1))
                    nc.scalar.activation(fq, fq, ACT.Exp, scale=s).then_inc(act_done.sem, 1)
                    nc.scalar.activation(fqe, b, ACT.Exp, scale=s).then_inc(act_done.sem, 1)
                    nc.scalar.activation(chunk_decay, bc[:, :, end], ACT.Exp, scale=s).then_inc(act_done.sem, 1)
                    for i in range(2):
                        act.wait_ge(pe_done.sem, pe_done.at(3 + i))
                        w = nt // P
                        nc.scalar.copy(attm[:, 0:w, i::2, :],
                                       psum[:, i, :].rearrange("p (t h i) -> p t h i", t=4, h=2)[:, 0:w]).then_inc(act_done.sem, 1)
                    act_done.made += 7

                @block.gpsimd
                def _(pool):
                    pool.wait_ge(act_done.sem, act_done.at(7))
                    w = nt // P
                    for half in range(2):
                        m = attm[half * CH:half * CH + CH, 0:w, :, :].rearrange("p t h i -> p (t h) i")
                        sign = 1 if z == 0 else -1
                        nc.gpsimd.affine_select(out=m, in_=m, compare_op=ALU.is_ge, fill=0.0, base=0,
                                                pattern=[[0, w * GH], [sign, CH]], channel_multiplier=-sign).then_inc(pool_done.sem, 1)
                    pool_done.made += 2

                @block.tensor
                def _(pe):
                    pe.wait_ge(dve_done.sem, dve_done.at(4))
                    for n in range(2):
                        for tt in range(4):
                            mm = nc.tensor.transpose(psum[:, 2 + n, tt * P:tt * P + P], fke[:, n, tt * P:tt * P + P], ident[:])
                        mm.then_inc(pe_done.sem, 1)
                    pe.wait_ge(dve_done.sem, dve_done.at(6))
                    for i in range(2):
                        for c in range(nt // CH):
                            for n in range(2):
                                rows = slice(i * GDK, i * GDK + GDK)
                                at = ((c // 2) * 2 + n) * CH
                                mm = nc.tensor.matmul(psum[(c % 2) * CH:(c % 2) * CH + CH, i, at:at + CH],
                                                      fk[rows, n, c * CH:c * CH + CH], fq[rows, n, c * CH:c * CH + CH],
                                                      start=True, stop=True)
                        mm.then_inc(pe_done.sem, 1)
                    pe_done.made += 4
            end_stage()

            order = [4, 5, 6, 7, 0, 1, 2, 3] if z == 0 else [7, 6, 5, 4, 3, 2, 1, 0]
            shown = [c < nt // CH for c in order]
            before = [sum(4 + shown[j] for j in range(n)) for n in range(NCH + 1)]
            with nc.Block() as block:
                @block.tensor
                def _(pe):
                    for n, c in enumerate(order):
                        tt, half = c // 2, slice((c % 2) * CH, (c % 2) * CH + CH)
                        for h in range(GH):
                            rows = slice((h % 2) * GDK, (h % 2) * GDK + GDK)
                            if n >= 2:
                                pe.wait_ge(dve_done.sem, dve_done.at(before[n - 1]))
                            mm = nc.tensor.matmul(psum[rows, 2 + n % 2, (h // 2) * P:(h // 2) * P + P],
                                                  ke_tok[half, tt, h * GDK:h * GDK + GDK], v_tok[half, tt, h * P:h * P + P],
                                                  start=True, stop=True)
                        mm.then_inc(pe_done.sem, 1)
                        if n > 0:
                            pe.wait_ge(dve_done.sem, dve_done.at(before[n]))
                        if shown[n]:
                            for h in range(GH):
                                o = psum[:, n % 2, h * CH:h * CH + CH]
                                nc.tensor.matmul(o, state[:, h, :], fqe[:, h // 2, c * CH:c * CH + CH], start=True, stop=False)
                                mm = nc.tensor.matmul(o, v_tok[half, tt, h * P:h * P + P], attm[half, tt, h, :],
                                                      start=False, stop=True)
                            mm.then_inc(pe_done.sem, 1)
                    pe_done.made += NCH + sum(shown)

                @block.vector
                def _(dve):
                    got = 0
                    for n, c in enumerate(order):
                        got += 1 + shown[n]
                        dve.wait_ge(pe_done.sem, pe_done.at(got))
                        if shown[n]:
                            o = o_t[:, :, c * CH:c * CH + CH]
                            p = psum[:, n % 2, 0:GH * CH].rearrange("p (h i) -> p h i", h=GH)
                            if z == 0:
                                nc.vector.tensor_copy(o, p).then_inc(dve_done.sem, 1)
                            else:
                                nc.vector.tensor_tensor(o, o, p, ALU.add).then_inc(dve_done.sem, 1)
                        for h in range(GH):
                            rows = slice((h % 2) * GDK, (h % 2) * GDK + GDK)
                            if n > 0:
                                dve.wait_ge(dve_done.sem, dve_done.at(before[n]))
                            nc.vector.scalar_tensor_tensor(
                                out=state[rows, h, :], in0=state[rows, h, :],
                                scalar=chunk_decay[rows, (h // 2) * NCH + c:(h // 2) * NCH + c + 1],
                                in1=psum[rows, 2 + n % 2, (h // 2) * P:(h // 2) * P + P],
                                op0=ALU.mult, op1=ALU.add).then_inc(dve_done.sem, 1)
                    dve_done.made += before[NCH]
            end_stage()

        def gla_output(l, nt):
            g = proj[:, T_G:T_G + GH, 0:nt]
            o = o_t[:, :, 0:nt]
            osq = feat.rearrange("p f n t -> p (f n) t")[:, 0:4, 0:nt]
            ors = feat.rearrange("p f n t -> p (f n) t")[:, 4:8, 0:nt]
            with nc.Block() as block:
                @block.scalar
                def _(act):
                    nc.scalar.activation(osq, o, ACT.Square).then_inc(act_done.sem, 1)
                    nc.scalar.activation(g, g, ACT.Silu).then_inc(act_done.sem, 1)
                    act.wait_ge(pe_done.sem, pe_done.at(1))
                    nc.scalar.activation(ors, psum[:, 0:4, 0:nt], ACT.Sqrt, bias=eps_col[:],
                                         scale=1.0 / GDV).then_inc(act_done.sem, 1)
                    act_done.made += 3

                @block.tensor
                def _(pe):
                    pe.wait_ge(act_done.sem, act_done.at(1))
                    for h in range(GH):
                        mm = nc.tensor.matmul(psum[:, h, 0:nt], ones[:], osq[:, h, :], start=True, stop=True)
                    mm.then_inc(pe_done.sem, 1)
                    pe_done.made += 1

                @block.vector
                def _(dve):
                    dve.wait_ge(act_done.sem, act_done.at(3))
                    dve_done.link(dve, nc.vector.reciprocal(ors, ors))
                    dve_done.link(dve, nc.vector.tensor_tensor(ors, ors, g, ALU.mult))
                    for h in range(GH):
                        nc.vector.scalar_tensor_tensor(out=o[:, h, :], in0=o[:, h, :], scalar=col(l, "gla_g", h),
                                                       in1=ors[:, h, :], op0=ALU.mult, op1=ALU.mult).then_inc(dve_done.sem, 1)
                    dve_done.made += GH
            end_stage()

        def neighbourhood(l, nt):
            units = [(qt, h) for qt in range(nt // P) for h in range(NH)]
            rows_of = [slice((h % 2) * NHD, (h % 2) * NHD + NHD) for h in range(NH)]
            with nc.Block() as block:
                @block.sync
                def _(sp):
                    for row in range(4):
                        half = slice((row % 2) * GRID_W, (row % 2) * GRID_W + GRID_W)
                        for h in range(NH):
                            at = ((l * NH + h) * (2 * KH - 1) + KH - 1 - row) * RPW
                            rpb = bass.AP(tensor=A["rpb"].tensor, offset=at, ap=[[1, GRID_W], [RPW, 4], [1, GRID_W]])
                            to = na_bias[half, row // 2, h].rearrange("p (r c) -> p r c", c=GRID_W)
                            sp.dma_start(to, rpb).then_inc(stage_in.sem, 16)
                    sp.dma_start(na_mask, A["na_mask"]).then_inc(stage_in.sem, 16)
                    stage_in.made += 16 * (4 * NH + 1)

                def keys_of(qt):
                    return 0 if qt < 2 else S

                @block.tensor
                def _(pe):
                    def scores(u):
                        qt, h = units[u]
                        if u >= 2:
                            pe.wait_ge(dve_done.sem, dve_done.at(1 + 6 * (u - 2) + 2))
                        k0 = keys_of(qt)
                        nc.tensor.matmul(psum[:, u % 2, k0:NT], proj[rows_of[h], T_NQ + h // 2, qt * P:qt * P + P],
                                         proj[rows_of[h], T_NK + h // 2, k0:NT], start=True, stop=True).then_inc(pe_done.sem, 1)

                    def transposes(u):
                        qt, h = units[u]
                        pe.wait_ge(dve_done.sem, dve_done.at(1 + 6 * u + 6))
                        if u >= 2:
                            pe.wait_ge(act_done.sem, act_done.at(2 + 3 * (u - 2)))
                        for kt in range(keys_of(qt) // P, 4):
                            mm = nc.tensor.transpose(psum[:, 2 + u % 2, kt * P:kt * P + P], prob[:, u % 2, kt * P:kt * P + P], ident[:])
                        mm.then_inc(pe_done.sem, 1)

                    def values(u):
                        qt, h = units[u]
                        pe.wait_ge(act_done.sem, act_done.at(2 + 3 * u))
                        if u >= 2:
                            pe.wait_ge(act_done.sem, act_done.at(3 + 3 * (u - 2)))
                        k0 = keys_of(qt) // P
                        for kt in range(k0, 4):
                            mm = nc.tensor.matmul(psum[rows_of[h], 4 + u % 2, 0:P], nv_tok[:, kt, h * NHD:h * NHD + NHD],
                                                  prob_t[:, u % 2, kt, :], start=(kt == k0), stop=(kt == 3))
                        mm.then_inc(pe_done.sem, 1)

                    scores(0)
                    for u in range(len(units)):
                        if u + 1 < len(units):
                            scores(u + 1)
                        else:
                            pass
                        transposes(u)
                        values(u)
                    pe_done.made += 3 * len(units)

                def pe_at(u, what):
                    last = len(units) - 1
                    if what == "scores":
                        return 1 if u == 0 else 1 + 3 * (u - 1) + 1
                    return 1 + 3 * u + (1 if u < last else 0) + {"transposes": 1, "values": 2}[what]

                @block.scalar
                def _(act):
                    for u, (qt, h) in enumerate(units):
                        k0 = keys_of(qt)
                        act.wait_ge(dve_done.sem, dve_done.at(1 + 6 * u + 4))
                        nc.scalar.activation(prob[:, u % 2, k0:NT], prob[:, u % 2, k0:NT], ACT.Exp,
                                             bias=na_stat[:, 0, u:u + 1], accum_out=na_stat[:, 1, u:u + 1]).then_inc(act_done.sem, 1)
                        act.wait_ge(pe_done.sem, pe_done.at(pe_at(u, "transposes")))
                        if u >= 2:
                            act.wait_ge(pe_done.sem, pe_done.at(pe_at(u - 2, "values")))
                        nc.scalar.copy(prob_t[:, u % 2, k0 // P:4, :],
                                       psum[:, 2 + u % 2, k0:NT].rearrange("p (k q) -> p k q", q=P)).then_inc(act_done.sem, 1)
                        act.wait_ge(pe_done.sem, pe_done.at(pe_at(u, "values")))
                        nc.scalar.copy(na_t[rows_of[h], h // 2, qt * P:qt * P + P],
                                       psum[rows_of[h], 4 + u % 2, 0:P]).then_inc(act_done.sem, 1)
                    act_done.made += 3 * len(units)

                @block.vector
                def _(dve):
                    dve.wait_ge(stage_in.sem, stage_in.at(16 * (4 * NH + 1)))
                    biasv = na_bias.rearrange("p r h (k c) -> p (r h k) c", c=GRID_W)
                    dve_done.link(dve, nc.vector.tensor_tensor(
                        biasv, biasv, na_mask.unsqueeze(1).to_broadcast([P, 2 * NH * 4, GRID_W]), ALU.add))
                    for u, (qt, h) in enumerate(units):
                        k0 = keys_of(qt)
                        dve.wait_ge(pe_done.sem, pe_done.at(pe_at(u, "scores")))
                        if u >= 2:
                            dve.wait_ge(pe_done.sem, pe_done.at(pe_at(u - 2, "transposes")))
                        s = prob[:, u % 2, :]
                        if k0 == 0:
                            dve_done.link(dve, nc.vector.scalar_tensor_tensor(
                                out=s[:, 0:S].rearrange("p (r c) -> p r c", c=GRID_W),
                                in0=psum[:, u % 2, 0:S].rearrange("p (r c) -> p r c", c=GRID_W), scalar=NHD ** -0.5,
                                in1=na_bias[:, qt, h, :].rearrange("p (r c) -> p r c", c=GRID_W)[:, :, ::-1],
                                op0=ALU.mult, op1=ALU.add))
                            rest = S
                        else:
                            dve_done.link(dve, nc.vector.tensor_scalar(s[:, S:S + P], psum[:, u % 2, S:S + P], NHD ** -0.5, None,
                                                                       ALU.mult))
                            rest = S + P
                        dve_done.link(dve, nc.vector.tensor_scalar(s[:, rest:NT], psum[:, u % 2, rest:NT], NHD ** -0.5, None,
                                                                   ALU.mult))
                        dve_done.link(dve, nc.vector.tensor_reduce(na_stat[:, 2, u:u + 1], s[:, k0:NT], AX.X, ALU.max))
                        dve_done.link(dve, nc.vector.tensor_scalar(na_stat[:, 0, u:u + 1], na_stat[:, 2, u:u + 1], -1.0, None, ALU.mult))
                        dve.wait_ge(act_done.sem, act_done.at(3 * u + 1))
                        dve_done.link(dve, nc.vector.reciprocal(na_stat[:, 2, u:u + 1], na_stat[:, 1, u:u + 1]))
                        dve_done.link(dve, nc.vector.tensor_scalar(s[:, k0:NT], s[:, k0:NT], na_stat[:, 2, u:u + 1], None, ALU.mult))
            end_stage()

        def merge(l, nt):
            branch = (conv, o_t, na_t)
            with nc.Block() as block:
                @block.sync
                def _(sp):
                    load_segment(sp)

                @block.tensor
                def _(pe):
                    for d in range(KC):
                        for j in range(3):
                            n = 5 * d + j
                            p = 3 * d + j
                            arrived(pe, n // RING, n % RING)
                            if p >= 4:
                                pe.wait_ge(act_done.sem, act_done.at(p - 3))
                            for k in range(KC):
                                mm = nc.tensor.matmul(psum[:, p % 4, 0:nt], blocks[n % RING][:, k, :], hT[:, k, 0:nt],
                                                      start=(k == 0), stop=(k == KC - 1))
                            mm.then_inc(used.sem, 1)
                        for j in range(3):
                            n = 5 * d + 3 + j // 2
                            p = 3 * d + j
                            if j != 1:
                                arrived(pe, n // RING, n % RING)
                            if p >= 4:
                                q = p - 4
                                pe.wait_ge(dve_done.sem, dve_done.at(5 * (q // 3) + (1, 2, 4)[q % 3]))
                            for k in range(4):
                                mm = nc.tensor.matmul(psum[:, 4 + p % 4, 0:nt], blocks[n % RING][:, 4 * (j % 2) + k, :],
                                                      branch[j][:, k, 0:nt], start=(k == 0), stop=(k == 3))
                            if j != 0:
                                mm.then_inc(used.sem, 1)
                    used.made += 40

                @block.scalar
                def _(act):
                    for p in range(3 * KC):
                        d, j = p // 3, p % 3
                        act.wait_ge(used.sem, used.at(5 * d + j + 1))
                        if p >= 4:
                            q = p - 4
                            act.wait_ge(dve_done.sem, dve_done.at(5 * (q // 3) + (1, 2, 4)[q % 3]))
                        nc.scalar.activation(gate_s[:, p % 4, 0:nt], psum[:, p % 4, 0:nt], ACT.Sigmoid,
                                             bias=col(l, "b_gate", j * KC + d)).then_inc(act_done.sem, 1)
                    act_done.made += 3 * KC

                @block.vector
                def _(dve):
                    for d in range(KC):
                        m = merged[:, d, 0:nt]
                        for j in range(3):
                            p = 3 * d + j
                            dve.wait_ge(act_done.sem, act_done.at(p + 1))
                            dve.wait_ge(used.sem, used.at(5 * d + (4, 4, 5)[j]))
                            to = m if j == 0 else branch_m[:, j - 1, 0:nt]
                            dve_done.link(dve, nc.vector.tensor_tensor(to, psum[:, 4 + p % 4, 0:nt], gate_s[:, p % 4, 0:nt], ALU.mult))
                            if j:
                                dve_done.link(dve, nc.vector.tensor_tensor(m, m, to, ALU.add))
            end_segment()

        def add_residual(dve, g, d, s, p):
            x = xT[:, d, s * S:s * S + S]
            return nc.vector.scalar_tensor_tensor(out=x, in0=p, scalar=mod[:, g + d, s:s + 1], in1=x, op0=ALU.mult, op1=ALU.add)

        def mixer_output(l, nt):
            with nc.Block() as block:
                @block.sync
                def _(sp):
                    load_segment(sp)

                @block.tensor
                def _(pe):
                    for d in range(KC):
                        arrived(pe, 0, d)
                        for k in range(KC):
                            mm = nc.tensor.matmul(psum[:, d, 0:nt], blocks[d][:, k, :], merged[:, k, 0:nt],
                                                  start=(k == 0), stop=(k == KC - 1))
                        mm.then_inc(used.sem, 1)
                    used.made += KC

                @block.vector
                def _(dve):
                    for d in range(KC):
                        dve.wait_ge(used.sem, used.at(d + 1))
                        for s in range(nt // S):
                            add_residual(dve, 16, d, s, psum[:, d, s * S:s * S + S])
            end_segment()

        def peer_scores(l, s):
            tok = slice(s * S, s * S + S)
            with nc.Block() as block:
                @block.sync
                def _(sp):
                    sp.dma_start(keys, A["keys"][l]).then_inc(stage_in.sem, 16)
                    stage_in.made += 16
                    load_segment(sp)

                @block.tensor
                def _(pe):
                    for n in range(16):
                        arrived(pe, n // RING, n % RING)
                        if n >= RING:
                            pe.wait_ge(act_done.sem, act_done.at(n - RING + 1))
                        for k in range(KC):
                            mm = nc.tensor.matmul(psum[:, n % 8, 0:S], blocks[n % RING][:, k, :], hT[:, k, tok],
                                                  start=(k == 0), stop=(k == KC - 1))
                        mm.then_inc(used.sem, 1)
                    used.made += 16
                    pe.wait_ge(stage_in.sem, stage_in.at(16))
                    pe.wait_ge(act_done.sem, act_done.at(16))
                    for tt in range(2):
                        for q in range(4):
                            for n in range(4 * q, 4 * q + 4):
                                mm = nc.tensor.matmul(psum[:, 4 * tt + q, (n % 4) * P:(n % 4) * P + P],
                                                      qry[:, n, tt * P:tt * P + P], keys[:, n, :], start=True, stop=True)
                            mm.then_inc(pe_done.sem, 1)
                    pe_done.made += 8

                @block.scalar
                def _(act):
                    for n in range(16):
                        act.wait_ge(used.sem, used.at(n + 1))
                        nc.scalar.copy(qry[:, n, :], psum[:, n % 8, 0:S]).then_inc(act_done.sem, 1)
                    for i in range(8):
                        act.wait_ge(pe_done.sem, pe_done.at(i + 1))
                        nc.scalar.copy(score[:, i // 4, 4 * (i % 4):4 * (i % 4) + 4, :],
                                       psum[:, i, :].rearrange("p (n k) -> p n k", n=4)).then_inc(act_done.sem, 1)
                    act_done.made += 24
            end_segment()

        def top16(dve, rows):
            group = 4
            for g in range(0, len(rows), group):
                lot = rows[g:g + group]
                start = dve_done.made
                for step in range(5):
                    for j, (val, big, place) in enumerate(lot):
                        if step:
                            dve.wait_ge(dve_done.sem, dve_done.at(start + (step - 1) * group + j + 1))
                        if step == 0:
                            ins = nc.vector.max(big[:, 0:8], val)
                        elif step == 1:
                            ins = nc.vector.max_index(place[:, 0:8], big[:, 0:8], val)
                        elif step == 2:
                            ins = nc.vector.match_replace(val, big[:, 0:8], val, NEG)
                        elif step == 3:
                            ins = nc.vector.max(big[:, 8:16], val)
                        else:
                            ins = nc.vector.max_index(place[:, 8:16], big[:, 8:16], val)
                        ins.then_inc(dve_done.sem, 1)
                dve_done.made += 5 * len(lot)
            dve.wait_ge(dve_done.sem, dve_done.at(dve_done.made))

        def peer_choice():
            with nc.Block() as block:
                @block.vector
                def _(dve):
                    top16(dve, [(score[:, tt, 2 * h + z, :], top_s[:, tt, h, z, :], top_iu[:, tt, h, z, :])
                                for tt in range(2) for h in range(PH) for z in range(2)])
                    dve_done.link(dve, nc.vector.tensor_copy(carve(11264, 512), top_i.bitcast(U32)))
                    full = [P, PH, PK, PK]
                    for tt in range(2):
                        dve_done.link(dve, nc.vector.tensor_tensor(
                            cand[:, tt].rearrange("p h (a b) -> p h a b", a=PK),
                            top_s[:, tt, :, 0, :].unsqueeze(3).to_broadcast(full),
                            top_s[:, tt, :, 1, :].unsqueeze(2).to_broadcast(full), ALU.add))
                    top16(dve, [(cand[:, tt, h, :], best_s[:, tt, h, :], best_ju[:, tt, h, :])
                                for tt in range(2) for h in range(PH)])
                    flat = best_j.bitcast(U32)
                    dve_done.link(dve, nc.vector.tensor_scalar(best_abu[:, 0, :], flat, 4, None, ALU.logical_shift_right))
                    dve_done.link(dve, nc.vector.tensor_scalar(best_abu[:, 1, :], flat, PK - 1, None, ALU.bitwise_and))
                    dve_done.link(dve, nc.vector.tensor_copy(carve(16896, 512), best_ab.bitcast(U32)))
                    for tt in range(2):
                        for z in range(2):
                            dve_done.link(dve, nc.vector.tensor_tensor(
                                hot, best_abf[:, z, tt].unsqueeze(3).to_broadcast(full),
                                iota[:, 0:PK].unsqueeze(1).unsqueeze(1).to_broadcast(full), ALU.is_equal))
                            dve_done.link(dve, nc.vector.tensor_tensor(
                                hot, hot, top_f[:, tt, :, z, :].unsqueeze(2).to_broadcast(full), ALU.mult))
                            dve_done.link(dve, nc.vector.tensor_reduce(
                                picked[:, z, tt, :].rearrange("p (h k) -> p h k", h=PH), hot, AX.X, ALU.add))
                    for tt in range(2):
                        g = picked[:, 2, tt, :].rearrange("p (h k) -> p h k", h=PH)
                        dve_done.link(dve, nc.vector.tensor_tensor(
                            g, best_s[:, tt], best_s[:, tt, :, 0:1].to_broadcast([P, PH, PK]), ALU.subtract))
                    made = dve_done.made
                    dve.wait_ge(act_done.sem, act_done.at(1))
                    dve_done.link(dve, nc.vector.tensor_reduce(
                        gsum[:, 0, :], picked[:, 2].rearrange("p t (h k) -> p (t h) k", h=PH), AX.X, ALU.add))
                    dve_done.link(dve, nc.vector.reciprocal(gsum[:, 1, :], gsum[:, 0, :]))
                    g = picked[:, 2].rearrange("p t (h k) -> p (t h) k", h=PH)
                    dve_done.link(dve, nc.vector.tensor_tensor(
                        g, g, gsum[:, 1, :].unsqueeze(2).to_broadcast([P, 2 * PH, PK]), ALU.mult))
                    peer_choice.exp_after = made

                @block.scalar
                def _(act):
                    act.wait_ge(dve_done.sem, dve_done.at(peer_choice.exp_after))
                    g = picked[:, 2]
                    act_done.link(act, nc.scalar.activation(g, g, ACT.Exp))
            end_stage()
            with nc.Block() as block:
                @block.tensor
                def _(pe):
                    for n in range(3):
                        for tt in range(2):
                            mm = nc.tensor.transpose(psum[:, n, tt * P:tt * P + P], picked[:, n, tt, :], ident[:])
                        mm.then_inc(pe_done.sem, 1)
                    pe_done.made += 3

                @block.vector
                def _(dve):
                    for n in range(3):
                        dve.wait_ge(pe_done.sem, pe_done.at(n + 1))
                        nc.vector.tensor_copy(sel_t[:, n, :], psum[:, n, 0:S])
            end_stage()

        def peer_gates():
            with nc.Block() as block:
                @block.vector
                def _(dve):
                    with dve.Fori(0, S // 4) as r:
                        for b in range(2):
                            dve.wait_ge(pe_done.sem, r * 2 + pe_done.at(b - 1))
                            for j in range(2):
                                t = r * 4 + (2 * b + j)
                                nc.vector.tensor_scalar(row_onehot[:, b, j, :], iota[:], sel_t[:, 0, bass.ds(t, 1)],
                                                        sel_t[:, 2, bass.ds(t, 1)], ALU.is_equal, ALU.mult).then_inc(dve_done.sem, 1)
                                nc.vector.tensor_scalar(col_onehot[:, b, j, :], iota[:], sel_t[:, 1, bass.ds(t, 1)], None,
                                                        ALU.is_equal).then_inc(dve_done.sem, 1)
                    dve_done.made += 2 * S

                @block.tensor
                def _(pe):
                    with pe.Fori(0, S // 4) as r:
                        for b in range(2):
                            if b == 0:
                                pe.wait_ge(tile_act.sem, r + tile_act.at(0))
                            pe.wait_ge(dve_done.sem, r * 8 + dve_done.at(4 * b + 4))
                            for j in range(2):
                                mm = nc.tensor.matmul(psum[:, b, j * P:j * P + P], col_onehot[:, b, j, :], row_onehot[:, b, j, :],
                                                      start=True, stop=True)
                            mm.then_inc(pe_done.sem, 1)
                    pe_done.made += S // 2

                @block.scalar
                def _(act):
                    with act.Fori(0, S // 4) as r:
                        act.wait_ge(pe_done.sem, r * 2 + pe_done.at(2))
                        nc.scalar.copy(gates[:, :, bass.ds(r * 4, 4)].rearrange("p i (b j) -> p i b j", b=2),
                                       psum[:, 0:2, 0:2 * P].rearrange("p b (j i) -> p i b j", i=P)).then_inc(tile_act.sem, 1)
                    tile_act.made += S // 4
            end_stage()

        def peer_experts(l, s):
            tok = slice(s * S, s * S + S)
            rounds = ET * 2 // RING

            def acc(d):
                return psum[:, 4 + d // 2, (d % 2) * S:(d % 2) * S + S]

            with nc.Block() as block:
                @block.sync
                def _(sp):
                    load_segment(sp)

                @block.tensor
                def _(pe):
                    def up(r, b, first=False):
                        slot = 0 if first else (2 * b - 1) % RING
                        before = r if b or first else r - 1
                        arrived(pe, before, slot)
                        pe.wait_ge(tile_act.sem, r * 4 + tile_act.at(b - 3))
                        for k in range(KC):
                            mm = nc.tensor.matmul(psum[:, b, 0:S], blocks[slot][:, k, :], hT[:, k, tok],
                                                  start=(k == 0), stop=(k == KC - 1))
                        mm.then_inc(used.sem, 1)

                    def down(r, b, first=False, last=False):
                        slot = (2 * b + 2) % RING if not last else RING - 1
                        after = r + (1 if b == 3 and not last else 0)
                        arrived(pe, after, slot)
                        pe.wait_ge(tile_dve.sem, r * 4 + tile_dve.at(b + 1))
                        for d in range(KC):
                            mm = nc.tensor.matmul(acc(d), ring[:, slot, d * P:d * P + P], wact[:, b % 2, :],
                                                  start=(first and d % 2 == 0), stop=last, skip_group_check=True)
                        mm.then_inc(used.sem, 1)

                    up(0, 0, first=True)
                    for b in range(1, 4):
                        up(0, b)
                        down(0, b - 1, first=(b == 1))
                    with pe.Fori(1, ET // 4) as r:
                        for b in range(4):
                            up(r, b)
                            if b:
                                down(r, b - 1)
                            else:
                                down(r - 1, 3)
                    down(ET // 4 - 1, 3, last=True)
                    used.made += 2 * ET

                @block.scalar
                def _(act):
                    def one(r, b, first=False):
                        act.wait_ge(used.sem, used.at(1) if first else r * 8 + used.at(2 * b))
                        act.wait_ge(tile_dve.sem, r * 4 + tile_dve.at(b - 1))
                        nc.scalar.activation(gelu[:, b % 2, :], psum[:, b, 0:S], ACT.Gelu).then_inc(tile_act.sem, 1)

                    for b in range(4):
                        one(0, b, first=(b == 0))
                    with act.Fori(1, ET // 4) as r:
                        for b in range(4):
                            one(r, b)
                    tile_act.made += ET

                @block.vector
                def _(dve):
                    def one(r, b, first=False):
                        dve.wait_ge(tile_act.sem, r * 4 + tile_act.at(b + 1))
                        if not first:
                            dve.wait_ge(used.sem, r * 8 + used.at(2 * b - 1))
                        nc.vector.tensor_tensor(wact[:, b % 2, :], gelu[:, b % 2, :], gates[:, r * 4 + b, :],
                                                ALU.mult).then_inc(tile_dve.sem, 1)

                    for b in range(4):
                        one(0, b, first=(b < 2))
                    with dve.Fori(1, ET // 4) as r:
                        for b in range(4):
                            one(r, b)
                    tile_dve.made += ET
                    dve.wait_ge(used.sem, used.at(2 * ET))
                    for d in range(KC):
                        add_residual(dve, 40, d, s, acc(d))
            end_segment()

        def final_norm():
            g0 = PARAMS["final"][0]
            with nc.Block() as block:
                @block.scalar
                def _(act):
                    for k in range(KC):
                        nc.scalar.activation(nsq[:, k, 0:S], xT[:, k, 0:S], ACT.Square).then_inc(act_done.sem, 1)
                    act.wait_ge(pe_done.sem, pe_done.at(1))
                    nc.scalar.activation(nrs[:, 0:S], psum[:, 0, 0:S], ACT.Sqrt, bias=eps_col[:],
                                         scale=1.0 / D).then_inc(act_done.sem, 1)
                    act_done.made += KC + 1

                @block.tensor
                def _(pe):
                    for k in range(KC):
                        pe.wait_ge(act_done.sem, act_done.at(k + 1))
                        mm = nc.tensor.matmul(psum[:, 0, 0:S], ones[:], nsq[:, k, 0:S], start=(k == 0), stop=(k == KC - 1))
                    mm.then_inc(pe_done.sem, 1)
                    pe_done.made += 1

                @block.vector
                def _(dve):
                    dve.wait_ge(act_done.sem, act_done.at(KC + 1))
                    dve_done.link(dve, nc.vector.reciprocal(nrs[:, 0:S], nrs[:, 0:S]))
                    for k in range(KC):
                        nc.vector.scalar_tensor_tensor(out=hT[:, k, 0:S], in0=xT[:, k, 0:S], scalar=par[:, 0, g0 + k:g0 + k + 1],
                                                       in1=nrs[:, 0:S], op0=ALU.mult, op1=ALU.mult).then_inc(dve_done.sem, 1)
                    dve_done.made += KC

                @block.sync
                def _(sp):
                    sp.wait_ge(dve_done.sem, dve_done.at(1 + KC))
                    sp.dma_start(out, hT[:, :, 0:S]).then_inc(out_done.sem, 16)
                    sp.wait_ge(out_done.sem, out_done.at(16))
                    out_done.made += 16
            end_stage()

        def dump(name, ap):
            if debug and name in debug:
                with nc.Block() as block:
                    @block.sync
                    def _(sp):
                        sp.dma_start(debug[name], ap).then_inc(out_done.sem, 16)
                        sp.wait_ge(out_done.sem, out_done.at(16))
                        out_done.made += 16
                end_stage()

        start()
        for l in range(DEPTH):
            nt = NT if l == 0 else S
            modulation(l)
            adaln(l, 0, NT)
            if l == 0:
                dump("h", hT[:])
            projection(l, nt)
            if l == 0:
                dump("proj", proj)
            conv_module(l, nt)
            gla_features(l)
            for z in range(2):
                gla_direction(l, z, nt)
            gla_output(l, nt)
            neighbourhood(l, nt)
            if l == 0:
                dump("conv", conv)
                dump("gla", o_t)
                dump("na", na_t)
            merge(l, nt)
            mixer_output(l, nt)
            if l == 0:
                dump("x1", xT[:])
            adaln(l, 1, nt)
            for s in range(nt // S):
                peer_scores(l, s)
                peer_choice()
                if l == 0 and s == 0:
                    dump("sel", sel_t[:])
                peer_gates()
                peer_experts(l, s)
            if l == 0:
                dump("x2", xT[:])
        final_norm()


def lay_out(i):
    f = {k: np.asarray(v) for k, v in i.items()}

    def chunks(v):
        return np.moveaxis(v.reshape(*v.shape[:-1], -1, P), -1, -2)

    def blocks_of(w):
        L, K, N = w.shape
        return w.reshape(L, K // P, P, N // P, P).transpose(0, 3, 2, 1, 4)

    a = {}
    x = np.concatenate([f["x"][0], f["ctx"][0]], 0)
    a["x"] = x.T.reshape(KC, P, NT).transpose(1, 0, 2)
    a["cond"] = np.stack([f["c"][0], f["c_ctx"]], -1).reshape(KC, P, 2).transpose(1, 0, 2)
    L = DEPTH
    cw = f["conv_w"].reshape(L, TAPS * CT, P)
    parts = [chunks(f["b_mod"]), chunks(f["norm1_g"]), chunks(f["norm2_g"]), chunks(f["b_gate"]), cw.transpose(0, 2, 1),
             chunks(f["conv_b"]), chunks(f["conv_ln_g"]), chunks(f["conv_ln_b"]), chunks(f["gla_ba"].reshape(L, -1)),
             chunks(f["gla_norm_g"]), np.broadcast_to(chunks(f["final_g"])[None], (L, P, KC))]
    a["params"] = np.concatenate(parts, -1).transpose(1, 0, 2)
    a["ident"] = np.eye(P, dtype=np.float32)
    a["iota"] = np.broadcast_to(np.arange(P, dtype=np.float32), (P, P))

    def flat(b):
        return b.reshape(b.shape[0], b.shape[1], P, D)

    a["w_mod"] = flat(blocks_of(f["w_mod"]))
    at = np.cumsum([0, 1024, 256, 256, 512, 512, 32, 512, 512, 512, 3072]).tolist()
    glu, q, k, v, g, wa, nq, nk, nv, br = (f["w_in"][:, :, at[n]:at[n + 1]] for n in range(10))
    a["w_proj"] = flat(blocks_of(np.concatenate([glu, g, nq, q, k, nk, v, nv], -1)))
    a["w_a"] = wa.reshape(L, KC, P, 32).transpose(0, 2, 1, 3)
    a["wa2"] = f["gla_wa2"].transpose(0, 2, 1, 3)
    gates = blocks_of(br).reshape(L, 3, KC, P, KC, P).transpose(0, 2, 1, 3, 4, 5)
    oc, og, on = (blocks_of(f[n])[:, :, None] for n in ("w_conv_o", "w_gla_o", "w_na_o"))
    pair = np.concatenate([oc, og], 4)
    alone = np.concatenate([on, np.zeros_like(on)], 4)
    a["w_merge"] = np.concatenate([gates, pair, alone], 2).reshape(L, 5 * KC, P, D)
    a["w_out"] = flat(blocks_of(f["w_out"]))
    a["w_query"] = flat(blocks_of(f["peer_wq"]))
    a["keys"] = f["peer_keys"].reshape(L, 2 * PH, NKEYS, P).transpose(0, 3, 1, 2)
    u = f["peer_u"].reshape(L, ET, P, KC, P).transpose(0, 1, 4, 3, 2).reshape(L, ET, P, D)
    v = f["peer_v"].reshape(L, ET, P, D)
    e = np.empty((L, 2 * ET, P, D), np.float32)
    e[:, 0], e[:, 2 * ET - 1] = u[:, 0], v[:, ET - 1]
    e[:, 1:2 * ET - 1:2], e[:, 2:2 * ET - 1:2] = u[:, 1:], v[:, :ET - 1]
    a["w_expert"] = e
    a["rpb"] = np.pad(f["na_rpb"][..., ::-1], ((0, 0), (0, 0), (0, 0), (GRID_W - KW, GRID_W - KW)))
    pos = np.arange(S)
    inv = np.float32(10000.0) ** (-np.arange(16, dtype=np.float32) / np.float32(16))
    ang = np.concatenate([(pos // GRID_W).astype(np.float32)[:, None] * inv, (pos % GRID_W).astype(np.float32)[:, None] * inv], -1)
    pair_of = (np.arange(P) % GDK) // 2
    a["rope"] = np.stack([np.cos(ang).T[pair_of], np.sin(ang).T[pair_of]], 1).astype(np.float32)
    swap = np.zeros((P, P), np.float32)
    swap[np.arange(1, P, 2), np.arange(0, P, 2)] = -1.0
    swap[np.arange(0, P, 2), np.arange(1, P, 2)] = 1.0
    a["swap"] = swap
    a["resets"] = np.broadcast_to((np.arange(NT) % CH != 0).astype(np.float32), (P, NT))
    cs = np.clip(np.arange(GRID_W) - KW // 2, 0, GRID_W - KW)
    ck = np.arange(GRID_W)
    ok = (ck[None] >= cs[:, None]) & (ck[None] < cs[:, None] + KW)
    a["na_mask"] = np.tile(np.where(ok, 0.0, -1e30).astype(np.float32)[:, ::-1], (2, 1))
    return {k: np.ascontiguousarray(v) for k, v in a.items()}


def kernel(**inputs):
    import concourse.bacc as _bacc
    from concourse.bass_utils import run_bass_kernel_spmd as _run

    arrays = lay_out(inputs)
    nc = _bacc.Bacc("TRN2", target_bir_lowering=False, num_devices=1)
    A = {n: nc.dram_tensor(f"in_{n}", a.shape, mybir.dt.from_np(a.dtype), kind="ExternalInput").ap() for n, a in arrays.items()}
    out = nc.dram_tensor("out", (P, KC, S), F32, kind="ExternalOutput").ap()
    build_program(nc, A, out)
    r = _run(nc, [{f"in_{n}": a for n, a in arrays.items()}], core_ids=[0])
    y = r.results[0]["out"]
    return np.ascontiguousarray(y.transpose(2, 1, 0).reshape(1, S, D))
```

```python
from contextlib import ExitStack

import numpy as np

import concourse.bass as bass
from concourse import mybir

F32 = mybir.dt.float32
F32R = mybir.dt.float32r
U32 = mybir.dt.uint32
ALU = mybir.AluOpType
ACT = mybir.ActivationFunctionType
AX = mybir.AxisListType

P = 128
D = 1024
KC = D // P
S = 256
NT = 2 * S
DEPTH = 2
EPS = 1e-6
GRID_W = 64
CONV, TAPS = 512, 31
HALO = TAPS // 2
CT = CONV // P
GH, GDK, GDV, GR = 4, 64, 128, 16
CH = 64
NCH = NT // CH
GATE_NORM = 16.0
NH, NHD = 8, 64
KH, KW = 8, 16
RPW = 2 * GRID_W - 1
PH, PK, NKEYS = 8, 16, 128
ET = NKEYS
RING = 8
SPLIT = 3
ONEHOTS = 4
NEG = -3.0e38

PARAMS = {}
_at = 0
for _name, _n in (("b_mod", 48), ("norm1", KC), ("norm2", KC), ("b_gate", 24), ("conv_w", TAPS * CT), ("conv_b", CT),
                  ("ln_g", CT), ("ln_b", CT), ("ba", 4), ("gla_g", GH), ("final", KC)):
    PARAMS[_name] = (_at, _at + _n)
    _at += _n
NPARAM = _at

T_GLU, T_G, T_NQ, T_Q, T_K, T_NK = 0, 8, 12, 16, 18, 20
CHANNEL_TILES = 24


class Count:

    def __init__(self, sem):
        self.sem, self.base, self.made = sem, 0, 0

    def at(self, n):
        return self.base + n

    def link(self, eng, ins):
        ins.then_inc(self.sem, 1)
        self.made += 1
        eng.wait_ge(self.sem, self.base + self.made)

    def close(self):
        self.base, self.made = self.base + self.made, 0


def build_program(nc, A, out, debug=None):
    ctx = ExitStack()
    with ctx:
        def sb(name, shape, dt=F32):
            return ctx.enter_context(nc.sbuf_tensor(name, shape, dt))

        counts = []

        def sem(name):
            return ctx.enter_context(nc.semaphore(name))

        def count(name):
            counts.append(Count(sem(name)))
            return counts[-1]

        xT = sb("xT", [P, KC, NT])
        h_at = (nc.sbuf_base + 31) // 32 * 32
        hT = sb("hT", [P, KC, NT])
        h_one = hT[:].rearrange("p k t -> p (k t)")[:, 0:KC * S].rearrange("p (k t) -> p k t", k=KC)
        h_lo = nc.alloc_sbuf_tensor_at("h_lo", [P, KC, S], F32R, offset=h_at)
        h_hi = nc.alloc_sbuf_tensor_at("h_hi", [P, KC, S], F32R, offset=h_at + 4 * KC * S)
        slab_at = (nc.sbuf_base + 31) // 32 * 32
        slab = sb("slab", [P, 3 * SPLIT * D])
        ring = slab[:, 0:RING * D].rearrange("p (b c) -> p b c", b=RING)
        blocks = [ring[:, b, :].rearrange("p (k c) -> p k c", k=KC) for b in range(RING)]
        raw = [slab[:, n * D:n * D + D] for n in range(SPLIT)]
        w_hi = [nc.alloc_sbuf_tensor_at(f"w_hi{n}", [P, D], F32R, offset=slab_at + 4 * D * (SPLIT + 2 * n)) for n in range(SPLIT)]
        w_lo = [nc.alloc_sbuf_tensor_at(f"w_lo{n}", [P, D], F32R, offset=slab_at + 4 * D * (SPLIT + 2 * n + 1)) for n in range(SPLIT)]
        sel_t = slab[:, SPLIT * D:SPLIT * D + 3 * S].rearrange("p (n t) -> p n t", n=3)
        onehot_at = SPLIT * D + 3 * S
        onehot = slab[:, onehot_at:onehot_at + ONEHOTS * 2 * 4 * P].rearrange("p (b z j i) -> p b z j i", b=ONEHOTS, z=2, j=4)
        par = sb("par", [P, DEPTH, NPARAM])
        mod = sb("mod", [P, 48, 2])
        scale1 = sb("scale1", [P, KC, 2])
        cond = sb("cond", [P, KC, 2])
        ident = sb("ident", [P, P])
        ones = sb("ones", [P, P])
        iota = sb("iota", [P, P])
        eps_col = sb("eps_col", [P, 1])
        act_hi = sb("act_hi", [P, SPLIT, S], F32R)
        act_lo = sb("act_lo", [P, SPLIT, S], F32R)
        arena = sb("arena", [P, ET * S])
        psum = ctx.enter_context(nc.psum_tensor("psum", [P, 8, 512], F32))

        def carve(at, n):
            return arena[:, at:at + n]

        proj = carve(0, CHANNEL_TILES * NT).rearrange("p (n t) -> p n t", n=CHANNEL_TILES)
        v_tok = carve(12288, 2048).rearrange("p (t c) -> p t c", t=4)
        nv_tok = carve(14336, 2048).rearrange("p (t c) -> p t c", t=4)
        conv = carve(16384, 2048).rearrange("p (n t) -> p n t", n=CT)
        o_t = carve(18432, 2048).rearrange("p (n t) -> p n t", n=GH)
        na_t = carve(20480, 2048).rearrange("p (n t) -> p n t", n=4)
        work = 22528
        upad = carve(work, CT * 2 * (S + 2 * HALO)).rearrange("p (n s t) -> p n s t", n=CT, s=2)
        sq = carve(work + 2304, 2048).rearrange("p (n t) -> p n t", n=CT)
        stat = carve(work + 4352, 1024).rearrange("p (n t) -> p n t", n=2)
        decay = carve(0, 2048).rearrange("p (n t) -> p n t", n=4)
        runsum = carve(2048, 2048).rearrange("p (n t) -> p n t", n=4)
        feat = carve(work, 4096).rearrange("p (f n t) -> p f n t", f=4, n=2)
        F_Q, F_K, F_QE, F_KE = range(4)
        ke_tok = carve(work + 4096, 1024).rearrange("p (t c) -> p t c", t=4)
        attm = carve(work + 5120, 1024).rearrange("p (t h i) -> p t h i", t=4, h=GH)
        state = carve(work + 6144, 512).rearrange("p (h e) -> p h e", h=GH)
        chunk_decay = carve(work + 6656, 16)
        a_t = carve(work + 6720, 1024).rearrange("p (z t) -> p z t", z=2)
        w_a = carve(work + 7744, 256).rearrange("p (k c) -> p k c", k=KC)
        wa2 = carve(work + 8000, 512).rearrange("p (z c) -> p z c", z=2)
        rope = carve(work + 8512, 512).rearrange("p (n t) -> p n t", n=2)
        swap = carve(work + 9024, 128)
        resets = carve(work + 9152, 512)
        na_bias = carve(work, 4096).rearrange("p (r h k) -> p r h k", r=2, h=NH)
        prob = carve(work + 4096, 1024).rearrange("p (b k) -> p b k", b=2)
        prob_t = carve(work + 5120, 1024).rearrange("p (b k q) -> p b k q", b=2, k=4)
        na_stat = carve(work + 6144, 32 * 3).rearrange("p (n u) -> p n u", n=3)
        na_mask = carve(work + 6272, 64)
        merged = carve(work, 4096).rearrange("p (n t) -> p n t", n=KC)
        gate_s = carve(work + 4096, 2048).rearrange("p (n t) -> p n t", n=4)
        branch_m = carve(work + 6144, 1024).rearrange("p (n t) -> p n t", n=2)
        nsq = carve(work, 4096).rearrange("p (n t) -> p n t", n=KC)
        nrs = carve(work + 4096, 512)
        mod_row = arena[0:2, work:work + 6 * D]
        gates = arena[:, :].rearrange("p (i t) -> p i t", i=ET)
        qry = carve(0, 4096).rearrange("p (n t) -> p n t", n=16)
        keys = carve(4096, 2048).rearrange("p (n k) -> p n k", n=16)
        score = carve(6144, 4096).rearrange("p (t n k) -> p t n k", t=2, n=16)
        top_s = carve(10240, 512).rearrange("p (t h z k) -> p t h z k", t=2, h=PH, z=2)
        top_i = carve(10752, 512)
        top_iu = top_i.bitcast(U32).rearrange("p (t h z k) -> p t h z k", t=2, h=PH, z=2)
        top_f = carve(11264, 512).rearrange("p (t h z k) -> p t h z k", t=2, h=PH, z=2)
        cand = carve(11776, 4096).rearrange("p (t h c) -> p t h c", t=2, h=PH)
        best_s = carve(15872, 256).rearrange("p (t h k) -> p t h k", t=2, h=PH)
        best_j = carve(16128, 256)
        best_ju = best_j.bitcast(U32).rearrange("p (t h k) -> p t h k", t=2, h=PH)
        best_ab = carve(16384, 512)
        best_abu = best_ab.bitcast(U32).rearrange("p (z u) -> p z u", z=2)
        best_abf = carve(16896, 512).rearrange("p (z t h k) -> p z t h k", z=2, t=2, h=PH)
        hot = carve(17408, 2048).rearrange("p (h k c) -> p h k c", h=PH, k=PK)
        picked = carve(19456, 768).rearrange("p (n t u) -> p n t u", n=3, t=2)
        gsum = carve(20224, 32).rearrange("p (n u) -> p n u", n=2)

        landed = [sem(f"block_landed_{b}") for b in range(RING)]
        used = count("block_used")
        expert_used = count("expert_block_used")
        par_in = count("param_landed")
        stage_in = count("stage_input_landed")
        pe_done = count("pe_group_done")
        act_done = count("act_step_done")
        dve_done = count("dve_step_done")
        pool_done = count("pool_step_done")
        out_done = count("output_written")
        raw_landed = [sem(f"raw_block_landed_{n}") for n in range(SPLIT)]
        hi_made = count("block_hi_made")
        lo_made = count("block_lo_made")
        gelu_made = count("gelu_made")
        gated_made = count("gated_made")
        act_hi_made = count("gated_hi_made")
        act_lo_made = count("gated_lo_made")
        onehots_made = count("onehots_made")
        gates_made = count("gates_in_psum")
        gates_out = count("gates_evacuated")
        tile_act = count("tile_evacuated_by_act")
        tile_dve = count("tile_evacuated_by_dve")

        def end_stage():
            for c in counts:
                c.close()

        segments = []
        for l in range(DEPTH):
            segments += [(A["w_mod"], l, 6, False), (A["w_proj"], l, 4, True), (A["w_merge"], l, 5, True), (A["w_out"], l, 1, True)]
            for s in range(2 if l == 0 else 1):
                segments += [(A["w_query"], l, 2, s == 0)]
        run_loads = [0] * SPLIT
        at_segment = [0]
        rounds_before = [0]

        def load_round(sp, seg, r, before, fresh=False):
            src, l = segments[seg][0:2]
            for b in range(RING):
                if not fresh:
                    sp.wait_ge(used.sem, (before + r - 1) * RING + b + 1)
                sp.dma_start(ring[:, b, :], src[l, r * RING + b]).then_inc(landed[b], 16)

        def load_segment(sp):
            seg, before = at_segment[0], rounds_before[0]
            n = segments[seg][2]
            if not segments[seg][3]:
                load_round(sp, seg, 0, before, fresh=True)
            if n > 2:
                with sp.Fori(1, n) as r:
                    load_round(sp, seg, r, before)
            elif n == 2:
                load_round(sp, seg, 1, before)
            if seg + 1 < len(segments) and segments[seg + 1][3]:
                load_round(sp, seg + 1, 0, before + n)

        def end_segment():
            rounds_before[0] += segments[at_segment[0]][2]
            at_segment[0] += 1
            end_stage()

        def arrived(pe, r, b):
            pe.wait_ge(landed[b], (r + rounds_before[0] + 1) * 16)

        def col(l, name, i):
            a = PARAMS[name][0] + i
            return par[:, l, a:a + 1]

        def start():
            block = nc.Block()
            with block as block:
                @block.sync
                def _(sp):
                    sp.dma_start(xT[:], A["x"]).then_inc(par_in.sem, 16)
                    sp.dma_start(par[:], A["params"]).then_inc(par_in.sem, 16)
                    sp.dma_start(cond[:], A["cond"]).then_inc(par_in.sem, 16)
                    sp.dma_start(ident[:], A["ident"]).then_inc(par_in.sem, 16)
                    sp.dma_start(iota[:], A["iota"]).then_inc(par_in.sem, 16)

                @block.vector
                def _(dve):
                    nc.vector.memset(ones[:], 1.0)
                    nc.vector.memset(eps_col[:], EPS)
                    dve.sem_inc(tile_dve.sem, 8)

                @block.scalar
                def _(act):
                    act.wait_ge(par_in.sem, 80)
                    nc.scalar.activation(cond[:], cond[:], ACT.Silu)
                    act.sem_inc(tile_act.sem, 8)
            par_in.made = 80
            tile_dve.made = 8
            tile_act.made = 8
            end_stage()

        def modulation(l):
            with nc.Block() as block:
                @block.sync
                def _(sp):
                    load_segment(sp)

                @block.tensor
                def _(pe):
                    with pe.Fori(0, 6) as c:
                        pe.wait_ge(tile_act.sem, c * 2 + tile_act.at(0))
                        for k in range(KC):
                            arrived(pe, c, k)
                            for n in range(2):
                                mm = nc.tensor.matmul(psum[0:2, n, :], cond[:, k, :], ring[:, k, n * 512:n * 512 + 512],
                                                      start=(k == 0), stop=(k == KC - 1))
                            mm.then_inc(used.sem, 1)
                    used.made += 48
                    pe.wait_ge(tile_act.sem, tile_act.at(12))
                    for n in range(48):
                        mm = nc.tensor.transpose(psum[:, 2, 2 * n:2 * n + 2], mod_row[:, n * P:n * P + P], ident[0:2, 0:2])
                    mm.then_inc(pe_done.sem, 1)
                    pe_done.made += 1

                @block.scalar
                def _(act):
                    with act.Fori(0, 6) as c:
                        act.wait_ge(used.sem, c * 8 + used.at(8))
                        for n in range(2):
                            nc.scalar.copy(mod_row[:, bass.ds(c * D + n * 512, 512)], psum[0:2, n, :]).then_inc(tile_act.sem, 1)
                    tile_act.made += 12

                @block.vector
                def _(dve):
                    dve.wait_ge(pe_done.sem, pe_done.at(1))
                    a, b = PARAMS["b_mod"]
                    m = psum[:, 2, 0:96].rearrange("p (n s) -> p n s", s=2)
                    for s in range(2):
                        dve_done.link(dve, nc.vector.tensor_tensor(mod[:, :, s], m[:, :, s], par[:, l, a:b], ALU.add))
            end_segment()

        def adaln(l, which, streams, to):
            ns = len(streams)
            nt = ns * S
            cols = slice(streams[0] * S, streams[0] * S + nt)
            sh, sc = (0, 8) if which == 0 else (24, 32)
            g0, g1 = PARAMS["norm1" if which == 0 else "norm2"]
            with nc.Block() as block:
                @block.scalar
                def _(act):
                    for k in range(KC):
                        nc.scalar.activation(nsq[:, k, 0:nt], xT[:, k, cols], ACT.Square).then_inc(act_done.sem, 1)
                    act.wait_ge(pe_done.sem, pe_done.at(1))
                    nc.scalar.activation(nrs[:, 0:nt], psum[:, 0, 0:nt], ACT.Sqrt, bias=eps_col[:],
                                         scale=1.0 / D).then_inc(act_done.sem, 1)
                    for k in range(KC):
                        for j, s in enumerate(streams):
                            act.wait_ge(dve_done.sem, dve_done.at(3 + k * ns + j + 1))
                            nc.scalar.activation(to[:, k, j * S:j * S + S], to[:, k, j * S:j * S + S], ACT.Identity,
                                                 bias=mod[:, sh + k, s:s + 1]).then_inc(act_done.sem, 1)
                    act_done.made += KC + 1 + KC * ns

                @block.tensor
                def _(pe):
                    for k in range(KC):
                        pe.wait_ge(act_done.sem, act_done.at(k + 1))
                        mm = nc.tensor.matmul(psum[:, 0, 0:nt], ones[:], nsq[:, k, 0:nt], start=(k == 0), stop=(k == KC - 1))
                    mm.then_inc(pe_done.sem, 1)
                    pe_done.made += 1

                @block.vector
                def _(dve):
                    for s in range(2):
                        dve_done.link(dve, nc.vector.scalar_tensor_tensor(
                            out=scale1[:, :, s], in0=mod[:, sc:sc + KC, s], scalar=1.0, in1=par[:, l, g0:g1],
                            op0=ALU.add, op1=ALU.mult))
                    dve.wait_ge(act_done.sem, act_done.at(KC + 1))
                    dve_done.link(dve, nc.vector.reciprocal(nrs[:, 0:nt], nrs[:, 0:nt]))
                    for k in range(KC):
                        for j, s in enumerate(streams):
                            t = slice(j * S, j * S + S)
                            nc.vector.scalar_tensor_tensor(
                                out=to[:, k, t], in0=xT[:, k, s * S:s * S + S], scalar=scale1[:, k, s:s + 1], in1=nrs[:, t],
                                op0=ALU.mult, op1=ALU.mult).then_inc(dve_done.sem, 1)
                    dve_done.made += KC * ns
            end_stage()

        def projection(l, nt):
            with nc.Block() as block:
                @block.sync
                def _(sp):
                    load_segment(sp)

                @block.tensor
                def _(pe):
                    def tile(r, b, width):
                        arrived(pe, r, b)
                        back = tile_act if b % 2 == 0 else tile_dve
                        pe.wait_ge(back.sem, r * 4 + back.at(b // 2 - 3))
                        for k in range(KC):
                            mm = nc.tensor.matmul(psum[:, b, 0:width], blocks[b][:, k, :], hT[:, k, 0:width],
                                                  start=(k == 0), stop=(k == KC - 1))
                        mm.then_inc(used.sem, 1)

                    with pe.Fori(0, 2) as r:
                        for b in range(RING):
                            tile(r, b, nt)
                    for b in range(RING):
                        tile(2, b, nt if b < 2 else NT)
                    for b in range(RING):
                        arrived(pe, 3, b)
                        back = tile_act if b % 2 == 0 else tile_dve
                        pe.wait_ge(back.sem, back.at(12 + b // 2 - 3))
                        for tt in range(4):
                            for k in range(KC):
                                mm = nc.tensor.matmul(psum[:, b, tt * P:tt * P + P], hT[:, k, tt * P:tt * P + P],
                                                      blocks[b][:, k, :], start=(k == 0), stop=(k == KC - 1))
                        mm.then_inc(used.sem, 1)
                    used.made += 32

                def evacuate(eng, copy, parity, back):
                    def one(r, b, width):
                        eng.wait_ge(used.sem, r * RING + used.at(b + 1))
                        copy(proj[:, r * RING + b, 0:width], psum[:, b, 0:width]).then_inc(back.sem, 1)

                    with eng.Fori(0, 2) as r:
                        for b in range(parity, RING, 2):
                            one(r, b, nt)
                    for b in range(parity, RING, 2):
                        one(2, b, nt if b < 2 else NT)
                    for b in range(parity, RING, 2):
                        eng.wait_ge(used.sem, used.at(24 + b + 1))
                        to = (v_tok if b < 4 else nv_tok)[:, :, (b % 4) * P:(b % 4) * P + P]
                        copy(to, psum[:, b, :].rearrange("p (t c) -> p t c", t=4)).then_inc(back.sem, 1)
                    back.made += 16

                @block.scalar
                def _(act):
                    evacuate(act, nc.scalar.copy, 0, tile_act)

                @block.vector
                def _(dve):
                    evacuate(dve, nc.vector.tensor_copy, 1, tile_dve)
            end_segment()

        def conv_module(l, nt):
            ns = nt // S
            acc = [conv[:, c, 0:nt].rearrange("p (s t) -> p s t", s=ns) for c in range(CT)]
            glu = proj[:, T_GLU:T_GLU + 4, 0:nt]
            gate = proj[:, T_GLU + 4:T_GLU + 8, 0:nt]
            w0 = PARAMS["conv_w"][0]
            cw = par[:, l, w0:w0 + TAPS * CT].rearrange("p (w c) -> p w c", c=CT)
            with nc.Block() as block:
                @block.scalar
                def _(act):
                    act_done.link(act, nc.scalar.activation(gate, gate, ACT.Sigmoid))
                    for c in range(CT):
                        act.wait_ge(dve_done.sem, dve_done.at(5 + CT * TAPS + 1 + c + 1))
                        nc.scalar.activation(sq[:, c, 0:nt], conv[:, c, 0:nt], ACT.Square).then_inc(act_done.sem, 1)
                    act.wait_ge(pe_done.sem, pe_done.at(2))
                    nc.scalar.activation(stat[:, 1, 0:nt], psum[:, 1, 0:nt], ACT.Sqrt, bias=eps_col[:],
                                         scale=1.0 / CONV).then_inc(act_done.sem, 1)
                    for c in range(CT):
                        act.wait_ge(dve_done.sem, dve_done.at(5 + CT * TAPS + 1 + CT + 1 + c + 1))
                        nc.scalar.activation(conv[:, c, 0:nt], conv[:, c, 0:nt], ACT.Silu,
                                             bias=col(l, "ln_b", c)).then_inc(act_done.sem, 1)
                    act_done.made += CT + 1 + CT

                @block.tensor
                def _(pe):
                    pe.wait_ge(dve_done.sem, dve_done.at(5 + CT * TAPS))
                    for c in range(CT):
                        mm = nc.tensor.matmul(psum[:, 0, 0:nt], ones[:], conv[:, c, 0:nt], start=(c == 0), stop=(c == CT - 1))
                    mm.then_inc(pe_done.sem, 1)
                    for c in range(CT):
                        pe.wait_ge(act_done.sem, act_done.at(1 + c + 1))
                        mm = nc.tensor.matmul(psum[:, 1, 0:nt], ones[:], sq[:, c, 0:nt], start=(c == 0), stop=(c == CT - 1))
                    mm.then_inc(pe_done.sem, 1)
                    pe_done.made += 2

                @block.vector
                def _(dve):
                    nc.vector.memset(upad, 0.0).then_inc(dve_done.sem, 1)
                    dve.wait_ge(dve_done.sem, dve_done.at(1))
                    dve.wait_ge(act_done.sem, act_done.at(1))
                    for c in range(CT):
                        nc.vector.tensor_tensor(
                            upad[:, c, 0:ns, HALO:HALO + S], glu[:, c, :].rearrange("p (s t) -> p s t", s=ns),
                            gate[:, c, :].rearrange("p (s t) -> p s t", s=ns), ALU.mult).then_inc(dve_done.sem, 1)
                    for c in range(CT):
                        dve.wait_ge(dve_done.sem, dve_done.at(1 + c + 1))
                        nc.vector.tensor_scalar(acc[c], upad[:, c, 0:ns, 0:S], cw[:, 0, c:c + 1], col(l, "conv_b", c),
                                                ALU.mult, ALU.add).then_inc(dve_done.sem, 1)
                    with dve.Fori(1, TAPS) as w:
                        for c in range(CT):
                            dve.wait_ge(dve_done.sem, w * CT + dve_done.at(5 + c + 1 - CT))
                            nc.vector.scalar_tensor_tensor(
                                out=acc[c], in0=upad[:, c, 0:ns, bass.ds(w, S)], scalar=cw[:, w, c:c + 1], in1=acc[c],
                                op0=ALU.mult, op1=ALU.add).then_inc(dve_done.sem, 1)
                    n = 5 + CT * TAPS
                    dve.wait_ge(pe_done.sem, pe_done.at(1))
                    nc.vector.tensor_scalar(stat[:, 0, 0:nt], psum[:, 0, 0:nt], 1.0 / CONV, None,
                                            ALU.mult).then_inc(dve_done.sem, 1)
                    dve.wait_ge(dve_done.sem, dve_done.at(n + 1))
                    for c in range(CT):
                        nc.vector.tensor_tensor(conv[:, c, 0:nt], conv[:, c, 0:nt], stat[:, 0, 0:nt],
                                                ALU.subtract).then_inc(dve_done.sem, 1)
                    dve.wait_ge(act_done.sem, act_done.at(1 + CT + 1))
                    nc.vector.reciprocal(stat[:, 1, 0:nt], stat[:, 1, 0:nt]).then_inc(dve_done.sem, 1)
                    dve.wait_ge(dve_done.sem, dve_done.at(n + 1 + CT + 1))
                    for c in range(CT):
                        nc.vector.scalar_tensor_tensor(
                            out=conv[:, c, 0:nt], in0=conv[:, c, 0:nt], scalar=col(l, "ln_g", c), in1=stat[:, 1, 0:nt],
                            op0=ALU.mult, op1=ALU.mult).then_inc(dve_done.sem, 1)
                    dve_done.made += n + 1 + CT + 1 + CT
            end_stage()

        def gla_features(l):
            with nc.Block() as block:
                @block.sync
                def _(sp):
                    for to, src in ((w_a, A["w_a"][l]), (wa2[0:GR], A["wa2"][l]), (rope, A["rope"]), (swap, A["swap"]),
                                    (resets, A["resets"])):
                        sp.dma_start(to, src).then_inc(stage_in.sem, 16)
                    stage_in.made += 80

                @block.tensor
                def _(pe):
                    pe.wait_ge(stage_in.sem, stage_in.at(80))
                    for z in range(2):
                        for k in range(KC):
                            mm = nc.tensor.matmul(psum[0:GR, z, :], w_a[:, k, z * GR:z * GR + GR], hT[:, k, :],
                                                  start=(k == 0), stop=(k == KC - 1))
                        mm.then_inc(pe_done.sem, 1)
                    for i in range(4):
                        nc.tensor.matmul(psum[:, 6 + i // 2, (i % 2) * S:(i % 2) * S + S], swap, proj[:, T_Q + i, 0:S],
                                         start=True, stop=True).then_inc(pe_done.sem, 1)
                    for z in range(2):
                        pe.wait_ge(act_done.sem, act_done.at(z + 1))
                        for n in range(2):
                            mm = nc.tensor.matmul(psum[:, 2 + 2 * z + n, :], wa2[0:GR, z, n * P:n * P + P], a_t[0:GR, z, :],
                                                  start=True, stop=True)
                        mm.then_inc(pe_done.sem, 1)
                    pe_done.made += 8

                @block.scalar
                def _(act):
                    for z in range(2):
                        act.wait_ge(pe_done.sem, pe_done.at(z + 1))
                        nc.scalar.copy(a_t[0:GR, z, :], psum[0:GR, z, :]).then_inc(act_done.sem, 1)
                    act.wait_ge(pe_done.sem, pe_done.at(8))
                    for i in range(4):
                        nc.scalar.activation(decay[:, i, :], psum[:, 2 + i, :], ACT.Identity,
                                             bias=col(l, "ba", i)).then_inc(act_done.sem, 1)
                    act.wait_ge(dve_done.sem, dve_done.at(12 + 1))
                    nc.scalar.activation(runsum, runsum, ACT.Exp, scale=-1.0).then_inc(act_done.sem, 1)
                    act.wait_ge(act_done.sem, act_done.at(7))
                    nc.scalar.activation(runsum, runsum, ACT.Ln, bias=1.0).then_inc(act_done.sem, 1)
                    act_done.made += 8

                @block.vector
                def _(dve):
                    dve.wait_ge(pe_done.sem, pe_done.at(6))
                    dve.wait_ge(stage_in.sem, stage_in.at(80))
                    for i in range(4):
                        x = proj[:, T_Q + i, 0:S]
                        tmp = feat[:, 0, 0, 0:S]
                        dve_done.link(dve, nc.vector.tensor_tensor(tmp, psum[:, 6 + i // 2, (i % 2) * S:(i % 2) * S + S],
                                                                   rope[:, 1, :], ALU.mult))
                        dve_done.link(dve, nc.vector.tensor_tensor(x, x, rope[:, 0, :], ALU.mult))
                        dve_done.link(dve, nc.vector.tensor_tensor(x, x, tmp, ALU.add))
                    dve.wait_ge(act_done.sem, act_done.at(6))
                    dve_done.link(dve, nc.vector.scalar_tensor_tensor(out=runsum, in0=decay, scalar=-1.0, in1=decay,
                                                                      op0=ALU.mult, op1=ALU.max))
                    dve.wait_ge(act_done.sem, act_done.at(8))
                    dve_done.link(dve, nc.vector.scalar_tensor_tensor(out=decay, in0=decay, scalar=0.0, in1=runsum,
                                                                      op0=ALU.min, op1=ALU.subtract))
                    for i in range(4):
                        step = 1 if i < 2 else -1
                        dve_done.link(dve, nc.vector.tensor_tensor_scan(
                            runsum[:, i, ::step], resets, decay[:, i, ::step], 0.0, ALU.mult, ALU.add))
            end_stage()

        def gla_direction(l, z, nt):
            mid, end = (CH // 2, CH - 1) if z == 0 else (CH // 2 - 1, 0)
            b = runsum[:, 2 * z:2 * z + 2, :]
            bc = b.rearrange("p n (c i) -> p (n c) i", i=CH)
            fq, fk, fqe, fke = (feat[:, f, :, :] for f in (F_Q, F_K, F_QE, F_KE))

            def chunks(x):
                return x.rearrange("p n (c i) -> p (n c) i", i=CH)
            with nc.Block() as block:
                @block.vector
                def _(dve):
                    n = [P, 2 * NCH, CH]
                    dve_done.link(dve, nc.vector.tensor_tensor(chunks(fq), bc, bc[:, :, mid:mid + 1].to_broadcast(n),
                                                               ALU.subtract))
                    dve_done.link(dve, nc.vector.tensor_tensor(chunks(fke), bc[:, :, end:end + 1].to_broadcast(n), bc,
                                                               ALU.subtract))
                    k = proj[:, T_K:T_K + 2, :]
                    q = proj[:, T_Q:T_Q + 2, 0:nt]
                    dve.wait_ge(act_done.sem, act_done.at(1))
                    nc.vector.tensor_tensor(fk, fk, k, ALU.mult).then_inc(dve_done.sem, 1)
                    dve.wait_ge(act_done.sem, act_done.at(2))
                    nc.vector.tensor_tensor(fke, fke, k, ALU.mult).then_inc(dve_done.sem, 1)
                    for j, f in ((3, fq), (4, fqe)):
                        dve.wait_ge(act_done.sem, act_done.at(j))
                        nc.vector.scalar_tensor_tensor(out=f[:, :, 0:nt], in0=q, scalar=GDK ** -0.5, in1=f[:, :, 0:nt],
                                                       op0=ALU.mult, op1=ALU.mult).then_inc(dve_done.sem, 1)
                    nc.vector.memset(state, 0.0).then_inc(dve_done.sem, 1)
                    for n in range(2):
                        dve.wait_ge(pe_done.sem, pe_done.at(n + 1))
                        nc.vector.tensor_copy(ke_tok[:, :, n * P:n * P + P],
                                              psum[:, 2 + n, :].rearrange("p (t c) -> p t c", t=4)).then_inc(dve_done.sem, 1)
                    dve_done.made += 7

                @block.scalar
                def _(act):
                    s = 1.0 / GATE_NORM
                    act.wait_ge(dve_done.sem, dve_done.at(2))
                    nc.scalar.activation(fk, fq, ACT.Exp, scale=-s).then_inc(act_done.sem, 1)
                    nc.scalar.activation(fke, fke, ACT.Exp, scale=s).then_inc(act_done.sem, 1)
                    act.wait_ge(act_done.sem, act_done.at(1))
                    nc.scalar.activation(fq, fq, ACT.Exp, scale=s).then_inc(act_done.sem, 1)
                    nc.scalar.activation(fqe, b, ACT.Exp, scale=s).then_inc(act_done.sem, 1)
                    nc.scalar.activation(chunk_decay, bc[:, :, end], ACT.Exp, scale=s).then_inc(act_done.sem, 1)
                    for i in range(2):
                        act.wait_ge(pe_done.sem, pe_done.at(3 + i))
                        w = nt // P
                        nc.scalar.copy(attm[:, 0:w, i::2, :],
                                       psum[:, i, :].rearrange("p (t h i) -> p t h i", t=4, h=2)[:, 0:w]).then_inc(act_done.sem, 1)
                    act_done.made += 7

                @block.gpsimd
                def _(pool):
                    pool.wait_ge(act_done.sem, act_done.at(7))
                    w = nt // P
                    for half in range(2):
                        m = attm[half * CH:half * CH + CH, 0:w, :, :].rearrange("p t h i -> p (t h) i")
                        sign = 1 if z == 0 else -1
                        nc.gpsimd.affine_select(out=m, in_=m, compare_op=ALU.is_ge, fill=0.0, base=0,
                                                pattern=[[0, w * GH], [sign, CH]], channel_multiplier=-sign).then_inc(pool_done.sem, 1)
                    pool_done.made += 2

                @block.tensor
                def _(pe):
                    pe.wait_ge(dve_done.sem, dve_done.at(4))
                    for n in range(2):
                        for tt in range(4):
                            mm = nc.tensor.transpose(psum[:, 2 + n, tt * P:tt * P + P], fke[:, n, tt * P:tt * P + P], ident[:])
                        mm.then_inc(pe_done.sem, 1)
                    pe.wait_ge(dve_done.sem, dve_done.at(6))
                    for i in range(2):
                        for c in range(nt // CH):
                            for n in range(2):
                                rows = slice(i * GDK, i * GDK + GDK)
                                at = ((c // 2) * 2 + n) * CH
                                mm = nc.tensor.matmul(psum[(c % 2) * CH:(c % 2) * CH + CH, i, at:at + CH],
                                                      fk[rows, n, c * CH:c * CH + CH], fq[rows, n, c * CH:c * CH + CH],
                                                      start=True, stop=True)
                        mm.then_inc(pe_done.sem, 1)
                    pe_done.made += 4
            end_stage()

            order = [4, 5, 6, 7, 0, 1, 2, 3] if z == 0 else [7, 6, 5, 4, 3, 2, 1, 0]
            shown = [c < nt // CH for c in order]
            before = [sum(4 + shown[j] for j in range(n)) for n in range(NCH + 1)]
            with nc.Block() as block:
                @block.tensor
                def _(pe):
                    for n, c in enumerate(order):
                        tt, half = c // 2, slice((c % 2) * CH, (c % 2) * CH + CH)
                        for h in range(GH):
                            rows = slice((h % 2) * GDK, (h % 2) * GDK + GDK)
                            if n >= 2:
                                pe.wait_ge(dve_done.sem, dve_done.at(before[n - 1]))
                            mm = nc.tensor.matmul(psum[rows, 2 + n % 2, (h // 2) * P:(h // 2) * P + P],
                                                  ke_tok[half, tt, h * GDK:h * GDK + GDK], v_tok[half, tt, h * P:h * P + P],
                                                  start=True, stop=True)
                        mm.then_inc(pe_done.sem, 1)
                        if n > 0:
                            pe.wait_ge(dve_done.sem, dve_done.at(before[n]))
                        if shown[n]:
                            for h in range(GH):
                                o = psum[:, n % 2, h * CH:h * CH + CH]
                                nc.tensor.matmul(o, state[:, h, :], fqe[:, h // 2, c * CH:c * CH + CH], start=True, stop=False)
                                mm = nc.tensor.matmul(o, v_tok[half, tt, h * P:h * P + P], attm[half, tt, h, :],
                                                      start=False, stop=True)
                            mm.then_inc(pe_done.sem, 1)
                    pe_done.made += NCH + sum(shown)

                @block.vector
                def _(dve):
                    got = 0
                    for n, c in enumerate(order):
                        got += 1 + shown[n]
                        dve.wait_ge(pe_done.sem, pe_done.at(got))
                        if shown[n]:
                            o = o_t[:, :, c * CH:c * CH + CH]
                            p = psum[:, n % 2, 0:GH * CH].rearrange("p (h i) -> p h i", h=GH)
                            if z == 0:
                                nc.vector.tensor_copy(o, p).then_inc(dve_done.sem, 1)
                            else:
                                nc.vector.tensor_tensor(o, o, p, ALU.add).then_inc(dve_done.sem, 1)
                        for h in range(GH):
                            rows = slice((h % 2) * GDK, (h % 2) * GDK + GDK)
                            if n > 0:
                                dve.wait_ge(dve_done.sem, dve_done.at(before[n]))
                            nc.vector.scalar_tensor_tensor(
                                out=state[rows, h, :], in0=state[rows, h, :],
                                scalar=chunk_decay[rows, (h // 2) * NCH + c:(h // 2) * NCH + c + 1],
                                in1=psum[rows, 2 + n % 2, (h // 2) * P:(h // 2) * P + P],
                                op0=ALU.mult, op1=ALU.add).then_inc(dve_done.sem, 1)
                    dve_done.made += before[NCH]
            end_stage()

        def gla_output(l, nt):
            g = proj[:, T_G:T_G + GH, 0:nt]
            o = o_t[:, :, 0:nt]
            osq = feat.rearrange("p f n t -> p (f n) t")[:, 0:4, 0:nt]
            ors = feat.rearrange("p f n t -> p (f n) t")[:, 4:8, 0:nt]
            with nc.Block() as block:
                @block.scalar
                def _(act):
                    nc.scalar.activation(osq, o, ACT.Square).then_inc(act_done.sem, 1)
                    nc.scalar.activation(g, g, ACT.Silu).then_inc(act_done.sem, 1)
                    act.wait_ge(pe_done.sem, pe_done.at(1))
                    nc.scalar.activation(ors, psum[:, 0:4, 0:nt], ACT.Sqrt, bias=eps_col[:],
                                         scale=1.0 / GDV).then_inc(act_done.sem, 1)
                    act_done.made += 3

                @block.tensor
                def _(pe):
                    pe.wait_ge(act_done.sem, act_done.at(1))
                    for h in range(GH):
                        mm = nc.tensor.matmul(psum[:, h, 0:nt], ones[:], osq[:, h, :], start=True, stop=True)
                    mm.then_inc(pe_done.sem, 1)
                    pe_done.made += 1

                @block.vector
                def _(dve):
                    dve.wait_ge(act_done.sem, act_done.at(3))
                    dve_done.link(dve, nc.vector.reciprocal(ors, ors))
                    dve_done.link(dve, nc.vector.tensor_tensor(ors, ors, g, ALU.mult))
                    for h in range(GH):
                        nc.vector.scalar_tensor_tensor(out=o[:, h, :], in0=o[:, h, :], scalar=col(l, "gla_g", h),
                                                       in1=ors[:, h, :], op0=ALU.mult, op1=ALU.mult).then_inc(dve_done.sem, 1)
                    dve_done.made += GH
            end_stage()

        def neighbourhood(l, nt):
            units = [(qt, h) for qt in range(nt // P) for h in range(NH)]
            rows_of = [slice((h % 2) * NHD, (h % 2) * NHD + NHD) for h in range(NH)]
            with nc.Block() as block:
                @block.sync
                def _(sp):
                    for row in range(4):
                        half = slice((row % 2) * GRID_W, (row % 2) * GRID_W + GRID_W)
                        for h in range(NH):
                            at = ((l * NH + h) * (2 * KH - 1) + KH - 1 - row) * RPW
                            rpb = bass.AP(tensor=A["rpb"].tensor, offset=at, ap=[[1, GRID_W], [RPW, 4], [1, GRID_W]])
                            to = na_bias[half, row // 2, h].rearrange("p (r c) -> p r c", c=GRID_W)
                            sp.dma_start(to, rpb).then_inc(stage_in.sem, 16)
                    sp.dma_start(na_mask, A["na_mask"]).then_inc(stage_in.sem, 16)
                    stage_in.made += 16 * (4 * NH + 1)

                def keys_of(qt):
                    return 0 if qt < 2 else S

                @block.tensor
                def _(pe):
                    def scores(u):
                        qt, h = units[u]
                        if u >= 2:
                            pe.wait_ge(dve_done.sem, dve_done.at(1 + 6 * (u - 2) + 2))
                        k0 = keys_of(qt)
                        nc.tensor.matmul(psum[:, u % 2, k0:NT], proj[rows_of[h], T_NQ + h // 2, qt * P:qt * P + P],
                                         proj[rows_of[h], T_NK + h // 2, k0:NT], start=True, stop=True).then_inc(pe_done.sem, 1)

                    def transposes(u):
                        qt, h = units[u]
                        pe.wait_ge(dve_done.sem, dve_done.at(1 + 6 * u + 6))
                        if u >= 2:
                            pe.wait_ge(act_done.sem, act_done.at(2 + 3 * (u - 2)))
                        for kt in range(keys_of(qt) // P, 4):
                            mm = nc.tensor.transpose(psum[:, 2 + u % 2, kt * P:kt * P + P], prob[:, u % 2, kt * P:kt * P + P], ident[:])
                        mm.then_inc(pe_done.sem, 1)

                    def values(u):
                        qt, h = units[u]
                        pe.wait_ge(act_done.sem, act_done.at(2 + 3 * u))
                        if u >= 2:
                            pe.wait_ge(act_done.sem, act_done.at(3 + 3 * (u - 2)))
                        k0 = keys_of(qt) // P
                        for kt in range(k0, 4):
                            mm = nc.tensor.matmul(psum[rows_of[h], 4 + u % 2, 0:P], nv_tok[:, kt, h * NHD:h * NHD + NHD],
                                                  prob_t[:, u % 2, kt, :], start=(kt == k0), stop=(kt == 3))
                        mm.then_inc(pe_done.sem, 1)

                    scores(0)
                    for u in range(len(units)):
                        if u + 1 < len(units):
                            scores(u + 1)
                        else:
                            pass
                        transposes(u)
                        values(u)
                    pe_done.made += 3 * len(units)

                def pe_at(u, what):
                    last = len(units) - 1
                    if what == "scores":
                        return 1 if u == 0 else 1 + 3 * (u - 1) + 1
                    return 1 + 3 * u + (1 if u < last else 0) + {"transposes": 1, "values": 2}[what]

                @block.scalar
                def _(act):
                    for u, (qt, h) in enumerate(units):
                        k0 = keys_of(qt)
                        act.wait_ge(dve_done.sem, dve_done.at(1 + 6 * u + 4))
                        nc.scalar.activation(prob[:, u % 2, k0:NT], prob[:, u % 2, k0:NT], ACT.Exp,
                                             bias=na_stat[:, 0, u:u + 1], accum_out=na_stat[:, 1, u:u + 1]).then_inc(act_done.sem, 1)
                        act.wait_ge(pe_done.sem, pe_done.at(pe_at(u, "transposes")))
                        if u >= 2:
                            act.wait_ge(pe_done.sem, pe_done.at(pe_at(u - 2, "values")))
                        nc.scalar.copy(prob_t[:, u % 2, k0 // P:4, :],
                                       psum[:, 2 + u % 2, k0:NT].rearrange("p (k q) -> p k q", q=P)).then_inc(act_done.sem, 1)
                        act.wait_ge(pe_done.sem, pe_done.at(pe_at(u, "values")))
                        nc.scalar.copy(na_t[rows_of[h], h // 2, qt * P:qt * P + P],
                                       psum[rows_of[h], 4 + u % 2, 0:P]).then_inc(act_done.sem, 1)
                    act_done.made += 3 * len(units)

                @block.vector
                def _(dve):
                    dve.wait_ge(stage_in.sem, stage_in.at(16 * (4 * NH + 1)))
                    biasv = na_bias.rearrange("p r h (k c) -> p (r h k) c", c=GRID_W)
                    dve_done.link(dve, nc.vector.tensor_tensor(
                        biasv, biasv, na_mask.unsqueeze(1).to_broadcast([P, 2 * NH * 4, GRID_W]), ALU.add))
                    for u, (qt, h) in enumerate(units):
                        k0 = keys_of(qt)
                        dve.wait_ge(pe_done.sem, pe_done.at(pe_at(u, "scores")))
                        if u >= 2:
                            dve.wait_ge(pe_done.sem, pe_done.at(pe_at(u - 2, "transposes")))
                        s = prob[:, u % 2, :]
                        if k0 == 0:
                            dve_done.link(dve, nc.vector.scalar_tensor_tensor(
                                out=s[:, 0:S].rearrange("p (r c) -> p r c", c=GRID_W),
                                in0=psum[:, u % 2, 0:S].rearrange("p (r c) -> p r c", c=GRID_W), scalar=NHD ** -0.5,
                                in1=na_bias[:, qt, h, :].rearrange("p (r c) -> p r c", c=GRID_W)[:, :, ::-1],
                                op0=ALU.mult, op1=ALU.add))
                            rest = S
                        else:
                            dve_done.link(dve, nc.vector.tensor_scalar(s[:, S:S + P], psum[:, u % 2, S:S + P], NHD ** -0.5, None,
                                                                       ALU.mult))
                            rest = S + P
                        dve_done.link(dve, nc.vector.tensor_scalar(s[:, rest:NT], psum[:, u % 2, rest:NT], NHD ** -0.5, None,
                                                                   ALU.mult))
                        dve_done.link(dve, nc.vector.tensor_reduce(na_stat[:, 2, u:u + 1], s[:, k0:NT], AX.X, ALU.max))
                        dve_done.link(dve, nc.vector.tensor_scalar(na_stat[:, 0, u:u + 1], na_stat[:, 2, u:u + 1], -1.0, None, ALU.mult))
                        dve.wait_ge(act_done.sem, act_done.at(3 * u + 1))
                        dve_done.link(dve, nc.vector.reciprocal(na_stat[:, 2, u:u + 1], na_stat[:, 1, u:u + 1]))
                        dve_done.link(dve, nc.vector.tensor_scalar(s[:, k0:NT], s[:, k0:NT], na_stat[:, 2, u:u + 1], None, ALU.mult))
            end_stage()

        def merge(l, nt):
            branch = (conv, o_t, na_t)
            with nc.Block() as block:
                @block.sync
                def _(sp):
                    load_segment(sp)

                @block.tensor
                def _(pe):
                    for d in range(KC):
                        for j in range(3):
                            n = 5 * d + j
                            p = 3 * d + j
                            arrived(pe, n // RING, n % RING)
                            if p >= 4:
                                pe.wait_ge(act_done.sem, act_done.at(p - 3))
                            for k in range(KC):
                                mm = nc.tensor.matmul(psum[:, p % 4, 0:nt], blocks[n % RING][:, k, :], hT[:, k, 0:nt],
                                                      start=(k == 0), stop=(k == KC - 1))
                            mm.then_inc(used.sem, 1)
                        for j in range(3):
                            n = 5 * d + 3 + j // 2
                            p = 3 * d + j
                            if j != 1:
                                arrived(pe, n // RING, n % RING)
                            if p >= 4:
                                q = p - 4
                                pe.wait_ge(dve_done.sem, dve_done.at(5 * (q // 3) + (1, 2, 4)[q % 3]))
                            for k in range(4):
                                mm = nc.tensor.matmul(psum[:, 4 + p % 4, 0:nt], blocks[n % RING][:, 4 * (j % 2) + k, :],
                                                      branch[j][:, k, 0:nt], start=(k == 0), stop=(k == 3))
                            if j != 0:
                                mm.then_inc(used.sem, 1)
                    used.made += 40

                @block.scalar
                def _(act):
                    for p in range(3 * KC):
                        d, j = p // 3, p % 3
                        act.wait_ge(used.sem, used.at(5 * d + j + 1))
                        if p >= 4:
                            q = p - 4
                            act.wait_ge(dve_done.sem, dve_done.at(5 * (q // 3) + (1, 2, 4)[q % 3]))
                        nc.scalar.activation(gate_s[:, p % 4, 0:nt], psum[:, p % 4, 0:nt], ACT.Sigmoid,
                                             bias=col(l, "b_gate", j * KC + d)).then_inc(act_done.sem, 1)
                    act_done.made += 3 * KC

                @block.vector
                def _(dve):
                    for d in range(KC):
                        m = merged[:, d, 0:nt]
                        for j in range(3):
                            p = 3 * d + j
                            dve.wait_ge(act_done.sem, act_done.at(p + 1))
                            dve.wait_ge(used.sem, used.at(5 * d + (4, 4, 5)[j]))
                            to = m if j == 0 else branch_m[:, j - 1, 0:nt]
                            dve_done.link(dve, nc.vector.tensor_tensor(to, psum[:, 4 + p % 4, 0:nt], gate_s[:, p % 4, 0:nt], ALU.mult))
                            if j:
                                dve_done.link(dve, nc.vector.tensor_tensor(m, m, to, ALU.add))
            end_segment()

        def add_residual(dve, g, d, s, p):
            x = xT[:, d, s * S:s * S + S]
            return nc.vector.scalar_tensor_tensor(out=x, in0=p, scalar=mod[:, g + d, s:s + 1], in1=x, op0=ALU.mult, op1=ALU.add)

        def mixer_output(l, nt):
            with nc.Block() as block:
                @block.sync
                def _(sp):
                    load_segment(sp)

                @block.tensor
                def _(pe):
                    for d in range(KC):
                        arrived(pe, 0, d)
                        for k in range(KC):
                            mm = nc.tensor.matmul(psum[:, d, 0:nt], blocks[d][:, k, :], merged[:, k, 0:nt],
                                                  start=(k == 0), stop=(k == KC - 1))
                        mm.then_inc(used.sem, 1)
                    used.made += KC

                @block.vector
                def _(dve):
                    for d in range(KC):
                        dve.wait_ge(used.sem, used.at(d + 1))
                        for s in range(nt // S):
                            add_residual(dve, 16, d, s, psum[:, d, s * S:s * S + S])
            end_segment()

        def peer_scores(l, s):
            with nc.Block() as block:
                @block.sync
                def _(sp):
                    sp.dma_start(keys, A["keys"][l]).then_inc(stage_in.sem, 16)
                    stage_in.made += 16
                    load_segment(sp)

                @block.tensor
                def _(pe):
                    for n in range(16):
                        arrived(pe, n // RING, n % RING)
                        if n >= RING:
                            pe.wait_ge(act_done.sem, act_done.at(n - RING + 1))
                        for k in range(KC):
                            mm = nc.tensor.matmul(psum[:, n % 8, 0:S], blocks[n % RING][:, k, :], h_one[:, k, :],
                                                  start=(k == 0), stop=(k == KC - 1))
                        mm.then_inc(used.sem, 1)
                    used.made += 16
                    pe.wait_ge(stage_in.sem, stage_in.at(16))
                    pe.wait_ge(act_done.sem, act_done.at(16))
                    for tt in range(2):
                        for q in range(4):
                            for n in range(4 * q, 4 * q + 4):
                                mm = nc.tensor.matmul(psum[:, 4 * tt + q, (n % 4) * P:(n % 4) * P + P],
                                                      qry[:, n, tt * P:tt * P + P], keys[:, n, :], start=True, stop=True)
                            mm.then_inc(pe_done.sem, 1)
                    pe_done.made += 8

                @block.scalar
                def _(act):
                    for n in range(16):
                        act.wait_ge(used.sem, used.at(n + 1))
                        nc.scalar.copy(qry[:, n, :], psum[:, n % 8, 0:S]).then_inc(act_done.sem, 1)
                    for i in range(8):
                        act.wait_ge(pe_done.sem, pe_done.at(i + 1))
                        nc.scalar.copy(score[:, i // 4, 4 * (i % 4):4 * (i % 4) + 4, :],
                                       psum[:, i, :].rearrange("p (n k) -> p n k", n=4)).then_inc(act_done.sem, 1)
                    act_done.made += 24
            end_segment()

        def top16(dve, rows):
            group = 4
            for g in range(0, len(rows), group):
                lot = rows[g:g + group]
                start = dve_done.made
                for step in range(5):
                    for j, (val, big, place) in enumerate(lot):
                        if step:
                            dve.wait_ge(dve_done.sem, dve_done.at(start + (step - 1) * group + j + 1))
                        if step == 0:
                            ins = nc.vector.max(big[:, 0:8], val)
                        elif step == 1:
                            ins = nc.vector.max_index(place[:, 0:8], big[:, 0:8], val)
                        elif step == 2:
                            ins = nc.vector.match_replace(val, big[:, 0:8], val, NEG)
                        elif step == 3:
                            ins = nc.vector.max(big[:, 8:16], val)
                        else:
                            ins = nc.vector.max_index(place[:, 8:16], big[:, 8:16], val)
                        ins.then_inc(dve_done.sem, 1)
                dve_done.made += 5 * len(lot)
            dve.wait_ge(dve_done.sem, dve_done.at(dve_done.made))

        def peer_choice():
            with nc.Block() as block:
                @block.vector
                def _(dve):
                    top16(dve, [(score[:, tt, 2 * h + z, :], top_s[:, tt, h, z, :], top_iu[:, tt, h, z, :])
                                for tt in range(2) for h in range(PH) for z in range(2)])
                    dve_done.link(dve, nc.vector.tensor_copy(carve(11264, 512), top_i.bitcast(U32)))
                    full = [P, PH, PK, PK]
                    for tt in range(2):
                        dve_done.link(dve, nc.vector.tensor_tensor(
                            cand[:, tt].rearrange("p h (a b) -> p h a b", a=PK),
                            top_s[:, tt, :, 0, :].unsqueeze(3).to_broadcast(full),
                            top_s[:, tt, :, 1, :].unsqueeze(2).to_broadcast(full), ALU.add))
                    top16(dve, [(cand[:, tt, h, :], best_s[:, tt, h, :], best_ju[:, tt, h, :])
                                for tt in range(2) for h in range(PH)])
                    flat = best_j.bitcast(U32)
                    dve_done.link(dve, nc.vector.tensor_scalar(best_abu[:, 0, :], flat, 4, None, ALU.logical_shift_right))
                    dve_done.link(dve, nc.vector.tensor_scalar(best_abu[:, 1, :], flat, PK - 1, None, ALU.bitwise_and))
                    dve_done.link(dve, nc.vector.tensor_copy(carve(16896, 512), best_ab.bitcast(U32)))
                    for tt in range(2):
                        for z in range(2):
                            dve_done.link(dve, nc.vector.tensor_tensor(
                                hot, best_abf[:, z, tt].unsqueeze(3).to_broadcast(full),
                                iota[:, 0:PK].unsqueeze(1).unsqueeze(1).to_broadcast(full), ALU.is_equal))
                            dve_done.link(dve, nc.vector.tensor_tensor(
                                hot, hot, top_f[:, tt, :, z, :].unsqueeze(2).to_broadcast(full), ALU.mult))
                            dve_done.link(dve, nc.vector.tensor_reduce(
                                picked[:, z, tt, :].rearrange("p (h k) -> p h k", h=PH), hot, AX.X, ALU.add))
                    for tt in range(2):
                        g = picked[:, 2, tt, :].rearrange("p (h k) -> p h k", h=PH)
                        dve_done.link(dve, nc.vector.tensor_tensor(
                            g, best_s[:, tt], best_s[:, tt, :, 0:1].to_broadcast([P, PH, PK]), ALU.subtract))
                    made = dve_done.made
                    dve.wait_ge(act_done.sem, act_done.at(1))
                    dve_done.link(dve, nc.vector.tensor_reduce(
                        gsum[:, 0, :], picked[:, 2].rearrange("p t (h k) -> p (t h) k", h=PH), AX.X, ALU.add))
                    dve_done.link(dve, nc.vector.reciprocal(gsum[:, 1, :], gsum[:, 0, :]))
                    g = picked[:, 2].rearrange("p t (h k) -> p (t h) k", h=PH)
                    dve_done.link(dve, nc.vector.tensor_tensor(
                        g, g, gsum[:, 1, :].unsqueeze(2).to_broadcast([P, 2 * PH, PK]), ALU.mult))
                    peer_choice.exp_after = made

                @block.scalar
                def _(act):
                    act.wait_ge(dve_done.sem, dve_done.at(peer_choice.exp_after))
                    g = picked[:, 2]
                    act_done.link(act, nc.scalar.activation(g, g, ACT.Exp))
            end_stage()
            with nc.Block() as block:
                @block.tensor
                def _(pe):
                    for n in range(3):
                        for tt in range(2):
                            mm = nc.tensor.transpose(psum[:, n, tt * P:tt * P + P], picked[:, n, tt, :], ident[:])
                        mm.then_inc(pe_done.sem, 1)
                    pe_done.made += 3

                @block.scalar
                def _(act):
                    nc.scalar.copy(h_hi[:], h_one).then_inc(act_done.sem, 1)
                    act_done.made += 1

                @block.vector
                def _(dve):
                    for n in range(3):
                        dve.wait_ge(pe_done.sem, pe_done.at(n + 1))
                        nc.vector.tensor_copy(sel_t[:, n, :], psum[:, n, 0:S])
                    dve.wait_ge(act_done.sem, act_done.at(1))
                    nc.vector.tensor_tensor(h_lo[:], h_one, h_hi[:].bitcast(F32), ALU.subtract)
            end_stage()

        def peer_gates(l):
            with nc.Block() as block:
                @block.sync
                def _(sp):
                    for n in range(SPLIT):
                        sp.dma_start(raw[n], A["w_expert"][l, n]).then_inc(raw_landed[n], 16)

                @block.vector
                def _(dve):
                    def step(r, b, first=False):
                        if not first:
                            dve.wait_ge(gates_made.sem, r * ONEHOTS + gates_made.at(b - ONEHOTS + 1))
                        t = r * 4 * ONEHOTS + 4 * b
                        four = [P, 4, P]
                        nc.vector.tensor_tensor(onehot[:, b, 1], iota[:].unsqueeze(1).to_broadcast(four),
                                                sel_t[:, 1, bass.ds(t, 4)].unsqueeze(2).to_broadcast(four),
                                                ALU.is_equal).then_inc(onehots_made.sem, 1)
                        for j in range(4):
                            nc.vector.tensor_scalar(onehot[:, b, 0, j, :], iota[:], sel_t[:, 0, bass.ds(t + j, 1)],
                                                    sel_t[:, 2, bass.ds(t + j, 1)], ALU.is_equal, ALU.mult).then_inc(onehots_made.sem, 1)

                    for b in range(ONEHOTS):
                        step(0, b, first=True)
                    with dve.Fori(1, S // 4 // ONEHOTS) as r:
                        for b in range(ONEHOTS):
                            step(r, b)
                    onehots_made.made += 5 * (S // 4)

                @block.tensor
                def _(pe):
                    def step(r, b, first=False):
                        if not first:
                            pe.wait_ge(gates_out.sem, r * ONEHOTS + gates_out.at(b - ONEHOTS + 1))
                        pe.wait_ge(onehots_made.sem, r * 5 * ONEHOTS + onehots_made.at(5 * b + 5))
                        for j in range(4):
                            mm = nc.tensor.matmul(psum[:, b, j * P:j * P + P], onehot[:, b, 1, j, :], onehot[:, b, 0, j, :],
                                                  start=True, stop=True)
                        mm.then_inc(gates_made.sem, 1)

                    for b in range(ONEHOTS):
                        step(0, b, first=True)
                    with pe.Fori(1, S // 4 // ONEHOTS) as r:
                        for b in range(ONEHOTS):
                            step(r, b)
                    gates_made.made += S // 4

                @block.scalar
                def _(act):
                    with act.Fori(0, S // 4 // ONEHOTS) as r:
                        for b in range(ONEHOTS):
                            act.wait_ge(gates_made.sem, r * ONEHOTS + gates_made.at(b + 1))
                            nc.scalar.copy(gates[:, :, bass.ds(r * 4 * ONEHOTS + 4 * b, 4)],
                                           psum[:, b, :].rearrange("p (j i) -> p i j", j=4)).then_inc(gates_out.sem, 1)
                    gates_out.made += S // 4
            end_stage()

        def peer_experts(l, s):
            rounds = (ET - 2) // SPLIT
            n_blocks = 2 * ET

            def place_u(r, b):
                if isinstance(r, int):
                    i = SPLIT * r + b
                    return 0, (i if i < 2 else 2 * i - 2)
                return r * 2 * SPLIT, 2 * b - 2

            def place_v(r, b):
                if isinstance(r, int):
                    i = SPLIT * r + b
                    return 0, (2 * i + 3 if i <= ET - 3 else i + ET)
                return r * 2 * SPLIT, 2 * b + 3

            def acc(d):
                return psum[:, 4 + d // 2, (d % 2) * S:(d % 2) * S + S]

            def every_tile(eng, one):
                for b in range(SPLIT):
                    one(0, b)
                with eng.Fori(1, rounds) as r:
                    for b in range(SPLIT):
                        one(r, b)
                for b in range(2):
                    one(rounds, b)

            def tile_at(r, b):
                return r * SPLIT + b if isinstance(r, int) else None

            with nc.Block() as block:
                @block.sync
                def _(sp):
                    def load(n, slot, lo_value):
                        sp.wait_ge(lo_made.sem, lo_value)
                        sp.dma_start(raw[slot], A["w_expert"][l, n]).then_inc(raw_landed[slot], 16)

                    with sp.Fori(1, n_blocks // SPLIT) as q:
                        for n in range(SPLIT):
                            load(q * SPLIT + n, n, q * SPLIT + lo_made.at(n - SPLIT + 1))
                    last = n_blocks - 1
                    load(last, last % SPLIT, lo_made.at(last - SPLIT + 1))

                @block.tensor
                def _(pe):
                    def three(out, w, x, x_at, first, last):
                        for n, (a, b) in enumerate(((0, 0), (0, 1), (1, 0))):
                            mm = nc.tensor.matmul(out, w[a], x[b][x_at], start=(first and n == 0), stop=(last and n == 2),
                                                  skip_group_check=True)
                        return mm

                    def up(r, b):
                        i = tile_at(r, b)
                        r6, c = place_u(r, b)
                        pe.wait_ge(lo_made.sem, r6 + lo_made.at(c + 1))
                        if i is None or i >= SPLIT:
                            pe.wait_ge(act_lo_made.sem, r * SPLIT + act_lo_made.at(b - SPLIT + 1))
                        slot = c % SPLIT
                        for k in range(KC):
                            ck = slice(k * P, k * P + P)
                            mm = three(psum[:, b % SPLIT, 0:S], (w_hi[slot][:, ck], w_lo[slot][:, ck]), (h_hi, h_lo),
                                       (slice(None), k), k == 0, k == KC - 1)
                        mm.then_inc(expert_used.sem, 1)

                    def down(r, b, first=False, last=False):
                        r6, c = place_v(r, b)
                        pe.wait_ge(lo_made.sem, r6 + lo_made.at(c + 1))
                        pe.wait_ge(act_lo_made.sem, r * SPLIT + act_lo_made.at(b + 1))
                        slot = c % SPLIT
                        for d in range(KC):
                            cd = slice(d * P, d * P + P)
                            mm = three(acc(d), (w_hi[slot][:, cd], w_lo[slot][:, cd]), (act_hi, act_lo),
                                       (slice(None), b % SPLIT), first and d % 2 == 0, last)
                        mm.then_inc(expert_used.sem, 1)

                    def one(r, b):
                        up(r, b)
                        i = tile_at(r, b)
                        if i is None or i >= 2:
                            down(r, b - 2, first=(i == 2))

                    every_tile(pe, one)
                    down(rounds, 0)
                    down(rounds, 1, last=True)
                    expert_used.made += n_blocks

                @block.scalar
                def _(act):
                    loads = [run_loads[n] for n in range(SPLIT)]

                    def hi(r, place):
                        r6, c = place
                        slot = c % SPLIT
                        ahead = c // SPLIT if isinstance(r6, int) else r * 2 + c // SPLIT
                        act.wait_ge(raw_landed[slot], (ahead + (loads[slot] + 1)) * 16)
                        if not isinstance(r6, int) or c >= SPLIT:
                            act.wait_ge(expert_used.sem, r6 + expert_used.at(c - SPLIT + 1))
                        nc.scalar.copy(w_hi[slot][:], raw[slot]).then_inc(hi_made.sem, 1)

                    def one(r, b):
                        i = tile_at(r, b)
                        if i is None or i + 1 < ET:
                            hi(r, place_u(r, b + 1))
                        r6, c = place_u(r, b)
                        act.wait_ge(expert_used.sem, r6 + expert_used.at(c + 1))
                        nc.scalar.activation(psum[:, b, 0:S], psum[:, b, 0:S], ACT.Gelu).then_inc(gelu_made.sem, 1)
                        if i is None or i >= 1:
                            hi(r, place_v(r, b - 1))
                        act.wait_ge(gated_made.sem, r * SPLIT + gated_made.at(b + 1))
                        if i is None or i >= SPLIT:
                            r6, c = place_v(r, b - SPLIT)
                            act.wait_ge(expert_used.sem, r6 + expert_used.at(c + 1))
                        nc.scalar.copy(act_hi[:, b, :], psum[:, b, 0:S]).then_inc(act_hi_made.sem, 1)

                    hi(0, place_u(0, 0))
                    every_tile(act, one)
                    hi(rounds, place_v(rounds, 1))
                    hi_made.made += n_blocks
                    gelu_made.made += ET
                    act_hi_made.made += ET

                @block.vector
                def _(dve):
                    def lo(r, place):
                        r6, c = place
                        slot = c % SPLIT
                        dve.wait_ge(hi_made.sem, r6 + hi_made.at(c + 1))
                        nc.vector.tensor_tensor(w_lo[slot][:], raw[slot], w_hi[slot][:].bitcast(F32),
                                                ALU.subtract).then_inc(lo_made.sem, 1)

                    def one(r, b):
                        i = tile_at(r, b)
                        if i is None or i + 1 < ET:
                            lo(r, place_u(r, b + 1))
                        dve.wait_ge(gelu_made.sem, r * SPLIT + gelu_made.at(b + 1))
                        nc.vector.tensor_tensor(psum[:, b, 0:S], psum[:, b, 0:S], gates[:, r * SPLIT + b, :],
                                                ALU.mult).then_inc(gated_made.sem, 1)
                        if i is None or i >= 1:
                            lo(r, place_v(r, b - 1))
                        dve.wait_ge(act_hi_made.sem, r * SPLIT + act_hi_made.at(b + 1))
                        nc.vector.tensor_tensor(act_lo[:, b, :], psum[:, b, 0:S], act_hi[:, b, :].bitcast(F32),
                                                ALU.subtract).then_inc(act_lo_made.sem, 1)

                    lo(0, place_u(0, 0))
                    every_tile(dve, one)
                    lo(rounds, place_v(rounds, 1))
                    lo_made.made += n_blocks
                    gated_made.made += ET
                    act_lo_made.made += ET
                    dve.wait_ge(expert_used.sem, expert_used.at(n_blocks))
                    for d in range(KC):
                        add_residual(dve, 40, d, s, acc(d))
            for n in range(SPLIT):
                run_loads[n] += len(range(n, n_blocks, SPLIT))
            end_stage()

        def final_norm():
            g0 = PARAMS["final"][0]
            with nc.Block() as block:
                @block.scalar
                def _(act):
                    for k in range(KC):
                        nc.scalar.activation(nsq[:, k, 0:S], xT[:, k, 0:S], ACT.Square).then_inc(act_done.sem, 1)
                    act.wait_ge(pe_done.sem, pe_done.at(1))
                    nc.scalar.activation(nrs[:, 0:S], psum[:, 0, 0:S], ACT.Sqrt, bias=eps_col[:],
                                         scale=1.0 / D).then_inc(act_done.sem, 1)
                    act_done.made += KC + 1

                @block.tensor
                def _(pe):
                    for k in range(KC):
                        pe.wait_ge(act_done.sem, act_done.at(k + 1))
                        mm = nc.tensor.matmul(psum[:, 0, 0:S], ones[:], nsq[:, k, 0:S], start=(k == 0), stop=(k == KC - 1))
                    mm.then_inc(pe_done.sem, 1)
                    pe_done.made += 1

                @block.vector
                def _(dve):
                    dve.wait_ge(act_done.sem, act_done.at(KC + 1))
                    dve_done.link(dve, nc.vector.reciprocal(nrs[:, 0:S], nrs[:, 0:S]))
                    for k in range(KC):
                        nc.vector.scalar_tensor_tensor(out=hT[:, k, 0:S], in0=xT[:, k, 0:S], scalar=par[:, 0, g0 + k:g0 + k + 1],
                                                       in1=nrs[:, 0:S], op0=ALU.mult, op1=ALU.mult).then_inc(dve_done.sem, 1)
                    dve_done.made += KC

                @block.sync
                def _(sp):
                    sp.wait_ge(dve_done.sem, dve_done.at(1 + KC))
                    sp.dma_start(out, hT[:, :, 0:S]).then_inc(out_done.sem, 16)
                    sp.wait_ge(out_done.sem, out_done.at(16))
                    out_done.made += 16
            end_stage()

        def dump(name, ap):
            if debug and name in debug:
                with nc.Block() as block:
                    @block.sync
                    def _(sp):
                        sp.dma_start(debug[name], ap).then_inc(out_done.sem, 16)
                        sp.wait_ge(out_done.sem, out_done.at(16))
                        out_done.made += 16
                end_stage()

        start()
        for l in range(DEPTH):
            nt = NT if l == 0 else S
            modulation(l)
            adaln(l, 0, (0, 1), hT)
            if l == 0:
                dump("h", hT[:])
            projection(l, nt)
            if l == 0:
                dump("proj", proj)
            conv_module(l, nt)
            gla_features(l)
            for z in range(2):
                gla_direction(l, z, nt)
            gla_output(l, nt)
            neighbourhood(l, nt)
            if l == 0:
                dump("conv", conv)
                dump("gla", o_t)
                dump("na", na_t)
            merge(l, nt)
            mixer_output(l, nt)
            if l == 0:
                dump("x1", xT[:])
            for s in range(nt // S):
                adaln(l, 1, (s,), h_one)
                peer_scores(l, s)
                peer_choice()
                if l == 0 and s == 0:
                    dump("sel", sel_t[:])
                peer_gates(l)
                peer_experts(l, s)
            if l == 0:
                dump("x2", xT[:])
        final_norm()


def lay_out(i):
    f = {k: np.asarray(v) for k, v in i.items()}

    def chunks(v):
        return np.moveaxis(v.reshape(*v.shape[:-1], -1, P), -1, -2)

    def blocks_of(w):
        L, K, N = w.shape
        return w.reshape(L, K // P, P, N // P, P).transpose(0, 3, 2, 1, 4)

    a = {}
    x = np.concatenate([f["x"][0], f["ctx"][0]], 0)
    a["x"] = x.T.reshape(KC, P, NT).transpose(1, 0, 2)
    a["cond"] = np.stack([f["c"][0], f["c_ctx"]], -1).reshape(KC, P, 2).transpose(1, 0, 2)
    L = DEPTH
    cw = f["conv_w"].reshape(L, TAPS * CT, P)
    parts = [chunks(f["b_mod"]), chunks(f["norm1_g"]), chunks(f["norm2_g"]), chunks(f["b_gate"]), cw.transpose(0, 2, 1),
             chunks(f["conv_b"]), chunks(f["conv_ln_g"]), chunks(f["conv_ln_b"]), chunks(f["gla_ba"].reshape(L, -1)),
             chunks(f["gla_norm_g"]), np.broadcast_to(chunks(f["final_g"])[None], (L, P, KC))]
    a["params"] = np.concatenate(parts, -1).transpose(1, 0, 2)
    a["ident"] = np.eye(P, dtype=np.float32)
    a["iota"] = np.broadcast_to(np.arange(P, dtype=np.float32), (P, P))

    def flat(b):
        return b.reshape(b.shape[0], b.shape[1], P, D)

    a["w_mod"] = f["w_mod"].reshape(L, KC, P, 6, D).transpose(0, 3, 1, 2, 4).reshape(L, 48, P, D)
    at = np.cumsum([0, 1024, 256, 256, 512, 512, 32, 512, 512, 512, 3072]).tolist()
    glu, q, k, v, g, wa, nq, nk, nv, br = (f["w_in"][:, :, at[n]:at[n + 1]] for n in range(10))
    a["w_proj"] = flat(blocks_of(np.concatenate([glu, g, nq, q, k, nk, v, nv], -1)))
    a["w_a"] = wa.reshape(L, KC, P, 32).transpose(0, 2, 1, 3)
    a["wa2"] = f["gla_wa2"].transpose(0, 2, 1, 3)
    gates = blocks_of(br).reshape(L, 3, KC, P, KC, P).transpose(0, 2, 1, 3, 4, 5)
    oc, og, on = (blocks_of(f[n])[:, :, None] for n in ("w_conv_o", "w_gla_o", "w_na_o"))
    pair = np.concatenate([oc, og], 4)
    alone = np.concatenate([on, np.zeros_like(on)], 4)
    a["w_merge"] = np.concatenate([gates, pair, alone], 2).reshape(L, 5 * KC, P, D)
    a["w_out"] = flat(blocks_of(f["w_out"]))
    a["w_query"] = flat(blocks_of(f["peer_wq"]))
    a["keys"] = f["peer_keys"].reshape(L, 2 * PH, NKEYS, P).transpose(0, 3, 1, 2)
    u = f["peer_u"].reshape(L, ET, P, KC, P).transpose(0, 1, 4, 3, 2).reshape(L, ET, P, D)
    v = f["peer_v"].reshape(L, ET, P, D)
    e = np.empty((L, 2 * ET, P, D), np.float32)
    e[:, 0:2], e[:, 2:2 * ET - 2:2], e[:, 3:2 * ET - 2:2], e[:, 2 * ET - 2:] = u[:, 0:2], u[:, 2:], v[:, :ET - 2], v[:, ET - 2:]
    a["w_expert"] = e
    a["rpb"] = np.pad(f["na_rpb"][..., ::-1], ((0, 0), (0, 0), (0, 0), (GRID_W - KW, GRID_W - KW)))
    pos = np.arange(S)
    inv = np.float32(10000.0) ** (-np.arange(16, dtype=np.float32) / np.float32(16))
    ang = np.concatenate([(pos // GRID_W).astype(np.float32)[:, None] * inv, (pos % GRID_W).astype(np.float32)[:, None] * inv], -1)
    pair_of = (np.arange(P) % GDK) // 2
    a["rope"] = np.stack([np.cos(ang).T[pair_of], np.sin(ang).T[pair_of]], 1).astype(np.float32)
    swap = np.zeros((P, P), np.float32)
    swap[np.arange(1, P, 2), np.arange(0, P, 2)] = -1.0
    swap[np.arange(0, P, 2), np.arange(1, P, 2)] = 1.0
    a["swap"] = swap
    a["resets"] = np.broadcast_to((np.arange(NT) % CH != 0).astype(np.float32), (P, NT))
    cs = np.clip(np.arange(GRID_W) - KW // 2, 0, GRID_W - KW)
    ck = np.arange(GRID_W)
    ok = (ck[None] >= cs[:, None]) & (ck[None] < cs[:, None] + KW)
    a["na_mask"] = np.tile(np.where(ok, 0.0, -1e30).astype(np.float32)[:, ::-1], (2, 1))
    return {k: np.ascontiguousarray(v) for k, v in a.items()}


def kernel(**inputs):
    import concourse.bacc as _bacc
    from concourse.bass_utils import run_bass_kernel_spmd as _run

    arrays = lay_out(inputs)
    nc = _bacc.Bacc("TRN2", target_bir_lowering=False, num_devices=1)
    A = {n: nc.dram_tensor(f"in_{n}", a.shape, mybir.dt.from_np(a.dtype), kind="ExternalInput").ap() for n, a in arrays.items()}
    out = nc.dram_tensor("out", (P, KC, S), F32, kind="ExternalOutput").ap()
    build_program(nc, A, out)
    r = _run(nc, [{f"in_{n}": a for n, a in arrays.items()}], core_ids=[0])
    y = r.results[0]["out"]
    return np.ascontiguousarray(y.transpose(2, 1, 0).reshape(1, S, D))
```

```python
from contextlib import ExitStack

import numpy as np

import concourse.bass as bass
from concourse import mybir

F32 = mybir.dt.float32
F32R = mybir.dt.float32r
U32 = mybir.dt.uint32
ALU = mybir.AluOpType
ACT = mybir.ActivationFunctionType
AX = mybir.AxisListType

P = 128
D = 1024
KC = D // P
S = 256
NT = 2 * S
DEPTH = 2
EPS = 1e-6
GRID_W = 64
CONV, TAPS = 512, 31
HALO = TAPS // 2
CT = CONV // P
GH, GDK, GDV, GR = 4, 64, 128, 16
CH = 64
NCH = NT // CH
GATE_NORM = 16.0
NH, NHD = 8, 64
KH, KW = 8, 16
RPW = 2 * GRID_W - 1
PH, PK, NKEYS = 8, 16, 128
ET = NKEYS
RING = 8
SPLIT = 3
ONEHOTS = 4
NEG = -3.0e38

PARAMS = {}
_at = 0
for _name, _n in (("b_mod", 48), ("norm1", KC), ("norm2", KC), ("b_gate", 24), ("conv_w", TAPS * CT), ("conv_b", CT),
                  ("ln_g", CT), ("ln_b", CT), ("ba", 4), ("gla_g", GH), ("final", KC)):
    PARAMS[_name] = (_at, _at + _n)
    _at += _n
NPARAM = _at

T_GLU, T_G, T_NQ, T_Q, T_K, T_NK = 0, 8, 12, 16, 18, 20
CHANNEL_TILES = 24


class Count:

    def __init__(self, sem):
        self.sem, self.base, self.made = sem, 0, 0

    def at(self, n):
        return self.base + n

    def link(self, eng, ins):
        ins.then_inc(self.sem, 1)
        self.made += 1
        eng.wait_ge(self.sem, self.base + self.made)

    def close(self):
        self.base, self.made = self.base + self.made, 0


def build_program(nc, A, out, debug=None):
    ctx = ExitStack()
    with ctx:
        def sb(name, shape, dt=F32):
            return ctx.enter_context(nc.sbuf_tensor(name, shape, dt))

        counts = []

        def sem(name):
            return ctx.enter_context(nc.semaphore(name))

        def count(name):
            counts.append(Count(sem(name)))
            return counts[-1]

        xT = sb("xT", [P, KC, NT])
        h_at = (nc.sbuf_base + 31) // 32 * 32
        hT = sb("hT", [P, KC, NT])
        h_one = hT[:].rearrange("p k t -> p (k t)")[:, 0:KC * S].rearrange("p (k t) -> p k t", k=KC)
        h_lo = nc.alloc_sbuf_tensor_at("h_lo", [P, KC, S], F32R, offset=h_at)
        h_hi = nc.alloc_sbuf_tensor_at("h_hi", [P, KC, S], F32R, offset=h_at + 4 * KC * S)
        slab_at = (nc.sbuf_base + 31) // 32 * 32
        slab = sb("slab", [P, 3 * SPLIT * D])
        ring = slab[:, 0:RING * D].rearrange("p (b c) -> p b c", b=RING)
        blocks = [ring[:, b, :].rearrange("p (k c) -> p k c", k=KC) for b in range(RING)]
        raw = [slab[:, n * D:n * D + D] for n in range(SPLIT)]
        w_hi = [nc.alloc_sbuf_tensor_at(f"w_hi{n}", [P, D], F32R, offset=slab_at + 4 * D * (SPLIT + 2 * n)) for n in range(SPLIT)]
        w_lo = [nc.alloc_sbuf_tensor_at(f"w_lo{n}", [P, D], F32R, offset=slab_at + 4 * D * (SPLIT + 2 * n + 1)) for n in range(SPLIT)]
        sel_t = slab[:, SPLIT * D:SPLIT * D + 3 * S].rearrange("p (n t) -> p n t", n=3)
        onehot_at = SPLIT * D + 3 * S
        onehot = slab[:, onehot_at:onehot_at + ONEHOTS * 2 * 4 * P].rearrange("p (b z j i) -> p b z j i", b=ONEHOTS, z=2, j=4)
        par = sb("par", [P, DEPTH, NPARAM])
        mods = sb("mods", [P, DEPTH, 48, 2])
        scale1 = sb("scale1", [P, KC, 2])
        cond = sb("cond", [P, KC, 2])
        ident = sb("ident", [P, P])
        ones = sb("ones", [P, P])
        iota = sb("iota", [P, P])
        eps_col = sb("eps_col", [P, 1])
        act_hi = sb("act_hi", [P, SPLIT, S], F32R)
        act_lo = sb("act_lo", [P, SPLIT, S], F32R)
        arena_at = (nc.sbuf_base + 31) // 32 * 32
        arena = sb("arena", [P, ET * S])

        def halves_at(name, n, at):
            return nc.alloc_sbuf_tensor_at(name, [P, n, NT], F32R, offset=arena_at + 4 * at)
        psum = ctx.enter_context(nc.psum_tensor("psum", [P, 8, 512], F32))

        def carve(at, n):
            return arena[:, at:at + n]

        proj = carve(0, CHANNEL_TILES * NT).rearrange("p (n t) -> p n t", n=CHANNEL_TILES)
        v_tok = carve(12288, 2048).rearrange("p (t c) -> p t c", t=4)
        nv_tok = carve(14336, 2048).rearrange("p (t c) -> p t c", t=4)
        conv = carve(16384, 2048).rearrange("p (n t) -> p n t", n=CT)
        o_t = carve(18432, 2048).rearrange("p (n t) -> p n t", n=GH)
        na_t = carve(20480, 2048).rearrange("p (n t) -> p n t", n=4)
        work = 22528
        ph_hi, ph_lo = halves_at("ph_hi", KC, 18432), halves_at("ph_lo", KC, 18432 + 4096)
        work_conv = 26624
        upad = carve(work_conv, CT * 2 * (S + 2 * HALO)).rearrange("p (n s t) -> p n s t", n=CT, s=2)
        sq = carve(20480, 2048).rearrange("p (n t) -> p n t", n=CT)
        MOD_ROWS = 18432
        stat = carve(19456, 1024).rearrange("p (n t) -> p n t", n=2)
        decay = carve(0, 2048).rearrange("p (n t) -> p n t", n=4)
        runsum = carve(2048, 2048).rearrange("p (n t) -> p n t", n=4)
        def tiles(at, n=2):
            return carve(at, n * NT).rearrange("p (n t) -> p n t", n=n)

        f_q, f_k = (tiles(work), tiles(0)), (tiles(work + 1024), tiles(1024))
        f_qe, f_ke = (tiles(work + 2048), tiles(20480)), (tiles(work + 3072), tiles(work + 8640))
        ke_tok = [carve(at, 1024).rearrange("p (t c) -> p t c", t=4) for at in (work + 4096, work + 6720)]
        attm = [carve(at, 1024).rearrange("p (t h i) -> p t h i", t=4, h=GH) for at in (work + 5120, 21504)]
        state = [carve(at, 512).rearrange("p (h e) -> p h e", h=GH) for at in (work + 6144, work + 7744)]
        chunk_decay = [carve(at, 16) for at in (work + 6656, work + 8256)]
        gla_sq, gla_rs = tiles(work, GH), tiles(work + 2048, GH)
        a_t = carve(work + 6720, NT)
        w_a = carve(work + 7744, 512).rearrange("p (k c) -> p k c", k=KC)
        wa2 = carve(work + 8256, 256)
        rope = carve(work + 8512, 512).rearrange("p (n t) -> p n t", n=2)
        swap = carve(work + 9024, 128)
        resets = carve(work + 9152, 512)
        na_bias = carve(0, 4096).rearrange("p (r h k) -> p r h k", r=2, h=NH)
        prob = carve(work + 4096, 1024).rearrange("p (b k) -> p b k", b=2)
        prob_t = carve(work + 5120, 1024).rearrange("p (b k q) -> p b k q", b=2, k=4)
        na_stat = carve(work + 6144, 32 * 4).rearrange("p (n u) -> p n u", n=4)
        na_mask = carve(work + 9664, 64)
        merged = carve(work, 4096).rearrange("p (n t) -> p n t", n=KC)
        gate_s = carve(work + 4096, 2048).rearrange("p (n t) -> p n t", n=4)
        branch_m = carve(work + 6144, 1024).rearrange("p (n t) -> p n t", n=2)
        mh_hi, mh_lo = halves_at("mh_hi", KC, 0), halves_at("mh_lo", KC, 4096)
        br_hi = [halves_at(f"br_hi{j}", 4, 8192 + 2048 * j) for j in range(3)]
        br_lo = [halves_at(f"br_lo{j}", 4, 16384 + 2048 * j) for j in range(3)]
        mg_hi, mg_lo = halves_at("mg_hi", KC, 0), halves_at("mg_lo", KC, work)
        nsq = carve(work, 4096).rearrange("p (n t) -> p n t", n=KC)
        nrs = carve(work + 4096, 512)
        mod_row = arena[0:2, work:work + 6 * D]
        gates = arena[:, :].rearrange("p (i t) -> p i t", i=ET)
        qry = carve(0, 4096).rearrange("p (n t) -> p n t", n=16)
        keys = carve(4096, 2048).rearrange("p (n k) -> p n k", n=16)
        score = carve(6144, 4096).rearrange("p (t n k) -> p t n k", t=2, n=16)
        top_s = carve(10240, 512).rearrange("p (t h z k) -> p t h z k", t=2, h=PH, z=2)
        top_i = carve(10752, 512)
        top_iu = top_i.bitcast(U32).rearrange("p (t h z k) -> p t h z k", t=2, h=PH, z=2)
        top_f = carve(11264, 512).rearrange("p (t h z k) -> p t h z k", t=2, h=PH, z=2)
        cand = carve(11776, 4096).rearrange("p (t h c) -> p t h c", t=2, h=PH)
        best_s = carve(15872, 256).rearrange("p (t h k) -> p t h k", t=2, h=PH)
        best_j = carve(16128, 256)
        best_ju = best_j.bitcast(U32).rearrange("p (t h k) -> p t h k", t=2, h=PH)
        best_ab = carve(16384, 512)
        best_abu = best_ab.bitcast(U32).rearrange("p (z u) -> p z u", z=2)
        best_abf = carve(16896, 512).rearrange("p (z t h k) -> p z t h k", z=2, t=2, h=PH)
        hot = carve(17408, 2048).rearrange("p (h k c) -> p h k c", h=PH, k=PK)
        picked = carve(19456, 768).rearrange("p (n t u) -> p n t u", n=3, t=2)
        gsum = carve(20224, 32).rearrange("p (n u) -> p n u", n=2)

        landed = [sem(f"block_landed_{b}") for b in range(RING)]
        rows_out = count("mod_rows_copied")
        half_made = count("mod_first_half_in_psum")
        logs_made = count("log_of_mean_made")
        columns_in = count("mod_columns_in_psum")
        used = count("mod_block_used")
        split_used = count("split_block_used")
        par_in = count("param_landed")
        stage_in = count("stage_input_landed")
        pe_done = count("pe_group_done")
        act_done = count("act_step_done")
        dve_done = count("dve_step_done")
        pool_done = count("pool_step_done")
        out_done = count("output_written")
        raw_landed = [sem(f"raw_block_landed_{n}") for n in range(SPLIT)]
        hi_made = count("block_hi_made")
        lo_made = count("block_lo_made")
        query_out = count("queries_copied")
        score_made = count("head_scores_in_psum")
        score_out = count("head_scores_copied")
        picks_made = count("best_sums_shifted")
        gelu_made = count("gelu_made")
        gated_made = count("gated_made")
        act_hi_made = count("gated_hi_made")
        act_lo_made = count("gated_lo_made")
        onehots_made = count("onehots_made")
        columns_made = count("column_onehots_by_act")
        distance_made = count("column_distances_by_act")
        gates_made = count("gates_in_psum")
        gates_out = count("gates_evacuated")
        tile_act = count("tile_evacuated_by_act")
        norm_pe, norm_act, norm_dve = count("conv_norm_sums"), count("conv_norm_act_step"), count("conv_norm_dve_step")
        gla_dve, gla_act, gla_pe = ([count(f"gla_{what}_{z}") for z in range(2)] for what in ("scaled", "factors", "products"))
        na_scored = count("na_scores_in_psum")
        na_maxed = count("na_maximum_taken")
        na_biased = count("na_bias_added")
        na_inverted = count("na_sum_inverted")
        na_exped = count("na_exponentials_made")
        na_normed = count("na_probabilities_made")
        na_turned = count("na_transposes_in_psum")
        na_copied = count("na_transposes_copied")
        na_valued = count("na_output_in_psum")
        na_out = count("na_output_copied")

        def end_stage():
            for c in counts:
                c.close()

        ada_squared, ada_summed, ada_root, ada_factors, ada_scaled, ada_shifted, ada_hi, ada_lo = (
            count(f"adaln_{what}") for what in ("chunk_squared", "squares_summed", "inverse_root_made", "factors_made",
                                                "chunk_scaled", "chunk_shifted", "chunk_hi_made", "chunk_lo_made"))

        ring_rounds = [0]
        raw_loads = [0] * SPLIT

        def first_blocks(sp, src, after=None):
            for n in range(SPLIT):
                if after is not None:
                    last = max(m for m in range(after) if m % SPLIT == n)
                    sp.wait_ge(lo_made.sem, lo_made.at(last + 1))
                sp.dma_start(raw[n], src[n]).then_inc(raw_landed[n], 16)

        def load_blocks(sp, src, n_blocks):
            def load(n, slot, value):
                sp.wait_ge(lo_made.sem, value)
                sp.dma_start(raw[slot], src[n]).then_inc(raw_landed[slot], 16)

            whole = n_blocks // SPLIT
            with sp.Fori(1, whole) as q:
                for n in range(SPLIT):
                    load(q * SPLIT + n, n, q * SPLIT + lo_made.at(n - SPLIT + 1))
            for n in range(whole * SPLIT, n_blocks):
                load(n, n % SPLIT, lo_made.at(n - SPLIT + 1))

        def hi(act, n):
            slot = n % SPLIT
            act.wait_ge(raw_landed[slot], (raw_loads[slot] + n // SPLIT + 1) * 16)
            if n >= SPLIT:
                act.wait_ge(split_used.sem, split_used.at(n - SPLIT + 1))
            nc.scalar.copy(w_hi[slot][:], raw[slot]).then_inc(hi_made.sem, 1)

        def lo(eng, n):
            slot = n % SPLIT
            eng.wait_ge(hi_made.sem, hi_made.at(n + 1))
            eng.tensor_tensor(w_lo[slot][:], raw[slot], w_hi[slot][:].bitcast(F32), ALU.subtract).then_inc(lo_made.sem, 1)

        def end_stream(n_blocks):
            hi_made.made += n_blocks
            lo_made.made += n_blocks
            split_used.made += n_blocks
            for n in range(SPLIT):
                raw_loads[n] += len(range(n, n_blocks, SPLIT))
            end_stage()

        def three(out, w, x, first, last):
            for n, (a, b) in enumerate(((0, 0), (0, 1), (1, 0))):
                mm = nc.tensor.matmul(out, w[a], x[b], start=(first and n == 0), stop=(last and n == 2), skip_group_check=True)
            return mm

        def halves(n, k):
            c = slice(k * P, k * P + P)
            return w_hi[n % SPLIT][:, c], w_lo[n % SPLIT][:, c]

        def col(l, name, i):
            a = PARAMS[name][0] + i
            return par[:, l, a:a + 1]

        def inverse_root(act, out, mean_of, n, count_):
            nc.scalar.activation(out, mean_of, ACT.Ln, bias=eps_col[:], scale=1.0 / n).then_inc(logs_made.sem, 1)
            logs_made.made += 1
            act.wait_ge(logs_made.sem, logs_made.at(logs_made.made))
            nc.scalar.activation(out, out, ACT.Exp, scale=-0.5).then_inc(count_.sem, 1)

        def start():
            with nc.Block() as block:
                @block.sync
                def _(sp):
                    sp.dma_start(cond[:], A["cond"]).then_inc(par_in.sem, 16)

                @block.vector
                def _(dve):
                    nc.vector.memset(ones[:], 1.0)
                    nc.vector.memset(eps_col[:], EPS)

                @block.scalar
                def _(act):
                    act.wait_ge(par_in.sem, 16)
                    nc.scalar.activation(cond[:], cond[:], ACT.Silu)
            par_in.made = 16
            end_stage()

        def load_inputs(sp):
            for to, src in ((par, "params"), (ident, "ident"), (iota, "iota"), (xT, "x")):
                sp.dma_start(to[:], A[src]).then_inc(par_in.sem, 16)
            par_in.made += 64

        class Modulation:

            def __init__(self, l, first, last, bank, row_at=work):
                self.l, self.first, self.rounds, self.bank = l, first, last - first, bank
                self.rows = arena[0:2, row_at:row_at + self.rounds * D]
                self.before = ring_rounds[0]

            def load_round(self, sp, r):
                for b in range(RING):
                    if not isinstance(r, int) or r > 0:
                        sp.wait_ge(used.sem, (self.before + r - 1) * RING + b + 1)
                    sp.dma_start(ring[:, b, :], A["w_mod"][self.l, (self.first + r) * RING + b]).then_inc(landed[b], 16)

            def load(self, sp):
                self.load_round(sp, 0)
                with sp.Fori(1, self.rounds) as r:
                    self.load_round(sp, r)

            def products(self, pe, a, b):
                def one(c, fresh):
                    if not fresh:
                        pe.wait_ge(rows_out.sem, c * 2 + rows_out.at(0))
                    for k in range(KC):
                        pe.wait_ge(landed[k], (c + self.before + 1) * 16)
                        for n in range(2):
                            mm = nc.tensor.matmul(psum[0:2, self.bank + n, :], cond[:, k, :], ring[:, k, n * 512:n * 512 + 512],
                                                  start=(k == 0), stop=(k == KC - 1))
                        mm.then_inc(used.sem, 1)
                one(a, True)
                if b > a + 1:
                    with pe.Fori(a + 1, b) as c:
                        one(c, False)

            def copy_rows(self, act, a, b):
                with act.Fori(a, b) as c:
                    act.wait_ge(used.sem, c * RING + used.at(RING))
                    for n in range(2):
                        nc.scalar.copy(self.rows[:, bass.ds(c * D + n * 512, 512)],
                                       psum[0:2, self.bank + n, :]).then_inc(rows_out.sem, 1)

            def one_product(self, pe, u):
                c, n, k = u // 16, u // 8 % 2, u % 8
                if k == 0 and u:
                    pe.wait_ge(rows_out.sem, rows_out.at(u // 8))
                if n == 0:
                    pe.wait_ge(landed[k], (c + self.before + 1) * 16)
                mm = nc.tensor.matmul(psum[0:2, self.bank, :], cond[:, k, :], ring[:, k, n * 512:n * 512 + 512],
                                      start=(k == 0), stop=(k == KC - 1))
                if n == 1:
                    mm.then_inc(used.sem, 1)
                elif k == KC - 1:
                    mm.then_inc(half_made.sem, 1)

            def copy_half(self, act, i):
                if i % 2:
                    act.wait_ge(used.sem, used.at(RING * (i // 2 + 1)))
                else:
                    act.wait_ge(half_made.sem, half_made.at(i // 2 + 1))
                nc.scalar.copy(self.rows[:, i * 512:i * 512 + 512], psum[0:2, self.bank, :]).then_inc(rows_out.sem, 1)

            def columns(self, pe, a, b):
                pe.wait_ge(rows_out.sem, rows_out.at(2 * b))
                for n in range(8 * a, 8 * b):
                    mm = nc.tensor.transpose(psum[:, self.bank, 2 * n:2 * n + 2], self.rows[:, n * P:n * P + P], ident[0:2, 0:2])
                mm.then_inc(columns_in.sem, 1)

            def add_bias(self, dve, a, b):
                columns_in.made += 1
                dve.wait_ge(columns_in.sem, columns_in.at(columns_in.made))
                lo_, hi_ = 8 * (self.first + a), 8 * (self.first + b)
                m = psum[:, self.bank, 16 * a:16 * b].rearrange("p (n s) -> p n s", s=2)
                at = PARAMS["b_mod"][0]
                for s in range(2):
                    dve_done.link(dve, nc.vector.tensor_tensor(mods[:, self.l, lo_:hi_, s], m[:, :, s],
                                                               par[:, self.l, at + lo_:at + hi_], ALU.add))

            def finish(self):
                used.made += self.rounds * RING
                rows_out.made += 2 * self.rounds
                ring_rounds[0] += self.rounds

        def modulation(l, first, last):
            mod = Modulation(l, first, last, 0)
            n = last - first
            with nc.Block() as block:
                @block.sync
                def _(sp):
                    mod.load_round(sp, 0)
                    load_inputs(sp)
                    for r in range(1, n):
                        mod.load_round(sp, r)

                @block.tensor
                def _(pe):
                    mod.products(pe, 0, n)
                    pe.wait_ge(par_in.sem, par_in.at(64))
                    mod.columns(pe, 0, n)

                @block.scalar
                def _(act):
                    mod.copy_rows(act, 0, n)

                @block.vector
                def _(dve):
                    mod.add_bias(dve, 0, n)
            mod.finish()
            end_stage()

        class AdaLN:

            def __init__(self, l, which, streams, to, to_hi, to_lo):
                self.l, self.streams, self.to, self.to_hi, self.to_lo = l, streams, to, to_hi, to_lo
                self.ns = len(streams)
                self.nt = self.ns * S
                self.cols = slice(streams[0] * S, streams[0] * S + self.nt)
                self.sh, self.sc = (0, 8) if which == 0 else (24, 32)
                self.g = PARAMS["norm1" if which == 0 else "norm2"]

            def squares(self, act):
                for k in range(KC):
                    nc.scalar.activation(nsq[:, k, 0:self.nt], xT[:, k, self.cols], ACT.Square).then_inc(ada_squared.sem, 1)

            def mean(self, pe):
                for k in range(KC):
                    pe.wait_ge(ada_squared.sem, ada_squared.at(k + 1))
                    mm = nc.tensor.matmul(psum[:, 0, 0:self.nt], ones[:], nsq[:, k, 0:self.nt], start=(k == 0), stop=(k == KC - 1))
                mm.then_inc(ada_summed.sem, 1)

            def shift(self, act):
                act.wait_ge(ada_summed.sem, ada_summed.at(1))
                inverse_root(act, nrs[:, 0:self.nt], psum[:, 0, 0:self.nt], D, ada_root)
                for k in range(KC):
                    for j, s in enumerate(self.streams):
                        t = slice(j * S, j * S + S)
                        act.wait_ge(ada_scaled.sem, ada_scaled.at(k * self.ns + j + 1))
                        nc.scalar.activation(self.to[:, k, t], self.to[:, k, t], ACT.Identity,
                                             bias=mods[:, self.l, self.sh + k, s:s + 1]).then_inc(ada_shifted.sem, 1)
                    act.wait_ge(ada_shifted.sem, ada_shifted.at((k + 1) * self.ns))
                    nc.scalar.copy(self.to_hi[:, k, 0:self.nt], self.to[:, k, 0:self.nt]).then_inc(ada_hi.sem, 1)

            def factors(self, dve):
                a, b = self.g
                for s in range(2):
                    nc.vector.scalar_tensor_tensor(
                        out=scale1[:, :, s], in0=mods[:, self.l, self.sc:self.sc + KC, s], scalar=1.0,
                        in1=par[:, self.l, a:b], op0=ALU.add, op1=ALU.mult).then_inc(ada_factors.sem, 1)

            def scale(self, dve):
                dve.wait_ge(ada_factors.sem, ada_factors.at(2))
                dve.wait_ge(ada_root.sem, ada_root.at(1))
                for k in range(KC + 1):
                    if k < KC:
                        for j, s in enumerate(self.streams):
                            t = slice(j * S, j * S + S)
                            nc.vector.scalar_tensor_tensor(
                                out=self.to[:, k, t], in0=xT[:, k, s * S:s * S + S], scalar=scale1[:, k, s:s + 1],
                                in1=nrs[:, t], op0=ALU.mult, op1=ALU.mult).then_inc(ada_scaled.sem, 1)
                    if k:
                        dve.wait_ge(ada_hi.sem, ada_hi.at(k))
                        nc.vector.tensor_tensor(self.to_lo[:, k - 1, 0:self.nt], self.to[:, k - 1, 0:self.nt],
                                                self.to_hi[:, k - 1, 0:self.nt].bitcast(F32), ALU.subtract).then_inc(ada_lo.sem, 1)

            def finish(self):
                for c, n in ((ada_squared, KC), (ada_summed, 1), (ada_root, 1), (ada_factors, 2), (ada_scaled, KC * self.ns),
                             (ada_shifted, KC * self.ns), (ada_hi, KC), (ada_lo, KC)):
                    c.made += n

        def projection_and_conv(l, nt, ada):
            ns = nt // S
            n_blocks = 32
            first_conv = 8
            acc = [conv[:, c, 0:nt].rearrange("p (s t) -> p s t", s=ns) for c in range(CT)]
            w0 = PARAMS["conv_w"][0]
            cw = par[:, l, w0:w0 + TAPS * CT].rearrange("p (w c) -> p w c", c=CT)

            def tile_of(n):
                return n if n < 8 else n - 8

            def evacuations(n):
                return n + 1 if n < 8 else 8 + (n >= 11) + (n >= 15) + max(0, n - 15)

            with nc.Block() as block:
                @block.sync
                def _(sp):
                    first_blocks(sp, A["w_proj"][l])
                    load_blocks(sp, A["w_proj"][l], n_blocks)
                    for to, src in ((w_a, A["w_a"][l]), (wa2[0:GR], A["wa2"][l, 0]), (wa2[32:32 + GR], A["wa2"][l, 1]), (rope, A["rope"]), (swap, A["swap"]),
                                    (resets, A["resets"])):
                        sp.dma_start(to, src).then_inc(stage_in.sem, 16)
                    stage_in.made += 96

                @block.tensor
                def _(pe):
                    ada.mean(pe)
                    for n in range(n_blocks):
                        pe.wait_ge(lo_made.sem, lo_made.at(n + 1))
                        if 8 <= n < 16:
                            if n == 12:
                                pe.wait_ge(tile_act.sem, tile_act.at(evacuations(11)))
                            for tt in range(4):
                                for kk in range(2):
                                    k = 2 * (n % 4) + kk
                                    t = slice(tt * P, tt * P + P)
                                    c = slice(kk * 512, kk * 512 + 512)
                                    mm = three(psum[:, 4 + tt, :], (ph_hi[:, k, t], ph_lo[:, k, t]),
                                               (w_hi[n % SPLIT][:, c], w_lo[n % SPLIT][:, c]), k == 0, k == KC - 1)
                        else:
                            c = tile_of(n)
                            if c >= SPLIT:
                                back = n - SPLIT if n < 8 or n >= 16 + SPLIT else n - 8 - SPLIT
                                pe.wait_ge(tile_act.sem, tile_act.at(evacuations(back)))
                            width = nt if c < T_K else NT
                            for k in range(KC):
                                if n == 0:
                                    pe.wait_ge(ada_lo.sem, ada_lo.at(k + 1))
                                mm = three(psum[:, c % SPLIT, 0:width], halves(n, k),
                                           (ph_hi[:, k, 0:width], ph_lo[:, k, 0:width]), k == 0, k == KC - 1)
                        mm.then_inc(split_used.sem, 1)

                @block.scalar
                def _(act):
                    ada.squares(act)
                    for n in range(SPLIT):
                        hi(act, n)
                    ada.shift(act)
                    for n in range(n_blocks):
                        if n < 8 or n >= 16:
                            c = tile_of(n)
                            width = nt if c < T_K else NT
                            act.wait_ge(split_used.sem, split_used.at(n + 1))
                            func = ACT.Sigmoid if 4 <= n < 8 else ACT.Copy
                            scale = NHD ** -0.5 if T_NQ <= c < T_Q else 1.0
                            nc.scalar.activation(proj[:, c, 0:width], psum[:, c % SPLIT, 0:width], func,
                                                 scale=scale).then_inc(tile_act.sem, 1)
                        elif n in (11, 15):
                            act.wait_ge(split_used.sem, split_used.at(n + 1))
                            nc.scalar.copy(v_tok if n == 11 else nv_tok, psum[:, 4:8, :]).then_inc(tile_act.sem, 1)
                        if n + SPLIT < n_blocks:
                            hi(act, n + SPLIT)
                    tile_act.made += evacuations(n_blocks - 1)

                @block.vector
                def _(dve):
                    def glu(c):
                        dve.wait_ge(tile_act.sem, tile_act.at(evacuations(4 + c)))
                        dve.wait_ge(dve_done.sem, dve_done.at(1))
                        nc.vector.tensor_tensor(
                            upad[:, c, 0:ns, HALO:HALO + S], proj[:, T_GLU + c, 0:nt].rearrange("p (s t) -> p s t", s=ns),
                            proj[:, T_GLU + 4 + c, 0:nt].rearrange("p (s t) -> p s t", s=ns), ALU.mult).then_inc(dve_done.sem, 1)

                    def tap(m):
                        w, c = m // CT, m % CT
                        if w == 0:
                            dve.wait_ge(dve_done.sem, dve_done.at(1 + c + 1))
                            nc.vector.tensor_scalar(acc[c], upad[:, c, 0:ns, 0:S], cw[:, 0, c:c + 1], col(l, "conv_b", c),
                                                    ALU.mult, ALU.add).then_inc(dve_done.sem, 1)
                        else:
                            dve.wait_ge(dve_done.sem, dve_done.at(5 + m - CT + 1))
                            nc.vector.scalar_tensor_tensor(
                                out=acc[c], in0=upad[:, c, 0:ns, w:w + S], scalar=cw[:, w, c:c + 1], in1=acc[c],
                                op0=ALU.mult, op1=ALU.add).then_inc(dve_done.sem, 1)

                    ada.factors(dve)
                    for n in range(SPLIT):
                        lo(dve, n)
                    ada.scale(dve)
                    dve.wait_ge(ada_scaled.sem, ada_scaled.at(KC * ada.ns))
                    nc.vector.memset(upad, 0.0).then_inc(dve_done.sem, 1)
                    taps = 0
                    for n in range(n_blocks):
                        if n + SPLIT < n_blocks:
                            lo(dve, n + SPLIT)
                        if 4 <= n < 8:
                            glu(n - 4)
                        if n >= first_conv:
                            for _ in range(6 if nt == NT else 10):
                                if taps < TAPS * CT:
                                    tap(taps)
                                    taps += 1
                    while taps < TAPS * CT:
                        tap(taps)
                        taps += 1
                    dve_done.made += 5 + CT * TAPS
            ada.finish()
            end_stream(n_blocks)

        def gla_features(l, nt, mod):
            with nc.Block() as block:
                if mod:
                    @block.sync
                    def _(sp):
                        mod.load(sp)

                @block.tensor
                def _(pe):
                    pe.wait_ge(stage_in.sem, stage_in.at(0))
                    for k in range(KC):
                        mm = nc.tensor.matmul(psum[0:64, 0, :], w_a[:, k, :], hT[:, k, :], start=(k == 0), stop=(k == KC - 1))
                    mm.then_inc(pe_done.sem, 1)
                    for i in range(4):
                        nc.tensor.matmul(psum[:, 6 + i // 2, (i % 2) * S:(i % 2) * S + S], swap, proj[:, T_Q + i, 0:S],
                                         start=True, stop=True).then_inc(pe_done.sem, 1)
                    pe.wait_ge(act_done.sem, act_done.at(1))
                    for z in range(2):
                        rows = slice(32 * z, 32 * z + GR)
                        for n in range(2):
                            mm = nc.tensor.matmul(psum[:, 2 + 2 * z + n, :], wa2[rows, n * P:n * P + P], a_t[rows, :],
                                                  start=True, stop=True)
                        mm.then_inc(pe_done.sem, 1)
                    pe_done.made += 7
                    for c in range(CT):
                        mm = nc.tensor.matmul(psum[:, 0, 0:nt], ones[:], conv[:, c, 0:nt], start=(c == 0), stop=(c == CT - 1))
                    mm.then_inc(norm_pe.sem, 1)
                    for c in range(CT):
                        pe.wait_ge(norm_act.sem, norm_act.at(c + 1))
                        mm = nc.tensor.matmul(psum[:, 1, 0:nt], ones[:], sq[:, c, 0:nt], start=(c == 0), stop=(c == CT - 1))
                    mm.then_inc(norm_pe.sem, 1)
                    norm_pe.made += 2
                    if mod:
                        pe.wait_ge(dve_done.sem, dve_done.at(12))
                        mod.products(pe, 0, 1)
                        mod.columns(pe, 0, 1)

                @block.scalar
                def _(act):
                    act.wait_ge(pe_done.sem, pe_done.at(1))
                    nc.scalar.copy(a_t[0:64, :], psum[0:64, 0, :]).then_inc(act_done.sem, 1)
                    act.wait_ge(pe_done.sem, pe_done.at(7))
                    for i in range(4):
                        nc.scalar.activation(decay[:, i, :], psum[:, 2 + i, :], ACT.Identity,
                                             bias=col(l, "ba", i)).then_inc(act_done.sem, 1)
                    for c in range(CT):
                        act.wait_ge(norm_dve.sem, norm_dve.at(1 + c + 1))
                        nc.scalar.activation(sq[:, c, 0:nt], conv[:, c, 0:nt], ACT.Square).then_inc(norm_act.sem, 1)
                    act.wait_ge(dve_done.sem, dve_done.at(12 + 1))
                    nc.scalar.activation(runsum, runsum, ACT.Exp, scale=-1.0).then_inc(act_done.sem, 1)
                    act.wait_ge(act_done.sem, act_done.at(6))
                    nc.scalar.activation(runsum, runsum, ACT.Ln, bias=1.0).then_inc(act_done.sem, 1)
                    act_done.made += 7
                    act.wait_ge(norm_pe.sem, norm_pe.at(2))
                    inverse_root(act, stat[:, 1, 0:nt], psum[:, 1, 0:nt], CONV, norm_act)
                    if mod:
                        mod.copy_rows(act, 0, 1)
                    for c in range(CT):
                        act.wait_ge(norm_dve.sem, norm_dve.at(1 + CT + c + 1))
                        nc.scalar.activation(conv[:, c, 0:nt], conv[:, c, 0:nt], ACT.Silu,
                                             bias=col(l, "ln_b", c)).then_inc(norm_act.sem, 1)
                    norm_act.made += CT + 1 + CT

                @block.vector
                def _(dve):
                    dve.wait_ge(pe_done.sem, pe_done.at(5))
                    dve.wait_ge(stage_in.sem, stage_in.at(0))
                    for i in range(4):
                        x = proj[:, T_Q + i, 0:S]
                        tmp = f_q[0][:, 0, 0:S]
                        dve_done.link(dve, nc.vector.tensor_tensor(tmp, psum[:, 6 + i // 2, (i % 2) * S:(i % 2) * S + S],
                                                                   rope[:, 1, :], ALU.mult))
                        dve_done.link(dve, nc.vector.tensor_tensor(x, x, rope[:, 0, :], ALU.mult))
                        dve_done.link(dve, nc.vector.tensor_tensor(x, x, tmp, ALU.add))
                    dve.wait_ge(norm_pe.sem, norm_pe.at(1))
                    nc.vector.tensor_scalar(stat[:, 0, 0:nt], psum[:, 0, 0:nt], 1.0 / CONV, None,
                                            ALU.mult).then_inc(norm_dve.sem, 1)
                    dve.wait_ge(norm_dve.sem, norm_dve.at(1))
                    for c in range(CT):
                        nc.vector.tensor_tensor(conv[:, c, 0:nt], conv[:, c, 0:nt], stat[:, 0, 0:nt],
                                                ALU.subtract).then_inc(norm_dve.sem, 1)
                    dve.wait_ge(act_done.sem, act_done.at(5))
                    dve_done.link(dve, nc.vector.scalar_tensor_tensor(out=runsum, in0=decay, scalar=-1.0, in1=decay,
                                                                      op0=ALU.mult, op1=ALU.max))
                    dve.wait_ge(act_done.sem, act_done.at(7))
                    dve_done.link(dve, nc.vector.scalar_tensor_tensor(out=decay, in0=decay, scalar=0.0, in1=runsum,
                                                                      op0=ALU.min, op1=ALU.subtract))
                    for i in range(4):
                        step = 1 if i < 2 else -1
                        dve_done.link(dve, nc.vector.tensor_tensor_scan(
                            runsum[:, i, ::step], resets, decay[:, i, ::step], 0.0, ALU.mult, ALU.add))
                    dve.wait_ge(norm_act.sem, norm_act.at(CT + 1))
                    for c in range(CT):
                        nc.vector.scalar_tensor_tensor(
                            out=conv[:, c, 0:nt], in0=conv[:, c, 0:nt], scalar=col(l, "ln_g", c), in1=stat[:, 1, 0:nt],
                            op0=ALU.mult, op1=ALU.mult).then_inc(norm_dve.sem, 1)
                    norm_dve.made += 1 + CT + CT
                    if mod:
                        mod.add_bias(dve, 0, 1)
            end_stage()

        def gla_scaled(l, nt, mod):
            mid, end = (CH // 2, CH // 2 - 1), (CH - 1, 0)
            b = [runsum[:, 2 * z:2 * z + 2, :] for z in range(2)]
            bc = [x.rearrange("p n (c i) -> p (n c) i", i=CH) for x in b]
            w = nt // P

            def chunks(x):
                return x.rearrange("p n (c i) -> p (n c) i", i=CH)
            with nc.Block() as block:
                @block.vector
                def _(dve):
                    n = [P, 2 * NCH, CH]
                    k = proj[:, T_K:T_K + 2, :]
                    q = proj[:, T_Q:T_Q + 2, 0:nt]
                    for z in range(2):
                        nc.vector.tensor_tensor(chunks(f_q[z]), bc[z], bc[z][:, :, mid[z]:mid[z] + 1].to_broadcast(n),
                                                ALU.subtract).then_inc(gla_dve[z].sem, 1)
                        nc.vector.tensor_tensor(chunks(f_ke[z]), bc[z][:, :, end[z]:end[z] + 1].to_broadcast(n), bc[z],
                                                ALU.subtract).then_inc(gla_dve[z].sem, 1)
                    for z in range(2):
                        dve.wait_ge(gla_act[z].sem, gla_act[z].at(2))
                        nc.vector.tensor_tensor(f_ke[z], f_ke[z], k, ALU.mult).then_inc(gla_dve[z].sem, 1)
                        nc.vector.tensor_tensor(f_k[z], f_k[z], k, ALU.mult).then_inc(gla_dve[z].sem, 1)
                        for j, f in ((3, f_q[z]), (4, f_qe[z])):
                            dve.wait_ge(gla_act[z].sem, gla_act[z].at(j))
                            nc.vector.scalar_tensor_tensor(out=f[:, :, 0:nt], in0=q, scalar=GDK ** -0.5, in1=f[:, :, 0:nt],
                                                           op0=ALU.mult, op1=ALU.mult).then_inc(gla_dve[z].sem, 1)
                        nc.vector.memset(state[z], 0.0).then_inc(gla_dve[z].sem, 1)
                    if mod:
                        mod.add_bias(dve, 1, 2)
                    for z in range(2):
                        for n in range(2):
                            dve.wait_ge(gla_pe[z].sem, gla_pe[z].at(n + 1))
                            nc.vector.tensor_copy(ke_tok[z][:, :, n * P:n * P + P],
                                                  psum[:, 4 * z + 2 + n, :].rearrange("p (t c) -> p t c", t=4)).then_inc(gla_dve[z].sem, 1)

                @block.scalar
                def _(act):
                    s = 1.0 / GATE_NORM
                    for z in range(2):
                        act.wait_ge(gla_dve[z].sem, gla_dve[z].at(2))
                        nc.scalar.activation(f_k[z], f_q[z], ACT.Exp, scale=-s).then_inc(gla_act[z].sem, 1)
                        nc.scalar.activation(f_ke[z], f_ke[z], ACT.Exp, scale=s).then_inc(gla_act[z].sem, 1)
                        act.wait_ge(gla_act[z].sem, gla_act[z].at(1))
                        nc.scalar.activation(f_q[z], f_q[z], ACT.Exp, scale=s).then_inc(gla_act[z].sem, 1)
                        nc.scalar.activation(f_qe[z], b[z], ACT.Exp, scale=s).then_inc(gla_act[z].sem, 1)
                        nc.scalar.activation(chunk_decay[z], bc[z][:, :, end[z]], ACT.Exp, scale=s).then_inc(gla_act[z].sem, 1)
                    if mod:
                        mod.copy_rows(act, 1, 2)
                    for z in range(2):
                        for i in range(2):
                            act.wait_ge(gla_pe[z].sem, gla_pe[z].at(3 + i))
                            nc.scalar.copy(attm[z][:, 0:w, i::2, :], psum[:, 4 * z + i, :].rearrange(
                                "p (t h i) -> p t h i", t=4, h=2)[:, 0:w]).then_inc(gla_act[z].sem, 1)

                @block.gpsimd
                def _(pool):
                    for z in range(2):
                        pool.wait_ge(gla_act[z].sem, gla_act[z].at(7))
                        for half in range(2):
                            m = attm[z][half * CH:half * CH + CH, 0:w, :, :].rearrange("p t h i -> p (t h) i")
                            sign = 1 if z == 0 else -1
                            nc.gpsimd.affine_select(out=m, in_=m, compare_op=ALU.is_ge, fill=0.0, base=0,
                                                    pattern=[[0, w * GH], [sign, CH]], channel_multiplier=-sign).then_inc(pool_done.sem, 1)
                    pool_done.made += 4

                @block.tensor
                def _(pe):
                    if mod:
                        mod.products(pe, 1, 2)
                    for z in range(2):
                        if mod and z == 1:
                            mod.columns(pe, 1, 2)
                            pe.wait_ge(dve_done.sem, dve_done.at(2))
                        pe.wait_ge(gla_dve[z].sem, gla_dve[z].at(3))
                        for n in range(2):
                            for tt in range(4):
                                mm = nc.tensor.transpose(psum[:, 4 * z + 2 + n, tt * P:tt * P + P],
                                                         f_ke[z][:, n, tt * P:tt * P + P], ident[:])
                            mm.then_inc(gla_pe[z].sem, 1)
                        pe.wait_ge(gla_dve[z].sem, gla_dve[z].at(5))
                        for i in range(2):
                            for c in range(nt // CH):
                                for n in range(2):
                                    rows = slice(i * GDK, i * GDK + GDK)
                                    at = ((c // 2) * 2 + n) * CH
                                    mm = nc.tensor.matmul(psum[(c % 2) * CH:(c % 2) * CH + CH, 4 * z + i, at:at + CH],
                                                          f_k[z][rows, n, c * CH:c * CH + CH], f_q[z][rows, n, c * CH:c * CH + CH],
                                                          start=True, stop=True)
                            mm.then_inc(gla_pe[z].sem, 1)
            for z in range(2):
                gla_dve[z].made += 9
                gla_act[z].made += 7
                gla_pe[z].made += 4
            if mod:
                mod.finish()
            end_stage()

        def gla_scan(l, nt, mod):
            order = ([4, 5, 6, 7, 0, 1, 2, 3], [7, 6, 5, 4, 3, 2, 1, 0])
            shown = [[c < nt // CH for c in o] for o in order]
            before = [[sum(4 * (j < NCH - 1) + x[j] for j in range(n)) for n in range(NCH + 1)] for x in shown]
            groups = [[sum((j < NCH - 1) + x[j] for j in range(n)) for n in range(NCH + 1)] for x in shown]

            def comes_first(z, n):
                return (n, z) < (order[1 - z].index(order[z][n]), 1 - z)
            with nc.Block() as block:
                @block.sync
                def _(sp):
                    if mod:
                        mod.load_round(sp, 0)
                    else:
                        first_blocks(sp, A["w_merge"][l])
                    na_tables(sp, l)

                @block.tensor
                def _(pe):
                    for n in range(NCH):
                        for z in range(2):
                            c = order[z][n]
                            tt, half = c // 2, slice((c % 2) * CH, (c % 2) * CH + CH)
                            if n >= 2:
                                pe.wait_ge(gla_dve[z].sem, gla_dve[z].at(before[z][n - 1]))
                            if n == NCH - 1:
                                continue
                            for h in range(GH):
                                rows = slice((h % 2) * GDK, (h % 2) * GDK + GDK)
                                mm = nc.tensor.matmul(psum[rows, 4 * z + 2 + n % 2, (h // 2) * P:(h // 2) * P + P],
                                                      ke_tok[z][half, tt, h * GDK:h * GDK + GDK], v_tok[half, tt, h * P:h * P + P],
                                                      start=True, stop=True)
                            mm.then_inc(gla_pe[z].sem, 1)
                        for z in range(2):
                            c = order[z][n]
                            tt, half = c // 2, slice((c % 2) * CH, (c % 2) * CH + CH)
                            if shown[z][n]:
                                if n > 0:
                                    pe.wait_ge(gla_dve[z].sem, gla_dve[z].at(before[z][n]))
                                else:
                                    pe.wait_ge(dve_done.sem, dve_done.at(1))
                                own = comes_first(z, n)
                                for h in range(GH):
                                    o = psum[:, 4 * z + n % 2, h * CH:h * CH + CH]
                                    if n > 0:
                                        mm = nc.tensor.matmul(o, state[z][:, h, :], f_qe[z][:, h // 2, c * CH:c * CH + CH],
                                                              start=True, stop=not own)
                                    if own:
                                        mm = nc.tensor.matmul(o, v_tok[half, tt, h * P:h * P + P], attm[0][half, tt, h, :],
                                                              start=(n == 0), stop=True)
                                mm.then_inc(gla_pe[z].sem, 1)

                @block.vector
                def _(dve):
                    w = nt // P
                    nc.vector.tensor_tensor(attm[0][:, 0:w], attm[0][:, 0:w], attm[1][:, 0:w], ALU.add).then_inc(dve_done.sem, 1)
                    dve_done.made += 1
                    for n in range(NCH):
                        for z in range(2):
                            c = order[z][n]
                            dve.wait_ge(gla_pe[z].sem, gla_pe[z].at(groups[z][n + 1]))
                            for h in range(GH if n < NCH - 1 else 0):
                                rows = slice((h % 2) * GDK, (h % 2) * GDK + GDK)
                                if n > 0 and h == 0:
                                    dve.wait_ge(gla_dve[z].sem, gla_dve[z].at(before[z][n]))
                                nc.vector.scalar_tensor_tensor(
                                    out=state[z][rows, h, :], in0=state[z][rows, h, :],
                                    scalar=chunk_decay[z][rows, (h // 2) * NCH + c:(h // 2) * NCH + c + 1],
                                    in1=psum[rows, 4 * z + 2 + n % 2, (h // 2) * P:(h // 2) * P + P],
                                    op0=ALU.mult, op1=ALU.add).then_inc(gla_dve[z].sem, 1)
                            if shown[z][n]:
                                o = o_t[:, :, c * CH:c * CH + CH]
                                p = psum[:, 4 * z + n % 2, 0:GH * CH].rearrange("p (h i) -> p h i", h=GH)
                                other = order[1 - z].index(c)
                                if comes_first(z, n):
                                    nc.vector.tensor_copy(o, p).then_inc(gla_dve[z].sem, 1)
                                else:
                                    dve.wait_ge(gla_dve[1 - z].sem, gla_dve[1 - z].at(before[1 - z][other + 1]))
                                    nc.vector.tensor_tensor(o, o, p, ALU.add).then_inc(gla_dve[z].sem, 1)
            for z in range(2):
                gla_dve[z].made += before[z][NCH]
                gla_pe[z].made += groups[z][NCH]
            end_stage()

        def gla_output(l, nt):
            g = proj[:, T_G:T_G + GH, 0:nt]
            o = o_t[:, :, 0:nt]
            osq = gla_sq[:, :, 0:nt]
            ors = gla_rs[:, :, 0:nt]
            with nc.Block() as block:
                @block.scalar
                def _(act):
                    nc.scalar.activation(osq, o, ACT.Square).then_inc(act_done.sem, 1)
                    nc.scalar.activation(g, g, ACT.Silu).then_inc(act_done.sem, 1)
                    act.wait_ge(pe_done.sem, pe_done.at(1))
                    inverse_root(act, ors, psum[:, 0:4, 0:nt], GDV, act_done)
                    act_done.made += 3

                @block.tensor
                def _(pe):
                    pe.wait_ge(act_done.sem, act_done.at(1))
                    for h in range(GH):
                        mm = nc.tensor.matmul(psum[:, h, 0:nt], ones[:], osq[:, h, :], start=True, stop=True)
                    mm.then_inc(pe_done.sem, 1)
                    pe_done.made += 1

                @block.vector
                def _(dve):
                    dve.wait_ge(act_done.sem, act_done.at(3))
                    dve_done.link(dve, nc.vector.tensor_tensor(ors, ors, g, ALU.mult))
                    for h in range(GH):
                        nc.vector.scalar_tensor_tensor(out=o[:, h, :], in0=o[:, h, :], scalar=col(l, "gla_g", h),
                                                       in1=ors[:, h, :], op0=ALU.mult, op1=ALU.mult).then_inc(dve_done.sem, 1)
                    dve_done.made += GH
            end_stage()

        def na_tables(sp, l):
            for row in range(4):
                half = slice((row % 2) * GRID_W, (row % 2) * GRID_W + GRID_W)
                for h in range(NH):
                    at = ((l * NH + h) * (2 * KH - 1) + KH - 1 - row) * RPW
                    rpb = bass.AP(tensor=A["rpb"].tensor, offset=at, ap=[[1, GRID_W], [RPW, 4], [1, GRID_W]])
                    to = na_bias[half, row // 2, h].rearrange("p (r c) -> p r c", c=GRID_W)
                    sp.dma_start(to, rpb).then_inc(stage_in.sem, 16)
            sp.dma_start(na_mask, A["na_mask"]).then_inc(stage_in.sem, 16)
            stage_in.made += 16 * (4 * NH + 1)

        def neighbourhood(l, nt, mod):
            units = [(qt, h) for qt in range(nt // P) for h in range(NH)]
            rows_of = [slice((h % 2) * NHD, (h % 2) * NHD + NHD) for h in range(NH)]
            n_units = len(units)
            with nc.Block() as block:
                if mod:
                    @block.sync
                    def _(sp):
                        mod.load_round(sp, 1)
                        sp.wait_ge(used.sem, used.at(2 * RING))
                        first_blocks(sp, A["w_merge"][l])

                def keys_of(qt):
                    return 0 if qt < 2 else S

                @block.tensor
                def _(pe):
                    def scores(u):
                        qt, h = units[u]
                        if u >= 3:
                            pe.wait_ge(na_exped.sem, na_exped.at(u - 3 + 1))
                        k0 = keys_of(qt)
                        nc.tensor.matmul(psum[:, u % 3, k0:NT], proj[rows_of[h], T_NQ + h // 2, qt * P:qt * P + P],
                                         proj[rows_of[h], T_NK + h // 2, k0:NT], start=True, stop=True).then_inc(na_scored.sem, 1)

                    def transposes(u):
                        qt, h = units[u]
                        pe.wait_ge(na_normed.sem, na_normed.at(u + 1))
                        if u >= 2:
                            pe.wait_ge(na_copied.sem, na_copied.at(u - 2 + 1))
                        for kt in range(keys_of(qt) // P, 4):
                            mm = nc.tensor.transpose(psum[:, 3 + u % 2, kt * P:kt * P + P], prob[:, u % 2, kt * P:kt * P + P], ident[:])
                        mm.then_inc(na_turned.sem, 1)

                    def values(u):
                        qt, h = units[u]
                        pe.wait_ge(na_copied.sem, na_copied.at(u + 1))
                        if u >= 2:
                            pe.wait_ge(na_out.sem, na_out.at(u - 2 + 1))
                        k0 = keys_of(qt) // P
                        for kt in range(k0, 4):
                            mm = nc.tensor.matmul(psum[rows_of[h], 5 + u % 2, 0:P], nv_tok[:, kt, h * NHD:h * NHD + NHD],
                                                  prob_t[:, u % 2, kt, :], start=(kt == k0), stop=(kt == 3))
                        mm.then_inc(na_valued.sem, 1)

                    scores(0)
                    scores(1)
                    for u in range(n_units):
                        if u + 2 < n_units:
                            scores(u + 2)
                        transposes(u)
                        if u:
                            values(u - 1)
                        if mod:
                            mod.one_product(pe, u)
                    values(n_units - 1)
                    if mod:
                        mod.columns(pe, 0, 2)

                @block.scalar
                def _(act):
                    def exp(u):
                        k0 = keys_of(units[u][0])
                        act.wait_ge(na_maxed.sem, na_maxed.at(u + 1))
                        if u >= 2:
                            act.wait_ge(na_turned.sem, na_turned.at(u - 2 + 1))
                        nc.scalar.activation(prob[:, u % 2, k0:NT], psum[:, u % 3, k0:NT], ACT.Exp,
                                             bias=na_stat[:, 0, u:u + 1], accum_out=na_stat[:, 1, u:u + 1]).then_inc(na_exped.sem, 1)

                    def copy_turned(u):
                        k0 = keys_of(units[u][0])
                        act.wait_ge(na_turned.sem, na_turned.at(u + 1))
                        if u >= 2:
                            act.wait_ge(na_valued.sem, na_valued.at(u - 2 + 1))
                        nc.scalar.copy(prob_t[:, u % 2, k0 // P:4, :],
                                       psum[:, 3 + u % 2, k0:NT].rearrange("p (k q) -> p k q", q=P)).then_inc(na_copied.sem, 1)

                    def copy_out(u):
                        qt, h = units[u]
                        act.wait_ge(na_valued.sem, na_valued.at(u + 1))
                        nc.scalar.copy(na_t[rows_of[h], h // 2, qt * P:qt * P + P],
                                       psum[rows_of[h], 5 + u % 2, 0:P]).then_inc(na_out.sem, 1)

                    exp(0)
                    for u in range(n_units):
                        if u + 1 < n_units:
                            exp(u + 1)
                        copy_turned(u)
                        if u:
                            copy_out(u - 1)
                        if mod and u % 8 == 7:
                            mod.copy_half(act, u // 8)
                    copy_out(n_units - 1)

                @block.vector
                def _(dve):
                    def step(n):
                        a, b = n + 1 < n_units, n >= 0
                        u = n + 1
                        if a:
                            qt, h = units[u]
                            dve.wait_ge(na_scored.sem, na_scored.at(u + 1))
                            if keys_of(qt) == 0:
                                s = psum[:, u % 3, 0:S].rearrange("p (r c) -> p r c", c=GRID_W)
                                nc.vector.tensor_tensor(s, s, na_bias[:, qt, h, :].rearrange("p (r c) -> p r c", c=GRID_W)[:, :, ::-1],
                                                        ALU.add).then_inc(na_biased.sem, 1)
                                na_biased.made += 1
                        if b:
                            dve.wait_ge(na_exped.sem, na_exped.at(n + 1))
                            nc.vector.reciprocal(na_stat[:, 3, n:n + 1], na_stat[:, 1, n:n + 1]).then_inc(na_inverted.sem, 1)
                        if a:
                            dve.wait_ge(na_biased.sem, na_biased.at(na_biased.made))
                            nc.vector.tensor_reduce(na_stat[:, 0, u:u + 1], psum[:, u % 3, keys_of(qt):NT], AX.X, ALU.max,
                                                    negate=True).then_inc(na_maxed.sem, 1)
                        if b:
                            s = prob[:, n % 2, keys_of(units[n][0]):NT]
                            dve.wait_ge(na_inverted.sem, na_inverted.at(n + 1))
                            nc.vector.tensor_scalar(s, s, na_stat[:, 3, n:n + 1], None, ALU.mult).then_inc(na_normed.sem, 1)

                    dve.wait_ge(stage_in.sem, stage_in.at(0))
                    biasv = na_bias.rearrange("p r h (k c) -> p (r h k) c", c=GRID_W)
                    dve_done.link(dve, nc.vector.tensor_tensor(
                        biasv, biasv, na_mask.unsqueeze(1).to_broadcast([P, 2 * NH * 4, GRID_W]), ALU.add))
                    for n in range(-1, n_units):
                        step(n)
                    if mod:
                        mod.add_bias(dve, 0, 2)
            na_inverted.made += n_units
            for c in (na_scored, na_maxed, na_exped, na_normed, na_turned, na_copied, na_valued, na_out):
                c.made += n_units
            if mod:
                half_made.made += 2
                mod.finish()
            end_stage()

        def merge(l, nt):
            branch = (conv, o_t, na_t)
            n_blocks = 5 * KC
            split_x = KC + 12

            def product_taken(p):
                return split_x + 5 * (p // 3) + (1, 2, 4)[p % 3]

            chunks = [(mh_hi, mh_lo, hT, k) for k in range(KC)] + [(br_hi[j], br_lo[j], branch[j], k) for j in range(3) for k in range(4)]
            with nc.Block() as block:
                @block.sync
                def _(sp):
                    load_blocks(sp, A["w_merge"][l], n_blocks)
                    first_blocks(sp, A["w_out"][l], after=n_blocks)

                @block.tensor
                def _(pe):
                    for d in range(KC):
                        for j in range(3):
                            n = 5 * d + j
                            p = 3 * d + j
                            pe.wait_ge(lo_made.sem, lo_made.at(n + 1))
                            if p >= 4:
                                pe.wait_ge(act_done.sem, act_done.at(split_x + p - 3))
                            for k in range(KC):
                                if n == 0:
                                    pe.wait_ge(dve_done.sem, dve_done.at(k + 1))
                                mm = three(psum[:, p % 4, 0:nt], halves(n, k), (mh_hi[:, k, 0:nt], mh_lo[:, k, 0:nt]),
                                           k == 0, k == KC - 1)
                            mm.then_inc(split_used.sem, 1)
                        for j in range(3):
                            n = 5 * d + 3 + j // 2
                            p = 3 * d + j
                            pe.wait_ge(lo_made.sem, lo_made.at(n + 1))
                            pe.wait_ge(dve_done.sem, dve_done.at(split_x if p < 4 else product_taken(p - 4)))
                            for k in range(4):
                                mm = three(psum[:, 4 + p % 4, 0:nt], halves(n, 4 * (j % 2) + k),
                                           (br_hi[j][:, k, 0:nt], br_lo[j][:, k, 0:nt]), k == 0, k == 3)
                            if j != 0:
                                mm.then_inc(split_used.sem, 1)

                @block.scalar
                def _(act):
                    for n in range(SPLIT):
                        hi(act, n)
                    for xh, _, x, k in chunks:
                        nc.scalar.copy(xh[:, k, 0:nt], x[:, k, 0:nt]).then_inc(act_done.sem, 1)
                    for n in range(n_blocks):
                        d, j = n // 5, n % 5
                        if j < 3:
                            p = 3 * d + j
                            act.wait_ge(split_used.sem, split_used.at(n + 1))
                            if p >= 4:
                                act.wait_ge(dve_done.sem, dve_done.at(product_taken(p - 4)))
                            nc.scalar.activation(gate_s[:, p % 4, 0:nt], psum[:, p % 4, 0:nt], ACT.Sigmoid,
                                                 bias=col(l, "b_gate", j * KC + d)).then_inc(act_done.sem, 1)
                        if n + SPLIT < n_blocks:
                            hi(act, n + SPLIT)
                    act_done.made += split_x + 3 * KC

                @block.vector
                def _(dve):
                    for n in range(SPLIT):
                        lo(dve, n)
                    for m, (xh, xl, x, k) in enumerate(chunks):
                        dve.wait_ge(act_done.sem, act_done.at(m + 1))
                        nc.vector.tensor_tensor(xl[:, k, 0:nt], x[:, k, 0:nt], xh[:, k, 0:nt].bitcast(F32),
                                                ALU.subtract).then_inc(dve_done.sem, 1)
                    dve_done.made += split_x
                    for n in range(n_blocks):
                        if n + SPLIT < n_blocks:
                            lo(dve, n + SPLIT)
                        d = n // 5
                        for j in {3: (0, 1), 4: (2,)}.get(n % 5, ()):
                            p = 3 * d + j
                            m = merged[:, d, 0:nt]
                            dve.wait_ge(act_done.sem, act_done.at(split_x + p + 1))
                            dve.wait_ge(split_used.sem, split_used.at(n + 1))
                            to = m if j == 0 else branch_m[:, j - 1, 0:nt]
                            dve_done.link(dve, nc.vector.tensor_tensor(to, psum[:, 4 + p % 4, 0:nt], gate_s[:, p % 4, 0:nt], ALU.mult))
                            if j:
                                dve_done.link(dve, nc.vector.tensor_tensor(m, m, to, ALU.add))
            end_stream(n_blocks)

        def add_residual(l, g, d, s, p):
            x = xT[:, d, s * S:s * S + S]
            return nc.vector.scalar_tensor_tensor(out=x, in0=p, scalar=mods[:, l, g + d, s:s + 1], in1=x, op0=ALU.mult, op1=ALU.add)

        def mixer_output(l, nt):
            with nc.Block() as block:
                @block.sync
                def _(sp):
                    load_blocks(sp, A["w_out"][l], KC)
                    first_blocks(sp, A["w_query"][l], after=KC)

                @block.tensor
                def _(pe):
                    for d in range(KC):
                        pe.wait_ge(lo_made.sem, lo_made.at(d + 1))
                        for k in range(KC):
                            if d == 0:
                                pe.wait_ge(dve_done.sem, dve_done.at(k + 1))
                            mm = three(psum[:, d, 0:nt], halves(d, k), (mg_hi[:, k, 0:nt], mg_lo[:, k, 0:nt]), k == 0, k == KC - 1)
                        mm.then_inc(split_used.sem, 1)

                @block.scalar
                def _(act):
                    hi(act, 0)
                    for k in range(KC):
                        nc.scalar.copy(mg_hi[:, k, 0:nt], merged[:, k, 0:nt]).then_inc(act_done.sem, 1)
                    act_done.made += KC
                    for n in range(1, KC):
                        hi(act, n)

                @block.vector
                def _(dve):
                    lo(dve, 0)
                    for k in range(KC):
                        dve.wait_ge(act_done.sem, act_done.at(k + 1))
                        nc.vector.tensor_tensor(mg_lo[:, k, 0:nt], merged[:, k, 0:nt], mg_hi[:, k, 0:nt].bitcast(F32),
                                                ALU.subtract).then_inc(dve_done.sem, 1)
                    dve_done.made += KC
                    for n in range(1, KC):
                        lo(dve, n)
                    for d in range(KC):
                        dve.wait_ge(split_used.sem, split_used.at(d + 1))
                        for s in range(nt // S):
                            add_residual(l, 16, d, s, psum[:, d, s * S:s * S + S])
            end_stream(KC)

        def top16(dve, rows):
            start = dve_done.made
            for step in range(5):
                for j, (val, big, place) in enumerate(rows):
                    if step:
                        dve.wait_ge(dve_done.sem, dve_done.at(start + (step - 1) * len(rows) + j + 1))
                    if step == 0:
                        ins = nc.vector.max(big[:, 0:8], val)
                    elif step == 1:
                        ins = nc.vector.max_index(place[:, 0:8], big[:, 0:8], val)
                    elif step == 2:
                        ins = nc.vector.match_replace(val, big[:, 0:8], val, NEG)
                    elif step == 3:
                        ins = nc.vector.max(big[:, 8:16], val)
                    else:
                        ins = nc.vector.max_index(place[:, 8:16], big[:, 8:16], val)
                    ins.then_inc(dve_done.sem, 1)
            dve_done.made += 5 * len(rows)
            dve.wait_ge(dve_done.sem, dve_done.at(dve_done.made))

        def peer_choice(l, ada, prefetched, modulate=None):
            n_blocks = 2 * PH

            mod = Modulation(*modulate, 6) if modulate else None
            with nc.Block() as block:
                @block.sync
                def _(sp):
                    sp.dma_start(keys, A["keys"][l]).then_inc(stage_in.sem, 16)
                    stage_in.made += 16
                    if not prefetched:
                        first_blocks(sp, A["w_query"][l])
                    load_blocks(sp, A["w_query"][l], n_blocks)
                    if mod:
                        sp.wait_ge(split_used.sem, split_used.at(n_blocks))
                        mod.load(sp)

                @block.tensor
                def _(pe):
                    def scores(h):
                        pe.wait_ge(query_out.sem, query_out.at(2 * h + 2))
                        if h >= 2:
                            pe.wait_ge(score_out.sem, score_out.at(h - 2 + 1))
                        for tt in range(2):
                            for z in range(2):
                                at = (2 * tt + z) * P
                                mm = nc.tensor.matmul(psum[:, 4 + h % 2, at:at + P], qry[:, 2 * h + z, tt * P:tt * P + P],
                                                      keys[:, 2 * h + z, :], start=True, stop=True)
                        mm.then_inc(score_made.sem, 1)

                    ada.mean(pe)
                    for n in range(n_blocks):
                        pe.wait_ge(lo_made.sem, lo_made.at(n + 1))
                        if n >= 4:
                            pe.wait_ge(query_out.sem, query_out.at(n - 4 + 1))
                        for k in range(KC):
                            if n == 0:
                                pe.wait_ge(ada_lo.sem, ada_lo.at(k + 1))
                            mm = three(psum[:, n % 4, 0:S], halves(n, k), (h_hi[:, k, :], h_lo[:, k, :]), k == 0, k == KC - 1)
                        mm.then_inc(split_used.sem, 1)
                        if n == 1:
                            pe.wait_ge(stage_in.sem, stage_in.at(16))
                            scores(0)
                        if n % 2 == 0 and n > 2:
                            scores(n // 2 - 1)
                    scores(PH - 1)
                    if mod:
                        mod.products(pe, 0, mod.rounds)
                        mod.columns(pe, 0, mod.rounds)
                    for n in range(3):
                        pe.wait_ge(picks_made.sem, picks_made.at(1 + n // 2))
                        for tt in range(2):
                            mm = nc.tensor.transpose(psum[:, n, tt * P:tt * P + P], picked[:, n, tt, :], ident[:])
                        mm.then_inc(pe_done.sem, 1)
                    pe_done.made += 3

                @block.gpsimd
                def _(pool):
                    for n in range(n_blocks):
                        lo(pool, n)

                @block.scalar
                def _(act):
                    def copy_scores(h):
                        act.wait_ge(score_made.sem, score_made.at(h + 1))
                        nc.scalar.copy(score[:, :, 2 * h:2 * h + 2, :], psum[:, 4 + h % 2, :].rearrange(
                            "p (t z k) -> p t z k", t=2, z=2)).then_inc(score_out.sem, 1)

                    ada.squares(act)
                    for n in range(SPLIT):
                        hi(act, n)
                    ada.shift(act)
                    for n in range(n_blocks):
                        act.wait_ge(split_used.sem, split_used.at(n + 1))
                        nc.scalar.copy(qry[:, n, :], psum[:, n % 4, 0:S]).then_inc(query_out.sem, 1)
                        if n + SPLIT < n_blocks:
                            hi(act, n + SPLIT)
                        if n == 1 or (n % 2 == 0 and n > 2):
                            copy_scores(n // 2 - 1 if n > 2 else 0)
                    copy_scores(PH - 1)
                    if mod:
                        mod.copy_rows(act, 0, mod.rounds)
                    act.wait_ge(picks_made.sem, picks_made.at(1))
                    g = picked[:, 2]
                    act_done.link(act, nc.scalar.activation(g, g, ACT.Exp))

                @block.vector
                def _(dve):
                    ada.factors(dve)
                    ada.scale(dve)
                    full = [P, PH, PK, PK]
                    for h in range(PH + 1):
                        rows = []
                        if h < PH:
                            dve.wait_ge(score_out.sem, score_out.at(h + 1))
                            rows += [(score[:, tt, 2 * h + z, :], top_s[:, tt, h, z, :], top_iu[:, tt, h, z, :])
                                     for tt in range(2) for z in range(2)]
                        if h:
                            pairs = [P, 2, PK, PK]
                            dve_done.link(dve, nc.vector.tensor_tensor(
                                cand[:, :, h - 1].rearrange("p t (a b) -> p t a b", a=PK),
                                top_s[:, :, h - 1, 0, :].unsqueeze(3).to_broadcast(pairs),
                                top_s[:, :, h - 1, 1, :].unsqueeze(2).to_broadcast(pairs), ALU.add))
                            rows += [(cand[:, tt, h - 1, :], best_s[:, tt, h - 1, :], best_ju[:, tt, h - 1, :]) for tt in range(2)]
                        top16(dve, rows)
                    dve_done.link(dve, nc.vector.tensor_copy(carve(11264, 512), top_i.bitcast(U32)))
                    flat = best_j.bitcast(U32)
                    dve_done.link(dve, nc.vector.tensor_scalar(best_abu[:, 0, :], flat, 4, None, ALU.logical_shift_right))
                    dve_done.link(dve, nc.vector.tensor_scalar(best_abu[:, 1, :], flat, PK - 1, None, ALU.bitwise_and))
                    dve_done.link(dve, nc.vector.tensor_copy(carve(16896, 512), best_ab.bitcast(U32)))
                    for tt in range(2):
                        for z in range(2):
                            dve_done.link(dve, nc.vector.tensor_tensor(
                                hot, best_abf[:, z, tt].unsqueeze(3).to_broadcast(full),
                                iota[:, 0:PK].unsqueeze(1).unsqueeze(1).to_broadcast(full), ALU.is_equal))
                            dve_done.link(dve, nc.vector.tensor_tensor(
                                hot, hot, top_f[:, tt, :, z, :].unsqueeze(2).to_broadcast(full), ALU.mult))
                            dve_done.link(dve, nc.vector.tensor_reduce(
                                picked[:, z, tt, :].rearrange("p (h k) -> p h k", h=PH), hot, AX.X, ALU.add))
                    for tt in range(2):
                        g = picked[:, 2, tt, :].rearrange("p (h k) -> p h k", h=PH)
                        dve_done.link(dve, nc.vector.tensor_tensor(
                            g, best_s[:, tt], best_s[:, tt, :, 0:1].to_broadcast([P, PH, PK]), ALU.subtract))
                    dve.sem_inc(picks_made.sem, 1)
                    dve.wait_ge(act_done.sem, act_done.at(1))
                    dve_done.link(dve, nc.vector.tensor_reduce(
                        gsum[:, 0, :], picked[:, 2].rearrange("p t (h k) -> p (t h) k", h=PH), AX.X, ALU.add))
                    dve_done.link(dve, nc.vector.reciprocal(gsum[:, 1, :], gsum[:, 0, :]))
                    g = picked[:, 2].rearrange("p t (h k) -> p (t h) k", h=PH)
                    dve_done.link(dve, nc.vector.tensor_tensor(
                        g, g, gsum[:, 1, :].unsqueeze(2).to_broadcast([P, 2 * PH, PK]), ALU.mult))
                    dve.sem_inc(picks_made.sem, 1)
                    if mod:
                        mod.add_bias(dve, 0, mod.rounds)
                    for n in range(3):
                        dve.wait_ge(pe_done.sem, pe_done.at(n + 1))
                        nc.vector.tensor_copy(sel_t[:, n, :], psum[:, n, 0:S])
            if mod:
                mod.finish()
            ada.finish()
            query_out.made += n_blocks
            score_made.made += PH
            score_out.made += PH
            picks_made.made += 2
            end_stream(n_blocks)

        def peer_gates(l):
            rounds = S // 4 // ONEHOTS
            made = [sum(4 + n % 2 for n in range(b)) for b in range(ONEHOTS + 1)]
            with nc.Block() as block:
                @block.sync
                def _(sp):
                    first_blocks(sp, A["w_expert"][l])

                @block.vector
                def _(dve):
                    def step(r, b, first=False):
                        if not first:
                            dve.wait_ge(gates_made.sem, r * ONEHOTS + gates_made.at(b - ONEHOTS + 1))
                        t = r * 4 * ONEHOTS + 4 * b
                        four = [P, 4, P]
                        if b % 2:
                            nc.vector.tensor_tensor(onehot[:, b, 1], iota[:].unsqueeze(1).to_broadcast(four),
                                                    sel_t[:, 1, bass.ds(t, 4)].unsqueeze(2).to_broadcast(four),
                                                    ALU.is_equal).then_inc(onehots_made.sem, 1)
                        for j in range(4):
                            nc.vector.tensor_scalar(onehot[:, b, 0, j, :], iota[:], sel_t[:, 0, bass.ds(t + j, 1)],
                                                    sel_t[:, 2, bass.ds(t + j, 1)], ALU.is_equal, ALU.mult).then_inc(onehots_made.sem, 1)

                    for b in range(ONEHOTS):
                        step(0, b, first=True)
                    with dve.Fori(1, rounds) as r:
                        for b in range(ONEHOTS):
                            step(r, b)
                    onehots_made.made += rounds * made[ONEHOTS]

                @block.tensor
                def _(pe):
                    def step(r, b, first=False):
                        if not first:
                            pe.wait_ge(gates_out.sem, r * ONEHOTS + gates_out.at(b - ONEHOTS + 1))
                        pe.wait_ge(onehots_made.sem, r * made[ONEHOTS] + onehots_made.at(made[b + 1]))
                        if b % 2 == 0:
                            pe.wait_ge(columns_made.sem, r * (ONEHOTS // 2) + columns_made.at(b // 2 + 1))
                        for j in range(4):
                            mm = nc.tensor.matmul(psum[:, b, j * P:j * P + P], onehot[:, b, 1, j, :], onehot[:, b, 0, j, :],
                                                  start=True, stop=True)
                        mm.then_inc(gates_made.sem, 1)

                    for b in range(ONEHOTS):
                        step(0, b, first=True)
                    with pe.Fori(1, rounds) as r:
                        for b in range(ONEHOTS):
                            step(r, b)
                    gates_made.made += S // 4

                @block.scalar
                def _(act):
                    def columns(r, b, first=False):
                        if not first:
                            act.wait_ge(gates_made.sem, r * ONEHOTS + gates_made.at(b - ONEHOTS + 1))
                        for j in range(4):
                            nc.scalar.activation(onehot[:, b, 1, j, :], iota[:], ACT.Abs, scale=-1.0,
                                                 bias=sel_t[:, 1, bass.ds(r * 4 * ONEHOTS + 4 * b + j, 1)]).then_inc(distance_made.sem, 1)
                        act.wait_ge(distance_made.sem, r * 2 * ONEHOTS + distance_made.at(2 * b + 4))
                        nc.scalar.activation(onehot[:, b, 1], onehot[:, b, 1], ACT.Relu, scale=-1.0, bias=1.0).then_inc(columns_made.sem, 1)

                    def evacuate(r, b):
                        act.wait_ge(gates_made.sem, r * ONEHOTS + gates_made.at(b + 1))
                        nc.scalar.copy(gates[:, :, bass.ds(r * 4 * ONEHOTS + 4 * b, 4)],
                                       psum[:, b % ONEHOTS, :].rearrange("p (j i) -> p i j", j=4)).then_inc(gates_out.sem, 1)

                    for b in range(ONEHOTS):
                        if b % 2 == 0:
                            columns(0, b, first=True)
                        if b >= 2:
                            evacuate(0, b - 2)
                    with act.Fori(1, rounds) as r:
                        for b in range(ONEHOTS):
                            if b % 2 == 0:
                                columns(r, b)
                            evacuate(r, b - 2)
                    for b in range(2):
                        evacuate(rounds, b - 2)
                    columns_made.made += rounds * (ONEHOTS // 2)
                    distance_made.made += rounds * 2 * ONEHOTS
                    gates_out.made += S // 4
            end_stage()

        def peer_experts(l, s):
            rounds = (ET - 2) // SPLIT
            n_blocks = 2 * ET

            def place_u(r, b):
                if isinstance(r, int):
                    i = SPLIT * r + b
                    return 0, (i if i < 2 else 2 * i - 2)
                return r * 2 * SPLIT, 2 * b - 2

            def place_v(r, b):
                if isinstance(r, int):
                    i = SPLIT * r + b
                    return 0, (2 * i + 3 if i <= ET - 3 else i + ET)
                return r * 2 * SPLIT, 2 * b + 3

            def acc(d):
                return psum[:, 4 + d // 2, (d % 2) * S:(d % 2) * S + S]

            def every_tile(eng, one):
                for b in range(SPLIT):
                    one(0, b)
                with eng.Fori(1, rounds) as r:
                    for b in range(SPLIT):
                        one(r, b)
                for b in range(2):
                    one(rounds, b)

            def tile_at(r, b):
                return r * SPLIT + b if isinstance(r, int) else None

            with nc.Block() as block:
                @block.sync
                def _(sp):
                    load_blocks(sp, A["w_expert"][l], n_blocks)

                @block.tensor
                def _(pe):
                    def up(r, b):
                        i = tile_at(r, b)
                        r6, c = place_u(r, b)
                        pe.wait_ge(lo_made.sem, r6 + lo_made.at(c + 1))
                        if i is None or i >= SPLIT:
                            pe.wait_ge(act_lo_made.sem, r * SPLIT + act_lo_made.at(b - SPLIT + 1))
                        for k in range(KC):
                            mm = three(psum[:, b % SPLIT, 0:S], halves(c, k), (h_hi[:, k, :], h_lo[:, k, :]), k == 0, k == KC - 1)
                        mm.then_inc(split_used.sem, 1)

                    def down(r, b, first=False, last=False):
                        r6, c = place_v(r, b)
                        pe.wait_ge(lo_made.sem, r6 + lo_made.at(c + 1))
                        pe.wait_ge(act_lo_made.sem, r * SPLIT + act_lo_made.at(b + 1))
                        for d in range(KC):
                            mm = three(acc(d), halves(c, d), (act_hi[:, b % SPLIT, :], act_lo[:, b % SPLIT, :]),
                                       first and d % 2 == 0, last)
                        mm.then_inc(split_used.sem, 1)

                    def one(r, b):
                        up(r, b)
                        i = tile_at(r, b)
                        if i is None or i >= 2:
                            down(r, b - 2, first=(i == 2))

                    every_tile(pe, one)
                    down(rounds, 0)
                    down(rounds, 1, last=True)

                @block.scalar
                def _(act):
                    def hi(r, place):
                        r6, c = place
                        slot = c % SPLIT
                        ahead = c // SPLIT if isinstance(r6, int) else r * 2 + c // SPLIT
                        act.wait_ge(raw_landed[slot], (ahead + (raw_loads[slot] + 1)) * 16)
                        if not isinstance(r6, int) or c >= SPLIT:
                            act.wait_ge(split_used.sem, r6 + split_used.at(c - SPLIT + 1))
                        nc.scalar.copy(w_hi[slot][:], raw[slot]).then_inc(hi_made.sem, 1)

                    def one(r, b):
                        i = tile_at(r, b)
                        if i is None or i + 1 < ET:
                            hi(r, place_u(r, b + 1))
                        r6, c = place_u(r, b)
                        act.wait_ge(split_used.sem, r6 + split_used.at(c + 1))
                        nc.scalar.activation(psum[:, b, 0:S], psum[:, b, 0:S], ACT.Gelu).then_inc(gelu_made.sem, 1)
                        if i is None or i >= 1:
                            hi(r, place_v(r, b - 1))
                        act.wait_ge(gated_made.sem, r * SPLIT + gated_made.at(b + 1))
                        if i is None or i >= SPLIT:
                            r6, c = place_v(r, b - SPLIT)
                            act.wait_ge(split_used.sem, r6 + split_used.at(c + 1))
                        nc.scalar.copy(act_hi[:, b, :], psum[:, b, 0:S]).then_inc(act_hi_made.sem, 1)

                    hi(0, place_u(0, 0))
                    every_tile(act, one)
                    hi(rounds, place_v(rounds, 1))
                    gelu_made.made += ET
                    act_hi_made.made += ET

                @block.vector
                def _(dve):
                    def lo(r, place):
                        r6, c = place
                        slot = c % SPLIT
                        dve.wait_ge(hi_made.sem, r6 + hi_made.at(c + 1))
                        nc.vector.tensor_tensor(w_lo[slot][:], raw[slot], w_hi[slot][:].bitcast(F32),
                                                ALU.subtract).then_inc(lo_made.sem, 1)

                    def one(r, b):
                        i = tile_at(r, b)
                        if i is None or i + 1 < ET:
                            lo(r, place_u(r, b + 1))
                        dve.wait_ge(gelu_made.sem, r * SPLIT + gelu_made.at(b + 1))
                        nc.vector.tensor_tensor(psum[:, b, 0:S], psum[:, b, 0:S], gates[:, r * SPLIT + b, :],
                                                ALU.mult).then_inc(gated_made.sem, 1)
                        if i is None or i >= 1:
                            lo(r, place_v(r, b - 1))
                        dve.wait_ge(act_hi_made.sem, r * SPLIT + act_hi_made.at(b + 1))
                        nc.vector.tensor_tensor(act_lo[:, b, :], psum[:, b, 0:S], act_hi[:, b, :].bitcast(F32),
                                                ALU.subtract).then_inc(act_lo_made.sem, 1)

                    lo(0, place_u(0, 0))
                    every_tile(dve, one)
                    lo(rounds, place_v(rounds, 1))
                    gated_made.made += ET
                    act_lo_made.made += ET
                    dve.wait_ge(split_used.sem, split_used.at(n_blocks))
                    for d in range(KC):
                        add_residual(l, 40, d, s, acc(d))
            end_stream(n_blocks)

        def final_norm():
            g0 = PARAMS["final"][0]
            with nc.Block() as block:
                @block.scalar
                def _(act):
                    for k in range(KC):
                        nc.scalar.activation(nsq[:, k, 0:S], xT[:, k, 0:S], ACT.Square).then_inc(act_done.sem, 1)
                    act.wait_ge(pe_done.sem, pe_done.at(1))
                    inverse_root(act, nrs[:, 0:S], psum[:, 0, 0:S], D, act_done)
                    act_done.made += KC + 1

                @block.tensor
                def _(pe):
                    for k in range(KC):
                        pe.wait_ge(act_done.sem, act_done.at(k + 1))
                        mm = nc.tensor.matmul(psum[:, 0, 0:S], ones[:], nsq[:, k, 0:S], start=(k == 0), stop=(k == KC - 1))
                    mm.then_inc(pe_done.sem, 1)
                    pe_done.made += 1

                @block.vector
                def _(dve):
                    dve.wait_ge(act_done.sem, act_done.at(KC + 1))
                    for k in range(KC):
                        nc.vector.scalar_tensor_tensor(out=hT[:, k, 0:S], in0=xT[:, k, 0:S], scalar=par[:, 0, g0 + k:g0 + k + 1],
                                                       in1=nrs[:, 0:S], op0=ALU.mult, op1=ALU.mult).then_inc(dve_done.sem, 1)
                    dve_done.made += KC

                @block.sync
                def _(sp):
                    sp.wait_ge(dve_done.sem, dve_done.at(KC))
                    sp.dma_start(out, hT[:, :, 0:S]).then_inc(out_done.sem, 16)
                    sp.wait_ge(out_done.sem, out_done.at(16))
                    out_done.made += 16
            end_stage()

        def dump(name, ap):
            if debug and name in debug:
                with nc.Block() as block:
                    @block.sync
                    def _(sp):
                        sp.dma_start(debug[name], ap).then_inc(out_done.sem, 16)
                        sp.wait_ge(out_done.sem, out_done.at(16))
                        out_done.made += 16
                end_stage()

        start()
        modulation(0, 0, 2)
        for l in range(DEPTH):
            nt = NT if l == 0 else S
            projection_and_conv(l, nt, AdaLN(l, 0, (0, 1), hT, ph_hi, ph_lo))
            if l == 0:
                dump("h", hT[:])
            if l == 0:
                dump("proj", proj)
            mod = Modulation(0, 2, 4, 6, MOD_ROWS) if l == 0 else None
            gla_features(l, nt, mod)
            gla_scaled(l, nt, mod)
            mod = Modulation(0, 4, 6, 7, work + 7168) if l == 0 else None
            gla_scan(l, nt, mod)
            gla_output(l, nt)
            neighbourhood(l, nt, mod)
            if l == 0:
                dump("conv", conv)
                dump("gla", o_t)
                dump("na", na_t)
            merge(l, nt)
            mixer_output(l, nt)
            if l == 0:
                dump("x1", xT[:])
            for s in range(nt // S):
                peer_choice(l, AdaLN(l, 1, (s,), h_one, h_hi, h_lo), s == 0, (l + 1, 3 * s, 3 * s + 3) if l + 1 < DEPTH else None)
                if l == 0 and s == 0:
                    dump("sel", sel_t[:])
                peer_gates(l)
                peer_experts(l, s)
            if l == 0:
                dump("x2", xT[:])
        final_norm()


def lay_out(i):
    f = {k: np.asarray(v) for k, v in i.items()}

    def chunks(v):
        return np.moveaxis(v.reshape(*v.shape[:-1], -1, P), -1, -2)

    def blocks_of(w):
        L, K, N = w.shape
        return w.reshape(L, K // P, P, N // P, P).transpose(0, 3, 2, 1, 4)

    a = {}
    x = np.concatenate([f["x"][0], f["ctx"][0]], 0)
    a["x"] = x.T.reshape(KC, P, NT).transpose(1, 0, 2)
    a["cond"] = np.stack([f["c"][0], f["c_ctx"]], -1).reshape(KC, P, 2).transpose(1, 0, 2)
    L = DEPTH
    cw = f["conv_w"].reshape(L, TAPS * CT, P)
    parts = [chunks(f["b_mod"]), chunks(f["norm1_g"]), chunks(f["norm2_g"]), chunks(f["b_gate"]), cw.transpose(0, 2, 1),
             chunks(f["conv_b"]), chunks(f["conv_ln_g"]), chunks(f["conv_ln_b"]), chunks(f["gla_ba"].reshape(L, -1)),
             chunks(f["gla_norm_g"]), np.broadcast_to(chunks(f["final_g"])[None], (L, P, KC))]
    a["params"] = np.concatenate(parts, -1).transpose(1, 0, 2)
    a["ident"] = np.eye(P, dtype=np.float32)
    a["iota"] = np.broadcast_to(np.arange(P, dtype=np.float32), (P, P))

    def flat(b):
        return b.reshape(b.shape[0], b.shape[1], P, D)

    a["w_mod"] = f["w_mod"].reshape(L, KC, P, 6, D).transpose(0, 3, 1, 2, 4).reshape(L, 48, P, D)
    at = np.cumsum([0, 1024, 256, 256, 512, 512, 32, 512, 512, 512, 3072]).tolist()
    glu, q, k, v, g, wa, nq, nk, nv, br = (f["w_in"][:, :, at[n]:at[n + 1]] for n in range(10))

    def rows_of(w):
        return w.reshape(L, 4, 2, P, 512).transpose(0, 1, 3, 2, 4).reshape(L, 4, P, D)

    a["w_proj"] = np.concatenate([flat(blocks_of(glu)), rows_of(v), rows_of(nv),
                                  flat(blocks_of(np.concatenate([g, nq, q, k, nk], -1)))], 1)
    a["w_a"] = np.pad(wa.reshape(L, KC, P, 2, GR), ((0, 0), (0, 0), (0, 0), (0, 0), (0, 32 - GR))).reshape(L, KC, P, 64).transpose(0, 2, 1, 3)
    a["wa2"] = f["gla_wa2"]
    gates = blocks_of(br).reshape(L, 3, KC, P, KC, P).transpose(0, 2, 1, 3, 4, 5)
    oc, og, on = (blocks_of(f[n])[:, :, None] for n in ("w_conv_o", "w_gla_o", "w_na_o"))
    pair = np.concatenate([oc, og], 4)
    alone = np.concatenate([on, np.zeros_like(on)], 4)
    a["w_merge"] = np.concatenate([gates, pair, alone], 2).reshape(L, 5 * KC, P, D)
    a["w_out"] = flat(blocks_of(f["w_out"]))
    a["w_query"] = flat(blocks_of(f["peer_wq"]))
    a["keys"] = f["peer_keys"].reshape(L, 2 * PH, NKEYS, P).transpose(0, 3, 1, 2)
    u = f["peer_u"].reshape(L, ET, P, KC, P).transpose(0, 1, 4, 3, 2).reshape(L, ET, P, D)
    v = f["peer_v"].reshape(L, ET, P, D)
    e = np.empty((L, 2 * ET, P, D), np.float32)
    e[:, 0:2], e[:, 2:2 * ET - 2:2], e[:, 3:2 * ET - 2:2], e[:, 2 * ET - 2:] = u[:, 0:2], u[:, 2:], v[:, :ET - 2], v[:, ET - 2:]
    a["w_expert"] = e
    a["rpb"] = np.pad(f["na_rpb"][..., ::-1], ((0, 0), (0, 0), (0, 0), (GRID_W - KW, GRID_W - KW)))
    pos = np.arange(S)
    inv = np.float32(10000.0) ** (-np.arange(16, dtype=np.float32) / np.float32(16))
    ang = np.concatenate([(pos // GRID_W).astype(np.float32)[:, None] * inv, (pos % GRID_W).astype(np.float32)[:, None] * inv], -1)
    pair_of = (np.arange(P) % GDK) // 2
    a["rope"] = np.stack([np.cos(ang).T[pair_of], np.sin(ang).T[pair_of]], 1).astype(np.float32)
    swap = np.zeros((P, P), np.float32)
    swap[np.arange(1, P, 2), np.arange(0, P, 2)] = -1.0
    swap[np.arange(0, P, 2), np.arange(1, P, 2)] = 1.0
    a["swap"] = swap
    a["resets"] = np.broadcast_to((np.arange(NT) % CH != 0).astype(np.float32), (P, NT))
    cs = np.clip(np.arange(GRID_W) - KW // 2, 0, GRID_W - KW)
    ck = np.arange(GRID_W)
    ok = (ck[None] >= cs[:, None]) & (ck[None] < cs[:, None] + KW)
    a["na_mask"] = np.tile(np.where(ok, 0.0, -1e30).astype(np.float32)[:, ::-1], (2, 1))
    return {k: np.ascontiguousarray(v) for k, v in a.items()}


def kernel(**inputs):
    import concourse.bacc as _bacc
    from concourse.bass_utils import run_bass_kernel_spmd as _run

    arrays = lay_out(inputs)
    nc = _bacc.Bacc("TRN2", target_bir_lowering=False, num_devices=1)
    A = {n: nc.dram_tensor(f"in_{n}", a.shape, mybir.dt.from_np(a.dtype), kind="ExternalInput").ap() for n, a in arrays.items()}
    out = nc.dram_tensor("out", (P, KC, S), F32, kind="ExternalOutput").ap()
    build_program(nc, A, out)
    r = _run(nc, [{f"in_{n}": a for n, a in arrays.items()}], core_ids=[0])
    y = r.results[0]["out"]
    return np.ascontiguousarray(y.transpose(2, 1, 0).reshape(1, S, D))
```
